# Optimizing a Trainium2 kernel written in Bass

```python
import jax, jax.numpy as jnp
from jax import lax
import numpy as np

D_MODEL = 1024
BATCH = 1
SEQ = 512
DEPTH = 1

GRID_W = 64
CTX_LEN = 256

N_HEADS = 8
QK_NOPE_DIM = 128
ROPE_DIM = 64
V_HEAD_DIM = 128
QK_HEAD_DIM = QK_NOPE_DIM + ROPE_DIM
Q_LORA_RANK = 256
KV_LORA_RANK = 128
ROPE_BASE = 10000.0
ATTN_SCALE = QK_HEAD_DIM ** -0.5
Q_BLOCK = 128

POOL_WINDOWS = (2, 4, 8, 16)
POOL_GROUPS = 4
POOL_WIDTH = D_MODEL
POOL_GROUP_DIM = POOL_WIDTH // POOL_GROUPS

N_BRANCHES = 2
KV_IN = KV_LORA_RANK + ROPE_DIM
Q_OFF = KV_IN
POOL_OFF = Q_OFF + Q_LORA_RANK
GATE_OFF = POOL_OFF + POOL_WIDTH
IN_WIDTH = GATE_OFF + N_BRANCHES * D_MODEL

PEER_HEADS = 8
N_KEYS = 128
N_EXPERTS = N_KEYS * N_KEYS
PEER_QDIM = 256
PEER_HALF = PEER_QDIM // 2
PEER_TOPK = 16
TOKEN_CHUNK = 128

EPS = 1e-6

kernel_name = "hybrid_mla_pool_peer_dit_block"

def rmsnorm(x, g):
    xf = x.astype(jnp.float32)
    var = jnp.mean(jnp.square(xf), axis=-1, keepdims=True)
    return (xf * lax.rsqrt(var + EPS)).astype(x.dtype) * g

def modulate(h, shift, scale):
    return h * (1 + scale) + shift

def axial_rope_tables(rows, dtype):
    row = jnp.broadcast_to(jnp.arange(rows, dtype=jnp.float32)[:, None], (rows, GRID_W)).reshape(-1)
    col = jnp.broadcast_to(jnp.arange(GRID_W, dtype=jnp.float32)[None, :], (rows, GRID_W)).reshape(-1)
    n_freq = ROPE_DIM // 4
    inv_freq = ROPE_BASE ** (-jnp.arange(n_freq, dtype=jnp.float32) / n_freq)
    ang = jnp.stack([row[:, None] * inv_freq, col[:, None] * inv_freq], axis=1)
    return jnp.cos(ang).astype(dtype), jnp.sin(ang).astype(dtype)

def apply_axial_rope(x, cos, sin):
    xs = x.reshape(x.shape[:-1] + (2, 2, ROPE_DIM // 4))
    x1, x2 = xs[..., 0, :], xs[..., 1, :]
    out = jnp.stack([x1 * cos - x2 * sin, x1 * sin + x2 * cos], axis=-2)
    return out.reshape(x.shape)

def mla_kv(kv_in, g_kv_lora, w_ukv):
    ckv, k_rope = kv_in[..., :KV_LORA_RANK], kv_in[..., KV_LORA_RANK:]
    kv = rmsnorm(ckv, g_kv_lora) @ w_ukv
    kv = kv.reshape(kv.shape[:-1] + (N_HEADS, QK_NOPE_DIM + V_HEAD_DIM))
    return kv[..., :QK_NOPE_DIM], kv[..., QK_NOPE_DIM:], k_rope

def mla_q(cq, g_q_lora, w_uq):
    q = (rmsnorm(cq, g_q_lora) @ w_uq).reshape(cq.shape[:-1] + (N_HEADS, QK_HEAD_DIM))
    return q[..., :QK_NOPE_DIM], q[..., QK_NOPE_DIM:]

def mla_attend(q_nope, q_rope, k_nope, k_rope, v):
    s = (jnp.einsum('bqhd,bkhd->bhqk', q_nope, k_nope)
         + jnp.einsum('bqhr,bkr->bhqk', q_rope, k_rope))
    p = jax.nn.softmax(s.astype(jnp.float32) * ATTN_SCALE, axis=-1).astype(v.dtype)
    return jnp.einsum('bhqk,bkhd->bqhd', p, v)

def latent_attention(q_nope, q_rope, k_nope, k_rope, v):
    b, s = q_nope.shape[:2]
    nb = s // Q_BLOCK
    qn = q_nope.reshape(b, nb, Q_BLOCK, N_HEADS, QK_NOPE_DIM).transpose(1, 0, 2, 3, 4)
    qr = q_rope.reshape(b, nb, Q_BLOCK, N_HEADS, ROPE_DIM).transpose(1, 0, 2, 3, 4)
    out = lax.map(lambda blk: mla_attend(blk[0], blk[1], k_nope, k_rope, v), (qn, qr))
    return out.transpose(1, 0, 2, 3, 4).reshape(b, s, N_HEADS * V_HEAD_DIM)

def multiscale_pool(xp, w_pool, pool_scale):
    b, L, _ = xp.shape
    xg = xp.reshape(b, L, POOL_GROUPS, POOL_GROUP_DIM)
    cs = jnp.cumsum(xg.astype(jnp.float32), axis=1)
    cs = jnp.concatenate([jnp.zeros_like(cs[:, :1]), cs], axis=1)
    t = jnp.arange(L, dtype=jnp.int32)[:, None]
    half = (jnp.array(POOL_WINDOWS, dtype=jnp.int32) // 2)[None, :]
    lo = jnp.clip(t - half, 0, L)
    hi = jnp.clip(t + half, 0, L)
    gidx = jnp.arange(POOL_GROUPS, dtype=jnp.int32)[None, :]
    win_sum = cs[:, hi, gidx] - cs[:, lo, gidx]
    count = (hi - lo).astype(jnp.float32)[None, :, :, None]
    pooled = (win_sum / count - xg.astype(jnp.float32)).astype(xp.dtype)
    y = jnp.einsum('blgc,gcd->blgd', pooled, w_pool)
    return y.reshape(b, L, POOL_WIDTH) * pool_scale

def merge_branches(proj, attn_out, w_pool, pool_scale, w_out):
    y_pool = multiscale_pool(proj[..., POOL_OFF:GATE_OFF], w_pool, pool_scale)
    gates = jax.nn.sigmoid(proj[..., GATE_OFF:].astype(jnp.float32)).astype(proj.dtype)
    merged = gates[..., :D_MODEL] * attn_out + gates[..., D_MODEL:] * y_pool
    return merged @ w_out

def peer_ffn(h, peer_wq, peer_keys, peer_u, peer_v):
    shape = h.shape
    tokens = h.reshape(-1, TOKEN_CHUNK, D_MODEL)

    def chunk(xc):
        n_tok = xc.shape[0]
        q = (xc @ peer_wq).reshape(n_tok, PEER_HEADS, 2, PEER_HALF)
        s = jnp.einsum('thpc,pnc->thpn', q, peer_keys).astype(jnp.float32)
        s_top, i_top = lax.top_k(s, PEER_TOPK)
        cand = s_top[..., 0, :, None] + s_top[..., 1, None, :]
        cand_idx = i_top[..., 0, :, None] * N_KEYS + i_top[..., 1, None, :]
        best, pos = lax.top_k(cand.reshape(n_tok, PEER_HEADS, PEER_TOPK * PEER_TOPK), PEER_TOPK)
        experts = jnp.take_along_axis(
            cand_idx.reshape(n_tok, PEER_HEADS, PEER_TOPK * PEER_TOPK), pos, axis=-1)
        g = jax.nn.softmax(best, axis=-1).astype(xc.dtype)
        u = peer_u[experts]
        v = peer_v[experts]
        a = jax.nn.gelu(jnp.einsum('thkd,td->thk', u, xc), approximate=False) * g
        return jnp.einsum('thk,thkd->td', a, v)

    return lax.map(chunk, tokens).reshape(shape)

def setup_inputs(seed: int = 0) -> dict:
    key = jax.random.key(seed)
    ks = jax.random.split(key, 22)
    f32 = jnp.float32

    def nrm(k, shape, scale):
        return jax.random.normal(k, shape, f32) * scale

    def gain(k, shape):
        return 1.0 + 0.1 * jax.random.normal(k, shape, f32)

    return {
        "x": nrm(ks[0], (BATCH, SEQ, D_MODEL), 1.0),
        "c": nrm(ks[1], (BATCH, D_MODEL), 1.0),
        "ctx": nrm(ks[2], (BATCH, CTX_LEN, D_MODEL), 1.0),
        "c_ctx": nrm(ks[3], (D_MODEL,), 1.0),
        "w_ada": nrm(ks[4], (DEPTH, D_MODEL, 6 * D_MODEL), 0.5 * D_MODEL ** -0.5),
        "b_ada": nrm(ks[5], (DEPTH, 6 * D_MODEL), 0.01),
        "g_mix_pre": gain(ks[6], (DEPTH, D_MODEL)),
        "g_mix_post": gain(ks[7], (DEPTH, D_MODEL)),
        "g_ffn_pre": gain(ks[8], (DEPTH, D_MODEL)),
        "g_ffn_post": gain(ks[9], (DEPTH, D_MODEL)),
        "w_in": nrm(ks[10], (DEPTH, D_MODEL, IN_WIDTH), D_MODEL ** -0.5),
        "g_q_lora": gain(ks[11], (DEPTH, Q_LORA_RANK)),
        "w_uq": nrm(ks[12], (DEPTH, Q_LORA_RANK, N_HEADS * QK_HEAD_DIM), Q_LORA_RANK ** -0.5),
        "g_kv_lora": gain(ks[13], (DEPTH, KV_LORA_RANK)),
        "w_ukv": nrm(ks[14], (DEPTH, KV_LORA_RANK, N_HEADS * (QK_NOPE_DIM + V_HEAD_DIM)), KV_LORA_RANK ** -0.5),
        "w_pool": nrm(ks[15], (DEPTH, POOL_GROUPS, POOL_GROUP_DIM, POOL_GROUP_DIM), POOL_GROUP_DIM ** -0.5),
        "pool_scale": gain(ks[16], (DEPTH, POOL_WIDTH)),
        "w_out": nrm(ks[17], (DEPTH, D_MODEL, D_MODEL), D_MODEL ** -0.5),
        "peer_wq": nrm(ks[18], (DEPTH, D_MODEL, PEER_HEADS * PEER_QDIM), D_MODEL ** -0.5),
        "peer_keys": nrm(ks[19], (DEPTH, 2, N_KEYS, PEER_HALF), PEER_HALF ** -0.5),
        "peer_u": nrm(ks[20], (DEPTH, N_EXPERTS, D_MODEL), D_MODEL ** -0.5),
        "peer_v": nrm(ks[21], (DEPTH, N_EXPERTS, D_MODEL), D_MODEL ** -0.5),
    }

def reference(x, c, ctx, c_ctx, w_ada, b_ada, g_mix_pre, g_mix_post, g_ffn_pre, g_ffn_post,
              w_in, g_q_lora, w_uq, g_kv_lora, w_ukv, w_pool, pool_scale, w_out,
              peer_wq, peer_keys, peer_u, peer_v):
    ROWS = x.shape[1] // GRID_W
    cos, sin = axial_rope_tables(ROWS, x.dtype)
    for layer in range(DEPTH):
        last = layer == DEPTH - 1
        mod = jax.nn.silu(c) @ w_ada[layer] + b_ada[layer]
        sh_m, sc_m, gt_m, sh_f, sc_f, gt_f = jnp.split(mod[:, None, :], 6, axis=-1)
        mod_c = jax.nn.silu(c_ctx) @ w_ada[layer] + b_ada[layer]
        csh_m, csc_m, cgt_m, csh_f, csc_f, cgt_f = jnp.split(mod_c, 6, axis=-1)

        hc = modulate(rmsnorm(ctx, g_mix_pre[layer]), csh_m, csc_m)
        if last:
            kv_in_c = hc @ w_in[layer, :, :KV_IN]
        else:
            proj_c = hc @ w_in[layer]
            kv_in_c = proj_c[..., :KV_IN]
        kc_nope, vc, kc_rope = mla_kv(kv_in_c, g_kv_lora[layer], w_ukv[layer])

        h = modulate(rmsnorm(x, g_mix_pre[layer]), sh_m, sc_m)
        proj = h @ w_in[layer]
        k_nope, v, k_rope = mla_kv(proj[..., :KV_IN], g_kv_lora[layer], w_ukv[layer])
        k_rope = apply_axial_rope(k_rope, cos, sin)
        q_nope, q_rope = mla_q(proj[..., Q_OFF:POOL_OFF], g_q_lora[layer], w_uq[layer])
        q_rope = apply_axial_rope(q_rope, cos[:, None], sin[:, None])
        attn = latent_attention(q_nope, q_rope,
                                jnp.concatenate([kc_nope, k_nope], axis=1),
                                jnp.concatenate([kc_rope, k_rope], axis=1),
                                jnp.concatenate([vc, v], axis=1))
        y = merge_branches(proj, attn, w_pool[layer], pool_scale[layer], w_out[layer])
        x_mid = x + gt_m * rmsnorm(y, g_mix_post[layer])

        hf = modulate(rmsnorm(x_mid, g_ffn_pre[layer]), sh_f, sc_f)
        x_new = x_mid + gt_f * rmsnorm(
            peer_ffn(hf, peer_wq[layer], peer_keys[layer], peer_u[layer], peer_v[layer]),
            g_ffn_post[layer])

        if not last:
            qc_nope, qc_rope = mla_q(proj_c[..., Q_OFF:POOL_OFF], g_q_lora[layer], w_uq[layer])
            attn_c = mla_attend(qc_nope, qc_rope, kc_nope, kc_rope, vc)
            attn_c = attn_c.reshape(attn_c.shape[:2] + (N_HEADS * V_HEAD_DIM,))
            yc = merge_branches(proj_c, attn_c, w_pool[layer], pool_scale[layer], w_out[layer])
            ctx = ctx + cgt_m * rmsnorm(yc, g_mix_post[layer])
            hcf = modulate(rmsnorm(ctx, g_ffn_pre[layer]), csh_f, csc_f)
            ctx = ctx + cgt_f * rmsnorm(
                peer_ffn(hcf, peer_wq[layer], peer_keys[layer], peer_u[layer], peer_v[layer]),
                g_ffn_post[layer])
        x = x_new
    return x


_drawn_inputs = setup_inputs


def setup_inputs(seed=0):
    import zlib

    import numpy as np

    out = dict(_drawn_inputs(seed))
    spreads = {}
    factors = {'g_q_lora': 3.154}
    for name, (base, spread) in spreads.items():
        noise = np.random.default_rng([zlib.crc32(name.encode()), seed]).standard_normal(out[name].shape)
        drawn = base * np.exp(spread * noise) if base else spread * noise
        out[name] = __import__('jax').numpy.asarray(drawn.astype(out[name].dtype))
    for name, factor in factors.items():
        out[name] = (out[name] * factor).astype(out[name].dtype)
    return out
```

```python
import concourse.bass as bass
from concourse import mybir
from contextlib import ExitStack

F32 = mybir.dt.float32
F32R = mybir.dt.float32r
U32 = mybir.dt.uint32
ALU = mybir.AluOpType
ACT = mybir.ActivationFunctionType
AX = mybir.AxisListType

P = 128
D = 1024
KC = D // P
T = 512
TT = T // P
C = 256
CT = C // P
KEYS = T + C
H = 8
KT = KEYS // P
QDIM = 192
SCALE = float(QDIM) ** -0.5
WINDOWS = (2, 4, 8, 16)
PAD = 8
PH = 8
NK = 128
TOPK = 16
EPS = 1e-6
JT = 128
G_TOK = 8
G_BLK = 64

ADA_W = 256
ADA_CHUNKS = 6 * D // ADA_W
ADA_FIRST = 2 * D // ADA_W

R_IN = 0
R_KVQ, R_POOLX, R_GATES = 0, 4, 12
R_WPOOL = 28
R_WOUT = R_WPOOL + 2
R_WQ = R_WOUT + KC
R_U = R_WQ + 2 * PH
R_V = R_U + JT
R_END = R_V + JT

COLS = {"b_ada": 48, "g_mix_pre": KC, "g_mix_post": KC, "g_ffn_pre": KC, "g_ffn_post": KC,
        "pool_scale": KC, "g_q": 2, "g_kv": 1, "eps": 1}
COL_AT = {}
_n = 0
for _k, _w in COLS.items():
    COL_AT[_k] = _n
    _n += _w
NCOLS = _n


class Steps:

    def __init__(self, eng, sem):
        self.eng, self.sem, self.n = eng, sem, 0

    def add(self, ins):
        ins.then_inc(self.sem, 1)
        self.n = self.n + 1

    def sync(self):
        self.eng.wait_ge(self.sem, self.n)

    def link(self, ins):
        self.add(ins)
        self.sync()


def build(nc, a, out):
    ctx = ExitStack()
    with ctx:
        arena_bytes = nc.sbuf_bytes_remaining // 64 * 64
        ctx.enter_context(nc.sbuf_tensor("arena", [P, arena_bytes // 4], F32))
        base = nc.sbuf_base - arena_bytes

        class Region:

            def __init__(self, at):
                self.at = at

            def __call__(self, name, shape, dt=F32):
                n = 4
                for s in shape[1:]:
                    n *= s
                n = (n + 31) // 32 * 32
                assert self.at + n <= arena_bytes, (name, self.at + n, arena_bytes)
                t = nc.alloc_sbuf_tensor_at(name, list(shape), dt, offset=base + self.at)
                self.at += n
                return t

        sb = Region(0)
        ident = sb("ident", [P, P])
        ones = sb("ones", [P, P])
        fold = sb("fold", [P, P])
        iota = sb("iota", [P, P])
        cols = sb("cols", [P, NCOLS])
        modraw = sb("modraw", [P, 48, 2])
        modc = sb("modc", [P, 48, 2])
        a_mix = sb("a_mix", [P, KC, 2])
        a_ffn = sb("a_ffn", [P, KC])
        gcol = sb("gcol", [P, 2, KC])
        cond = sb("cond", [P, KC, 2])
        silu = sb("silu", [P, KC, 2])
        edge = sb("edge", [P, 4, 2 * PAD])
        ss = sb("ss", [P, 8])
        std = sb("std", [P, 8])
        rs = sb("rs", [P, 8])
        ss2 = sb("ss2", [P, 8])
        std2 = sb("std2", [P, 8])
        rs2 = sb("rs2", [P, 8])
        spacer = sb("spacer", [P, 1])
        g_row = sb("g_row", [P, 2, D])
        x_sb = sb("x_sb", [P, TT, D])
        w_raw = [sb(f"w_raw{b}", [P, D]) for b in range(2)]
        w_hi = [sb(f"w_hi{b}", [P, D], F32R) for b in range(2)]
        w_lo = [sb(f"w_lo{b}", [P, D], F32R) for b in range(2)]
        ht_hi = sb("ht_hi", [P, KC, T], F32R)
        ht_lo = sb("ht_lo", [P, KC, T], F32R)
        S = sb.at

        sb = Region(S)
        ada = [sb(f"ada{b}", [P, KC, ADA_W]) for b in range(2)]
        hc_hi = sb("hc_hi", [P, KC, C], F32R)
        hc_lo = sb("hc_lo", [P, KC, C], F32R)
        sq = Region(sb.at - 2 * 4 * KC * C)("sq", [P, KEYS + 2 * T])
        nstd = Region(sb.at - 2 * 4 * KC * C + 4 * (KEYS + 2 * T))("nstd", [P, KEYS + T])
        poolx = sb("poolx", [P, 2 * 4, T + 2 * PAD])
        POOLW_AT = sb.at
        poolw = [sb(f"poolw{b}", [P, 2, T + 2 * PAD]) for b in range(2)]
        ckv = sb("ckv", [P, KEYS])
        cq = sb("cq", [P, 2, T])
        krt = sb("krt", [P, KEYS])
        KV_AT = sb.at
        rot = sb("rot", [P, KEYS])
        kvn_hi = sb("kvn_hi", [P, KEYS], F32R)
        kvn_lo = sb("kvn_lo", [P, KEYS], F32R)
        cqn_hi = sb("cqn_hi", [P, 2, T], F32R)
        cqn_lo = sb("cqn_lo", [P, 2, T], F32R)
        kr_hi = sb("kr_hi", [P, KEYS], F32R)
        kr_lo = sb("kr_lo", [P, KEYS], F32R)
        gates = sb("gates", [P, 2 * KC, T])
        over = Region(sb.at - 4 * 2 * KC * T)
        xn = over("xn", [P, TT + CT, D])
        ctx_sb = over("ctx_sb", [P, CT, D])
        assert over.at <= sb.at
        over = Region(POOLW_AT)
        htmp = [over(f"htmp{b}", [P, T]) for b in range(2)]

        sb = Region(S)
        wqk_raw = sb("wqk_raw", [P, 5 * P])
        wqk_hi = sb("wqk_hi", [P, 5 * P], F32R)
        wqk_lo = sb("wqk_lo", [P, 5 * P], F32R)
        wv_raw = sb("wv_raw", [P, P])
        wv_hi = sb("wv_hi", [P, P], F32R)
        wv_lo = sb("wv_lo", [P, P], F32R)
        qn_hi = sb("qn_hi", [P, T], F32R)
        qn_lo = sb("qn_lo", [P, T], F32R)
        qr_f = sb("qr_f", [P, T])
        qr_hi = sb("qr_hi", [P, T], F32R)
        qr_lo = sb("qr_lo", [P, T], F32R)
        k_hi = sb("k_hi", [P, KEYS], F32R)
        k_lo = sb("k_lo", [P, KEYS], F32R)
        v_hi = sb("v_hi", [P, KT, P], F32R)
        v_lo = sb("v_lo", [P, KT, P], F32R)
        prob = [sb(f"prob{b}", [P, KEYS]) for b in range(2)]
        mrg = sb("mrg", [P, T])
        rowmax = sb("rowmax", [P, TT])
        nmax = sb("nmax", [P, TT])
        rsum = sb("rsum", [P, TT])
        rinv = sb("rinv", [P, TT])
        pt_hi = sb("pt_hi", [P, KT, T], F32R)
        pt_lo = sb("pt_lo", [P, KT, T], F32R)
        assert sb.at <= KV_AT, (sb.at, KV_AT)

        sb = Region(S)
        s_sb = sb("s_sb", [P, TT, 2 * PH, NK])
        diag = sb("diag", [P, 2, D])
        xm_n = sb("xm_n", [P, TT, D])
        ytmp = [sb(f"ytmp{b}", [P, D]) for b in range(2)]
        ftmp = [sb(f"ftmp{b}", [P, T]) for b in range(2)]
        junk = sb("junk", [P, D])
        sb = Region(S + 4 * TT * 2 * PH * NK)
        q_hi = [sb(f"q_hi{b}", [P, T], F32R) for b in range(2)]
        q_lo = [sb(f"q_lo{b}", [P, T], F32R) for b in range(2)]
        keys_raw = sb("keys_raw", [P, 2, NK])
        keys_hi = sb("keys_hi", [P, 2, NK], F32R)
        keys_lo = sb("keys_lo", [P, 2, NK], F32R)
        sb = Region(S + 4 * TT * 2 * PH * NK + 4 * 4 * T + 3 * 4 * 2 * NK)
        RT = sb.at
        s_cur = sb("s_cur", [P, 2 * PH, NK])
        s_work = sb("s_work", [P, 2 * PH, NK])
        ROUTE_END = sb.at
        cand = Region(RT)("cand", [P, PH, TOPK * TOPK])
        cand_work = Region(ROUTE_END - 4 * 2 * PH * NK)("cand_work", [P, PH, TOPK * TOPK])
        eq = sb("eq", [P, PH * TOPK, TOPK])
        eq2 = sb("eq2", [P, PH * TOPK, TOPK])
        top = sb("top", [P, 2 * PH, TOPK])
        top_i = sb("top_i", [P, 2 * PH, TOPK], U32)
        best = sb("best", [P, PH, TOPK])
        pos = sb("pos", [P, PH, TOPK], U32)
        pos_a = sb("pos_a", [P, PH * TOPK], U32)
        pos_b = sb("pos_b", [P, PH * TOPK], U32)
        ROUTE_TMP_END = sb.at
        sel_i = sb("sel_i", [P, TT, PH * TOPK])
        sel_j = sb("sel_j", [P, TT, PH * TOPK])
        sel_e = sb("sel_e", [P, TT * PH, TOPK])
        sel_s = sb("sel_s", [P, TT * PH])
        sel_r = sb("sel_r", [P, TT * PH])
        kt_i = sb("kt_i", [P, T])
        kt_j = sb("kt_j", [P, T])
        kt_ghi = sb("kt_ghi", [P, T], F32R)
        kt_g = sb("kt_g", [P, T])
        kt_glo = sb("kt_glo", [P, T])
        gh = [sb(f"gh{b}", [P, T]) for b in range(2)]
        KEEP_END = sb.at
        sb = Region(S)
        g_blk = [sb(f"g_blk{b}", [P, NK, G_BLK]) for b in range(2)]
        assert sb.at <= ROUTE_TMP_END, (sb.at, ROUTE_TMP_END)
        oh_i = [sb(f"oh_i{b}", [P, G_TOK, NK], F32R) for b in range(2)]
        assert sb.at <= ROUTE_TMP_END, (sb.at, ROUTE_TMP_END)
        sb = Region(KEEP_END)
        oh_jhi = [sb(f"oh_jhi{b}", [P, G_TOK, NK], F32R) for b in range(2)]
        oh_jlo = [sb(f"oh_jlo{b}", [P, G_TOK, NK], F32R) for b in range(2)]
        sb = Region(S)
        gh_in = [sb(f"gh_in{b}", [P, 2, T]) for b in range(2)]
        g_in = [sb(f"g_in{b}", [P, T // G_BLK, 2, G_BLK]) for b in range(2)]
        a_f = [sb(f"a_f{b}", [P, T]) for b in range(2)]
        a_hi = [sb(f"a_hi{b}", [P, T], F32R) for b in range(2)]
        a_lo = [sb(f"a_lo{b}", [P, T], F32R) for b in range(2)]

        ps = ctx.enter_context(nc.psum_tensor("ps", [P, 8, 512], F32))

        def bank(n, w=512):
            return ps[:, n, 0:w]

        def banks2(n, w):
            return ps[:, n:n + 2, :].rearrange("p a b -> p (a b)")[:, 0:w]

        def col(name, n=0):
            at = COL_AT[name] + n
            return cols[:, at:at + 1]

        gh_d = nc.dram_tensor("gelu_scratch", [JT, P, T], F32).ap()
        g_d = nc.dram_tensor("gate_scratch", [T // G_BLK, P, NK, G_BLK], F32).ap()

        def sem(name):
            return ctx.enter_context(nc.semaphore(name))

        cond_in, const_in, x_in, table_in, rot_in, keys_in = map(
            sem, ("cond_in", "const_in", "x_in", "table_in", "rot_in", "keys_in"))
        ring_in = [sem(f"ring_in{b}") for b in range(2)]
        ring_hi, ring_lo, ring_used = sem("ring_hi"), sem("ring_lo"), sem("ring_used")
        ada_in = [sem(f"ada_in{b}") for b in range(2)]
        mod_done, mod_copied = sem("mod_done"), sem("mod_copied")
        silu_ready, ones_ready, pads_ready = sem("silu_ready"), sem("ones_ready"), sem("pads_ready")
        dve_step, act_step = sem("dve_step"), sem("act_step")
        xstd_ready, xn_ready, amix_ready = sem("xstd_ready"), sem("xn_ready"), sem("amix_ready")
        ht_turned, ht_hi_ready, ht_lo_ready = sem("ht_turned"), sem("ht_hi_ready"), sem("ht_lo_ready")
        kvq_copied, krt_ready, sq_ready = map(sem, ("kvq_copied", "krt_ready", "sq_ready"))
        sums_done, nstd_ready, normed, split_hi, split_lo = map(
            sem, ("sums_done", "nstd_ready", "normed", "split_hi", "split_lo"))
        tile_copied = sem("tile_copied")
        pooled_ready, pooled_hi, pooled_lo, pmix_used = map(
            sem, ("pooled_ready", "pooled_hi", "pooled_lo", "pmix_used"))
        diag_ready, rows_done, rows_ready = sem("diag_ready"), sem("rows_done"), sem("rows_ready")
        wqk_in, wv_in, wqk_hi_s, wqk_lo_s, wv_hi_s, wv_lo_s = map(
            sem, ("wqk_in", "wv_in", "wqk_hi_s", "wqk_lo_s", "wv_hi_s", "wv_lo_s"))
        pj_done, pj_hi, pj_free = sem("pj_done"), sem("pj_hi"), sem("pj_free")
        qr_rotated = sem("qr_rotated")
        s_done, max_ready, exp_ready, prob_ready = map(sem, ("s_done", "max_ready", "exp_ready", "prob_ready"))
        pt_turned, pt_hi_s, pt_lo_s = sem("pt_turned"), sem("pt_hi_s"), sem("pt_lo_s")
        mrg_ready = sem("mrg_ready")
        y_done, ystd_ready, xmid_ready, xmstd_ready, xmn_ready = map(
            sem, ("y_done", "ystd_ready", "xmid_ready", "xmstd_ready", "xmn_ready"))
        hf_turned, hf_hi_ready, hf_lo_ready = sem("hf_turned"), sem("hf_hi_ready"), sem("hf_lo_ready")
        keys_hi_s, keys_lo_s = sem("keys_hi_s"), sem("keys_lo_s")
        q_hi_s, q_lo_s, sc_done, sc_copied = map(sem, ("q_hi_s", "q_lo_s", "sc_done", "sc_copied"))
        gelu_done = sem("gelu_done")
        gh_stored = [sem(f"gh_stored{b}") for b in range(2)]
        g_stored = [sem(f"g_stored{b}") for b in range(2)]
        logits_ready, exp_all, sel_ready, sel_turned = map(sem, ("logits_ready", "exp_all", "sel_ready", "sel_turned"))
        oh_ready, g_built, g_copied = sem("oh_ready"), sem("g_built"), sem("g_copied")
        pair_in = [sem(f"pair_in{b}") for b in range(2)]
        a_ready, a_hi_s, a_lo_s = sem("a_ready"), sem("a_hi_s"), sem("a_lo_s")
        o_done, ostd_ready, out_ready, out_stored = map(sem, ("o_done", "ostd_ready", "out_ready", "out_stored"))

        block = ctx.enter_context(nc.Block())

        def ring_src(t0, n):
            for name, first, count in (("w_in", R_IN, 28), ("w_pool", R_WPOOL, 2), ("w_out", R_WOUT, KC),
                                       ("wq", R_WQ, 2 * PH), ("u", R_U, JT), ("v", R_V, JT)):
                if first <= t0 and t0 + n <= first + count:
                    return a[name], t0 - first
            raise AssertionError(t0)

        @block.sync
        def _(sp):
            def ring(t, off, src, b, first=False):
                if not first:
                    sp.wait_ge(ring_lo, t - 1)
                sp.dma_start(w_raw[b][:, :], src[bass.ds(off, 1)].rearrange("o p n -> (o p) n")).then_inc(ring_in[b], 16)

            def ring_at(t):
                src, off = ring_src(t, 1)
                ring(t, off, src, t % 2, first=t < 2)

            def ada_load(c, b, first=False):
                if not first:
                    sp.wait_ge(mod_done, c - 1)
                sp.dma_start(ada[b].rearrange("p k n -> p (k n)"),
                             a["w_ada"][bass.ds(c, 1)].rearrange("o p n -> (o p) n")).then_inc(ada_in[b], 16)

            ada_load(0, 0, True)
            ada_load(1, 1, True)
            with sp.Fori(1, ADA_FIRST // 2) as i:
                for b in range(2):
                    ada_load(2 * i + b, b)
            ring_at(0)
            ring_at(1)
            ada_load(ADA_FIRST, 0)
            ada_load(ADA_FIRST + 1, 1)
            with sp.Fori(0, R_GATES // 2 - 1) as i:
                for b in range(2):
                    ring(2 * i + 2 + b, 2 * i + 2 + b, a["w_in"], b)
            ring_at(R_GATES)
            ring_at(R_GATES + 1)
            with sp.Fori(0, 7) as i:
                for b in range(2):
                    ring(R_GATES + 2 + 2 * i + b, R_GATES + 2 + 2 * i + b, a["w_in"], b)
                    ada_load(ADA_FIRST + 2 + 2 * i + b, b)
            ring_at(R_WPOOL)
            ring_at(R_WPOOL + 1)
            def head_weights(h, first=False):
                if not first:
                    sp.wait_ge(wqk_lo_s, h)
                sp.dma_start(wqk_raw[:, :], a["wqk"][bass.ds(h, 1)].rearrange("o p n -> (o p) n")).then_inc(wqk_in, 16)
                if not first:
                    sp.wait_ge(wv_lo_s, h)
                sp.dma_start(wv_raw[:, :], a["wv"][bass.ds(h, 1)].rearrange("o p n -> (o p) n")).then_inc(wv_in, 16)
            sp.wait_ge(pooled_lo, 4)
            sp.wait_ge(split_lo, 3)
            sp.wait_ge(mod_done, ADA_CHUNKS)
            head_weights(0, True)
            ring_at(R_WOUT)
            ring_at(R_WOUT + 1)
            with sp.Fori(1, H) as h:
                head_weights(h)
            for t in range(R_WOUT + 2, R_WQ):
                ring_at(t)
            with sp.Fori(0, PH) as i:
                for b in range(2):
                    ring(R_WQ + 2 * i + b, 2 * i + b, a["wq"], b)
            ring_at(R_U)
            ring_at(R_U + 1)

            def store_gelu(j, b):
                sp.wait_ge(gelu_done, j + 1)
                sp.dma_start(gh_d[bass.ds(j, 1)].rearrange("o p n -> (o p) n"), gh[b][:, :]).then_inc(gh_stored[b], 16)

            def u_step(half, b):
                j = 2 * half + b
                ring(R_U + 2 + j, j + 2, a["u"], b)
                store_gelu(j, b)
            with sp.Fori(0, JT // 4) as i:
                u_step(i, 0)
                u_step(i, 1)

            def g_store(blk, b):
                sp.wait_ge(g_copied, (blk + 1) * (G_BLK // G_TOK))
                sp.dma_start(g_d[bass.ds(blk, 1)].rearrange("o p n t -> (o p) (n t)"),
                             g_blk[b].rearrange("p n t -> p (n t)")).then_inc(g_stored[b], 16)
            PAIRS = G_BLK // G_TOK // 2
            with sp.Fori(0, T // G_BLK // 2 - 1) as q:
                for bb in range(2):
                    with sp.Fori(0, PAIRS) as i:
                        u_step(JT // 4 + (2 * q + bb) * PAIRS + i, 0)
                        u_step(JT // 4 + (2 * q + bb) * PAIRS + i, 1)
                    g_store(2 * q + bb, bb)
            with sp.Fori(0, PAIRS) as i:
                u_step(JT // 2 - 2 * PAIRS + i, 0)
                u_step(JT // 2 - 2 * PAIRS + i, 1)
            g_store(T // G_BLK - 2, 0)
            with sp.Fori(0, PAIRS - 1) as i:
                u_step(JT // 2 - PAIRS + i, 0)
                u_step(JT // 2 - PAIRS + i, 1)
            ring_at(R_V)
            store_gelu(JT - 2, 0)
            ring_at(R_V + 1)
            store_gelu(JT - 1, 1)
            g_store(T // G_BLK - 1, 1)
            for b in range(2):
                sp.wait_ge(gh_stored[b], 16 * JT // 2)
                sp.wait_ge(g_stored[b], 16 * T // G_BLK // 2)

            def pair_load(p, b):
                sp.dma_start(gh_in[b][:, :, :], gh_d[bass.ds(2 * p, 2)].rearrange("j p t -> p j t")).then_inc(pair_in[b], 16)
                sp.dma_start(g_in[b][:, :, :, :], g_d[:, :, bass.ds(2 * p, 2), :].rearrange("k p j t -> p k j t")).then_inc(pair_in[b], 16)
            pair_load(0, 0)
            pair_load(1, 1)
            with sp.Fori(0, JT // 4 - 1) as i:
                for q in range(2):
                    for b in range(2):
                        t = 4 * i + 2 * q + b
                        ring(R_V + 2 + t, t + 2, a["v"], b)
                    sp.wait_ge(a_ready, 4 * i + 2 * q + 2)
                    pair_load(2 * i + q + 2, q)
            ring_at(R_END - 2)
            ring_at(R_END - 1)
            for tt in range(TT):
                sp.wait_ge(out_ready, tt + 1)
                sp.dma_start(out[tt * P:(tt + 1) * P, :], x_sb[:, tt, :]).then_inc(out_stored, 16)
            sp.wait_ge(out_stored, 16 * TT)

        @block.gpsimd
        def _(pool):
            def lo(t, b):
                pool.wait_ge(ring_hi, t + 1)
                nc.gpsimd.tensor_tensor(w_lo[b][:, :], w_raw[b][:, :], w_hi[b][:, :].bitcast(F32),
                                        ALU.subtract).then_inc(ring_lo, 1)

            def head_lo(h):
                pool.wait_ge(wqk_hi_s, h + 1)
                nc.gpsimd.tensor_tensor(wqk_lo[:, :], wqk_raw[:, :], wqk_hi[:, :].bitcast(F32),
                                        ALU.subtract).then_inc(wqk_lo_s, 1)
                pool.wait_ge(wv_hi_s, h + 1)
                nc.gpsimd.tensor_tensor(wv_lo[:, :], wv_raw[:, :], wv_hi[:, :].bitcast(F32),
                                        ALU.subtract).then_inc(wv_lo_s, 1)

            nc.gpsimd.memset(ones[:, :], 1.0).then_inc(ones_ready, 1)
            nc.gpsimd.memset(poolx[:, :, :], 0.0).then_inc(pads_ready, 1)
            with pool.Fori(0, R_WOUT // 2) as i:
                lo(2 * i, 0)
                lo(2 * i + 1, 1)
            head_lo(0)
            lo(R_WOUT, 0)
            lo(R_WOUT + 1, 1)
            with pool.Fori(1, H) as h:
                head_lo(h)
            with pool.Fori(R_WOUT // 2 + 1, R_END // 2) as i:
                lo(2 * i, 0)
                lo(2 * i + 1, 1)

        @block.scalar
        def _(act):
            step = Steps(act, act_step)

            def hi(half, b, first=False):
                act.wait_ge(ring_in[b], 16 * half + 16)
                if not first:
                    act.wait_ge(ring_used, 2 * half + b - 1)
                nc.scalar.activation(w_hi[b][:, :], w_raw[b][:, :], ACT.Copy).then_inc(ring_hi, 1)

            def mod_copy(c, b):
                act.wait_ge(mod_done, c + 1)
                nc.scalar.activation(modraw.rearrange("p m s -> p (m s)")[:, bass.ds(4 * c, 4)],
                                     ps[:, 2 + b, 0:4], ACT.Copy).then_inc(mod_copied, 1)

            act.dma_start(cond[:, :, :], a["cond"]).then_inc(cond_in, 16)
            act.dma_start(x_sb[:, :, :], a["x"].rearrange("(a p) d -> p a d", p=P)).then_inc(x_in, 16)
            act.dma_start(ctx_sb[:, :, :], a["ctx"].rearrange("(a p) d -> p a d", p=P)).then_inc(x_in, 16)
            act.dma_start(cols[:, :], a["cols"]).then_inc(const_in, 16)
            act.dma_start(ident[:, :], a["ident"]).then_inc(const_in, 16)
            act.dma_start(fold[:, :], a["fold"]).then_inc(const_in, 16)
            act.dma_start(iota[:, :], a["iota"]).then_inc(const_in, 16)
            act.dma_start(edge[:, :, :], a["edge"]).then_inc(const_in, 16)
            act.dma_start(rot[:, :], a["rot"]).then_inc(const_in, 16)
            act.wait_ge(cond_in, 16)
            nc.scalar.activation(silu[:, :, :], cond[:, :, :], ACT.Silu).then_inc(silu_ready, 1)

            act.wait_ge(x_in, 32)
            for n in range(TT + CT):
                src = x_sb[:, n, :] if n < TT else ctx_sb[:, n - TT, :]
                step.add(nc.scalar.activation(xn[:, n, :], src, ACT.Square, accum_out=ss[:, n:n + 1]))
            step.sync()
            act.wait_ge(const_in, 96)
            nc.scalar.activation(std[:, 0:6], ss[:, 0:6], ACT.Sqrt, scale=1.0 / D, bias=col("eps")).then_inc(xstd_ready, 1)
            with act.Fori(0, ADA_FIRST // 2) as i:
                mod_copy(2 * i, 0)
                mod_copy(2 * i + 1, 1)
            hi(0, 0, True)
            hi(0, 1, True)
            act.wait_ge(amix_ready, 2)
            for k in range(KC):
                for s, (n, dst) in enumerate(((T, ht_hi), (C, hc_hi))):
                    act.wait_ge(ht_turned, 2 * k + s + 1)
                    nc.scalar.activation(dst[:, k, :], bank(4 + 2 * (k % 2) + s, n), ACT.Identity,
                                         scale=a_mix[:, k, s:s + 1], bias=modc[:, k, s:s + 1]).then_inc(ht_hi_ready, 1)
            hi(1, 0)
            act.wait_ge(ring_used, 1)
            step.add(nc.scalar.activation(ckv[:, 0:T], bank(0), ACT.Copy))
            nc.scalar.activation(ckv[:, T:KEYS], bank(1, C), ACT.Copy).then_inc(kvq_copied, 1)
            hi(1, 1)
            hi(2, 0)
            act.wait_ge(ring_used, 3)
            nc.scalar.activation(cq[:, 0, :], bank(4), ACT.Copy).then_inc(kvq_copied, 1)
            hi(2, 1)
            act.wait_ge(ring_used, 4)
            nc.scalar.activation(cq[:, 1, :], bank(5), ACT.Copy).then_inc(kvq_copied, 1)

            def pool_tile(half, b):
                n = 2 * half + b
                act.wait_ge(ring_used, R_POOLX + n + 1)
                nc.scalar.activation(poolx[:, bass.ds(n, 1), PAD:PAD + T].rearrange("p o t -> p (o t)"),
                                     bank(b), ACT.Copy).then_inc(tile_copied, 1)
                hi(R_POOLX // 2 + 1 + half, b)
            act.wait_ge(pads_ready, 1)
            with act.Fori(0, 4) as i:
                pool_tile(i, 0)
                pool_tile(i, 1)
            act.wait_ge(sums_done, 1)
            step.add(nc.scalar.activation(nstd[:, 0:KEYS], banks2(6, KEYS), ACT.Sqrt, scale=1.0 / P, bias=col("eps")))
            nc.scalar.activation(nstd[:, KEYS:KEYS + T], bank(4), ACT.Sqrt, scale=0.5 / P, bias=col("eps")).then_inc(nstd_ready, 1)
            act.wait_ge(sums_done, 2)
            nc.scalar.activation(kr_hi[:, 0:T], bank(5), ACT.Copy).then_inc(split_hi, 1)
            nc.scalar.activation(kr_hi[:, T:KEYS], bank(1, C), ACT.Copy).then_inc(split_hi, 1)

            def gate_tile(half, b, ahead=True):
                n = 2 * half + b
                act.wait_ge(ring_used, R_GATES + n + 1)
                nc.scalar.activation(gates[:, bass.ds(n, 1), :].rearrange("p o t -> p (o t)"),
                                     bank(b), ACT.Sigmoid).then_inc(tile_copied, 1)
                mod_copy(ADA_FIRST + n, b)
                hi(R_GATES // 2 + 1 + half, b)
            with act.Fori(0, 8) as i:
                gate_tile(i, 0)
                gate_tile(i, 1)
            act.wait_ge(normed, 1)
            nc.scalar.activation(kvn_hi[:, :], ckv[:, :], ACT.Copy).then_inc(split_hi, 1)
            act.wait_ge(normed, 3)
            nc.scalar.activation(cqn_hi[:, :, :], cq[:, :, :], ACT.Copy).then_inc(split_hi, 1)
            for g in range(4):
                act.wait_ge(pooled_ready, g + 1)
                nc.scalar.activation(ht_hi[:, 2 * g:2 * g + 2, :], poolx[:, 2 * g:2 * g + 2, PAD:PAD + T],
                                     ACT.Copy).then_inc(pooled_hi, 1)
            for n in range(2):
                act.wait_ge(rows_done, n + 1)
                nc.scalar.activation(g_row[:, n, :], banks2(2 * n, D), ACT.Copy).then_inc(rows_ready, 1)

            def wqk_split(h, before=None):
                act.wait_ge(wqk_in, 16 * h + 16)
                if before is not None:
                    act.wait_ge(pj_done, before)
                nc.scalar.activation(wqk_hi[:, :], wqk_raw[:, :], ACT.Copy).then_inc(wqk_hi_s, 1)

            def wv_split(h):
                act.wait_ge(wv_in, 16 * h + 16)
                nc.scalar.activation(wv_hi[:, :], wv_raw[:, :], ACT.Copy).then_inc(wv_hi_s, 1)

            def pj(n, dst, src):
                act.wait_ge(pj_done, n + 1)
                nc.scalar.activation(dst, src, ACT.Copy).then_inc(pj_hi, 1)

            def prob_exp(s, qt, first=False):
                act.wait_ge(max_ready, s + 1)
                if not first:
                    act.wait_ge(pt_turned, s - 1)
                nc.scalar.activation(prob[qt % 2][:, :], banks2(2 * (qt % 2), KEYS), ACT.Exp, scale=SCALE,
                                     bias=nmax[:, qt:qt + 1], accum_out=rsum[:, qt:qt + 1]).then_inc(exp_ready, 1)

            def pt_hi_copy(s, qt):
                act.wait_ge(pt_turned, s + 1)
                nc.scalar.activation(pt_hi[:, :, qt * P:(qt + 1) * P], banks2(4, KEYS).rearrange("p (k q) -> p k q", q=P),
                                     ACT.Copy).then_inc(pt_hi_s, 1)

            def qk_part(h, n):
                pj(n, qn_hi[:, :], bank(7))
                act.wait_ge(qr_rotated, h + 1)
                nc.scalar.activation(qr_hi[:, :], qr_f[:, :], ACT.Copy).then_inc(pj_hi, 1)

            def k_part(n):
                pj(n + 2, k_hi[:, 0:T], bank(7))
                pj(n + 3, k_hi[:, T:KEYS], bank(6, C))

            def mrg_hi_copy(h):
                act.wait_ge(mrg_ready, h + 1)
                nc.scalar.activation(ht_hi[:, bass.ds(h, 1), :].rearrange("p o t -> p (o t)"), mrg[:, :],
                                     ACT.Copy).then_inc(pj_hi, 1)

            def head(h, n, head0=False, last=False):
                s = 4 * h
                if not last:
                    wqk_split(h + 1, 4 if head0 else n)
                prob_exp(s, 0, head0)
                prob_exp(s + 1, 1, head0)
                if not head0:
                    mrg_hi_copy(h - 1)
                pj(n + 1, v_hi[:, 0:4, :], bank(7).rearrange("p (k v) -> p k v", v=P))
                pt_hi_copy(s, 0)
                prob_exp(s + 2, 2)
                pj(n + 2, v_hi[:, 4:6, :], bank(6, C).rearrange("p (k v) -> p k v", v=P))
                if not last:
                    wv_split(h + 1)
                pt_hi_copy(s + 1, 1)
                prob_exp(s + 3, 3)
                pt_hi_copy(s + 2, 2)
                if not last:
                    qk_part(h + 1, n + 3)
                    k_part(n + 3)
                pt_hi_copy(s + 3, 3)

            wqk_split(0)
            wv_split(0)
            hi(R_WOUT // 2, 0)
            hi(R_WOUT // 2, 1)
            qk_part(0, 0)
            k_part(0)
            head(0, 3, head0=True)
            with act.Fori(1, H - 1) as h:
                head(h, 7 * h + 3)
            head(H - 1, 7 * (H - 1) + 3, last=True)
            mrg_hi_copy(H - 1)

            for k in range(KC):
                hi(R_WOUT // 2 + 1 + k // 2, k % 2)

            def y_std(tt):
                if tt < TT - 1:
                    act.wait_ge(y_done, tt + 1)
                else:
                    act.wait_ge(ring_used, R_WQ)
                step.link(nc.scalar.activation(junk[:, :], banks2(2 * tt, D), ACT.Square, accum_out=ss[:, tt:tt + 1]))
                nc.scalar.activation(std[:, tt:tt + 1], ss[:, tt:tt + 1], ACT.Sqrt, scale=1.0 / D,
                                     bias=col("eps")).then_inc(ystd_ready, 1)

            def xm_std(tt):
                act.wait_ge(xmid_ready, tt + 1)
                step.link(nc.scalar.activation(junk[:, :], x_sb[:, tt, :], ACT.Square, accum_out=ss2[:, tt:tt + 1]))
                nc.scalar.activation(std2[:, tt:tt + 1], ss2[:, tt:tt + 1], ACT.Sqrt, scale=1.0 / D,
                                     bias=col("eps")).then_inc(xmstd_ready, 1)
            y_std(0)
            for tt in range(1, TT):
                y_std(tt)
                xm_std(tt - 1)
            xm_std(TT - 1)
            for k in range(KC):
                act.wait_ge(hf_turned, k + 1)
                nc.scalar.activation(ht_hi[:, k, :], bank(k % 4), ACT.Identity, scale=a_ffn[:, k:k + 1],
                                     bias=modc[:, 3 * KC + k, 0:1]).then_inc(hf_hi_ready, 1)
            act.dma_start(keys_raw[:, :, :], a["keys"]).then_inc(keys_in, 16)
            act.wait_ge(keys_in, 16)
            nc.scalar.activation(keys_hi[:, :, :], keys_raw[:, :, :], ACT.Copy).then_inc(keys_hi_s, 1)

            def route(half, b, first=False):
                m = 2 * half + b
                act.wait_ge(ring_used, R_WQ + m + 1)
                if not first:
                    act.wait_ge(sc_done, m - 1)
                nc.scalar.activation(q_hi[b][:, :], bank(b), ACT.Copy).then_inc(q_hi_s, 1)
                hi(R_WQ // 2 + 1 + half, b)
                act.wait_ge(sc_done, m + 1)
                nc.scalar.activation(s_sb[:, :, bass.ds(m, 1), :].rearrange("p a o n -> p a (o n)"),
                                     bank(2 + b).rearrange("p (a n) -> p a n", a=TT), ACT.Copy).then_inc(sc_copied, 1)
            route(0, 0, True)
            route(0, 1, True)
            with act.Fori(1, PH) as i:
                route(i, 0)
                route(i, 1)

            def expert(half, b, first=False):
                j = 2 * half + b
                act.wait_ge(ring_used, R_U + j + 1)
                if not first:
                    act.wait_ge(gh_stored[b], 16 * half)
                nc.scalar.activation(gh[b][:, :], bank(4 + b), ACT.Gelu).then_inc(gelu_done, 1)
                hi(R_U // 2 + 1 + half, b)
            expert(0, 0, True)
            expert(0, 1, True)
            with act.Fori(1, 30) as i:
                expert(i, 0)
                expert(i, 1)
            act.wait_ge(logits_ready, 2 * TT)
            nc.scalar.activation(sel_e[:, :, :], sel_e[:, :, :], ACT.Exp).then_inc(exp_all, 1)
            with act.Fori(30, 32) as i:
                expert(i, 0)
                expert(i, 1)

            def g_copy(u, at, blk):
                act.wait_ge(g_built, u + 1)
                for q in range(2):
                    ins = nc.scalar.activation(
                        g_blk[blk][:, :, bass.ds(at + 4 * q, 4)].rearrange("p n t -> p t n"),
                        bank(6 + q).rearrange("p (t n) -> p t n", t=4), ACT.Copy)
                ins.then_inc(g_copied, 1)
            PAIRS = G_BLK // G_TOK // 2

            def g_blocks(q, first=False):
                for bb in range(2):
                    if not first:
                        act.wait_ge(g_stored[bb], 16 * q)
                    with act.Fori(0, PAIRS) as i:
                        for b in range(2):
                            expert(JT // 4 + (2 * q + bb) * PAIRS + i, b)
                            g_copy(2 * ((2 * q + bb) * PAIRS + i) + b, 2 * G_TOK * i + G_TOK * b, bb)
            g_blocks(0, True)
            with act.Fori(1, T // G_BLK // 2) as q:
                g_blocks(q)

            def weigh(half, b, first=False):
                j = 2 * half + b
                act.wait_ge(a_ready, j + 1)
                if not first:
                    act.wait_ge(ring_used, R_V + j - 1)
                nc.scalar.activation(a_hi[b][:, :], a_f[b][:, :], ACT.Copy).then_inc(a_hi_s, 1)
            weigh(0, 0, True)
            weigh(0, 1, True)
            with act.Fori(1, JT // 2) as i:
                for b in range(2):
                    hi(R_V // 2 + i, b)
                    weigh(i, b)
            for tt in range(TT):
                if tt < TT - 1:
                    act.wait_ge(o_done, tt + 1)
                else:
                    act.wait_ge(ring_used, R_END)
                step.link(nc.scalar.activation(junk[:, :], banks2(2 * tt, D), ACT.Square, accum_out=ss[:, tt:tt + 1]))
                nc.scalar.activation(std[:, tt:tt + 1], ss[:, tt:tt + 1], ACT.Sqrt, scale=1.0 / D,
                                     bias=col("eps")).then_inc(ostd_ready, 1)

        @block.vector
        def _(dve):
            step = Steps(dve, dve_step)
            v = nc.vector

            dve.wait_ge(xstd_ready, 1)
            step.link(v.reciprocal(rs[:, 0:6], std[:, 0:6]))
            for n in range(TT + CT):
                src = x_sb[:, n, :] if n < TT else ctx_sb[:, n - TT, :]
                v.tensor_scalar(xn[:, n, :], src, rs[:, n:n + 1], None, ALU.mult).then_inc(xn_ready, 1)
            dve.wait_ge(mod_copied, ADA_FIRST)
            bada = cols[:, COL_AT["b_ada"]:COL_AT["b_ada"] + 48]

            def add_bias(m0, m1):
                step.link(v.tensor_tensor(modc[:, m0:m1, :], modraw[:, m0:m1, :],
                                          bada[:, m0:m1].unsqueeze(2).to_broadcast([P, m1 - m0, 2]), ALU.add))
            add_bias(0, 2 * KC)
            for s in range(2):
                g = cols[:, COL_AT["g_mix_pre"]:COL_AT["g_mix_pre"] + KC]
                v.scalar_tensor_tensor(out=a_mix[:, :, s], in0=modc[:, KC:2 * KC, s], scalar=1.0, in1=g,
                                       op0=ALU.add, op1=ALU.mult).then_inc(amix_ready, 1)
            def turned_lo(k, dst, src, n, scale, shift, tmp, hi_view):
                step.link(v.tensor_scalar(tmp[:, 0:n], src, scale, shift, ALU.mult, ALU.add))
                return v.tensor_tensor(dst, tmp[:, 0:n], hi_view.bitcast(F32), ALU.subtract)
            dve.wait_ge(amix_ready, 2)
            for k in range(KC):
                for s, (n, hi_t, lo_t) in enumerate(((T, ht_hi, ht_lo), (C, hc_hi, hc_lo))):
                    dve.wait_ge(ht_hi_ready, 2 * k + s + 1)
                    turned_lo(k, lo_t[:, k, :], bank(4 + 2 * (k % 2) + s, n), n, a_mix[:, k, s:s + 1],
                              modc[:, k, s:s + 1], htmp[s], hi_t[:, k, :]).then_inc(ht_lo_ready, 1)
            dve.wait_ge(ring_used, 2)
            v.tensor_tensor(krt[:, 0:T], bank(2), rot[:, 0:T], ALU.mult)
            v.tensor_tensor(krt[:, T:KEYS], bank(3, C), rot[:, T:KEYS], ALU.mult).then_inc(krt_ready, 1)
            dve.wait_ge(kvq_copied, 3)
            v.tensor_tensor(sq[:, 0:KEYS], ckv[:, :], ckv[:, :], ALU.mult)
            v.tensor_tensor(sq[:, KEYS:KEYS + 2 * T], cq.rearrange("p a t -> p (a t)"), cq.rearrange("p a t -> p (a t)"),
                            ALU.mult).then_inc(sq_ready, 1)
            dve.wait_ge(nstd_ready, 1)
            step.link(v.reciprocal(nstd[:, :], nstd[:, :]))
            v.scalar_tensor_tensor(out=ckv[:, :], in0=ckv[:, :], scalar=col("g_kv"), in1=nstd[:, 0:KEYS],
                                   op0=ALU.mult, op1=ALU.mult).then_inc(normed, 1)
            for k in range(2):
                v.scalar_tensor_tensor(out=cq[:, k, :], in0=cq[:, k, :], scalar=col("g_q", k),
                                       in1=nstd[:, KEYS:KEYS + T], op0=ALU.mult, op1=ALU.mult).then_inc(normed, 1)
            dve.wait_ge(split_hi, 2)
            v.tensor_tensor(kr_lo[:, 0:T], bank(5), kr_hi[:, 0:T].bitcast(F32), ALU.subtract)
            v.tensor_tensor(kr_lo[:, T:KEYS], bank(1, C), kr_hi[:, T:KEYS].bitcast(F32), ALU.subtract).then_inc(split_lo, 1)

            for g, w in enumerate(WINDOWS):
                gs = slice(2 * g, 2 * g + 2)
                dve.wait_ge(tile_copied, 2 * g + 2)
                if g:
                    dve.wait_ge(pooled_ready, g)
                xg = poolx[:, gs, :]
                lo_i, hi_i = 1, T + 2 * PAD
                step.link(v.tensor_tensor(poolw[0][:, :, 1:hi_i], xg[:, :, 0:hi_i - 1], xg[:, :, 1:hi_i], ALU.add))
                cur, sh = 0, 1
                while 2 * sh < w:
                    nl, nh = lo_i + sh, hi_i - sh
                    step.link(v.tensor_tensor(poolw[1 - cur][:, :, nl:nh], poolw[cur][:, :, nl - sh:nh - sh],
                                              poolw[cur][:, :, nl + sh:nh + sh], ALU.add))
                    lo_i, hi_i, cur, sh = nl, nh, 1 - cur, 2 * sh
                assert lo_i <= PAD and hi_i >= PAD + T
                W = poolw[cur]
                for e0, at in ((0, PAD), (PAD, T)):
                    ee = edge[:, g, e0:e0 + PAD].unsqueeze(1).to_broadcast([P, 2, PAD])
                    step.add(v.tensor_tensor(W[:, :, at:at + PAD], W[:, :, at:at + PAD], ee, ALU.mult))
                step.sync()
                v.scalar_tensor_tensor(out=poolx[:, gs, PAD:PAD + T], in0=W[:, :, PAD:PAD + T], scalar=1.0 / w,
                                       in1=poolx[:, gs, PAD:PAD + T], op0=ALU.mult, op1=ALU.subtract).then_inc(pooled_ready, 1)
            dve.wait_ge(split_hi, 3)
            v.tensor_tensor(kvn_lo[:, :], ckv[:, :], kvn_hi[:, :].bitcast(F32), ALU.subtract).then_inc(split_lo, 1)
            dve.wait_ge(split_hi, 4)
            v.tensor_tensor(cqn_lo[:, :, :], cq[:, :, :], cqn_hi[:, :, :].bitcast(F32), ALU.subtract).then_inc(split_lo, 1)
            for g in range(4):
                dve.wait_ge(pooled_hi, g + 1)
                v.tensor_tensor(ht_lo[:, 2 * g:2 * g + 2, :], poolx[:, 2 * g:2 * g + 2, PAD:PAD + T],
                                ht_hi[:, 2 * g:2 * g + 2, :].bitcast(F32), ALU.subtract).then_inc(pooled_lo, 1)
            dve.wait_ge(mod_copied, ADA_CHUNKS)
            add_bias(2 * KC, 6 * KC)
            g = cols[:, COL_AT["g_ffn_pre"]:COL_AT["g_ffn_pre"] + KC]
            step.add(v.scalar_tensor_tensor(out=a_ffn[:, :], in0=modc[:, 4 * KC:5 * KC, 0], scalar=1.0, in1=g,
                                            op0=ALU.add, op1=ALU.mult))
            for n, (m0, name) in enumerate(((2 * KC, "g_mix_post"), (5 * KC, "g_ffn_post"))):
                g = cols[:, COL_AT[name]:COL_AT[name] + KC]
                step.add(v.tensor_tensor(gcol[:, n, :], modc[:, m0:m0 + KC, 0], g, ALU.mult))
            step.sync()
            for n in range(2):
                for k in range(KC):
                    v.tensor_scalar(diag[:, n, k * P:(k + 1) * P], ident[:, :], gcol[:, n, k:k + 1], None,
                                    ALU.mult).then_inc(diag_ready, 1)
            for m in range(KC):
                dve.wait_ge(ring_used, R_WPOOL + m // 4 + 1)
                v.scalar_tensor_tensor(out=gates[:, KC + m, :], in0=bank(m), scalar=col("pool_scale", m),
                                       in1=gates[:, KC + m, :], op0=ALU.mult, op1=ALU.mult).then_inc(pmix_used, 1)

            def pj_lo(n, dst, src, hi_view):
                dve.wait_ge(pj_hi, n + 1)
                v.tensor_tensor(dst, src, hi_view.bitcast(F32), ALU.subtract).then_inc(pj_free, 1)

            rot_q = rot[:, 0:T]

            def row_max(s, qt, cnt):
                dve.wait_ge(s_done, s + 1)
                cnt.link(v.tensor_reduce(rowmax[:, qt:qt + 1], banks2(2 * (qt % 2), KEYS), AX.X, ALU.max))
                v.tensor_scalar(nmax[:, qt:qt + 1], rowmax[:, qt:qt + 1], -SCALE, None, ALU.mult).then_inc(max_ready, 1)

            def norm_rows(s, qt, cnt):
                dve.wait_ge(exp_ready, s + 1)
                cnt.link(v.reciprocal(rinv[:, qt:qt + 1], rsum[:, qt:qt + 1]))
                v.tensor_scalar(prob[qt % 2][:, :], prob[qt % 2][:, :], rinv[:, qt:qt + 1], None,
                                ALU.mult).then_inc(prob_ready, 1)

            def pt_lo_part(s, qt):
                dve.wait_ge(pt_hi_s, s + 1)
                q = slice(qt * P, (qt + 1) * P)
                v.tensor_tensor(pt_lo[:, :, q], banks2(4, KEYS).rearrange("p (k q) -> p k q", q=P),
                                pt_hi[:, :, q].bitcast(F32), ALU.subtract).then_inc(pt_lo_s, 1)

            def merge(h, n, cnt):
                dve.wait_ge(pj_done, n + 1)
                cnt.link(v.tensor_tensor(mrg[:, :], bank(6), gates[:, bass.ds(h, 1), :].rearrange("p o t -> p (o t)"), ALU.mult))
                v.tensor_tensor(mrg[:, :], mrg[:, :], gates[:, bass.ds(KC + h, 1), :].rearrange("p o t -> p (o t)"),
                                ALU.add).then_inc(mrg_ready, 1)
                dve.wait_ge(pj_hi, n + 1)
                v.tensor_tensor(ht_lo[:, bass.ds(h, 1), :].rearrange("p o t -> p (o t)"), mrg[:, :],
                                ht_hi[:, bass.ds(h, 1), :].rearrange("p o t -> p (o t)").bitcast(F32),
                                ALU.subtract).then_inc(pj_free, 1)

            def qk(h, n):
                dve.wait_ge(pj_done, n + 2)
                v.tensor_tensor(qr_f[:, :], bank(6), rot_q, ALU.mult).then_inc(qr_rotated, 1)
                pj_lo(n, qn_lo[:, :], bank(7), qn_hi[:, :])
                pj_lo(n + 1, qr_lo[:, :], qr_f[:, :], qr_hi[:, :])

            def head(h, n, cnt, head0=False, last=False):
                s = 4 * h
                row_max(s, 0, cnt)
                row_max(s + 1, 1, cnt)
                norm_rows(s, 0, cnt)
                norm_rows(s + 1, 1, cnt)
                if not head0:
                    merge(h - 1, n, cnt)
                pj_lo(n + 1, v_lo[:, 0:4, :], bank(7).rearrange("p (k v) -> p k v", v=P), v_hi[:, 0:4, :])
                pt_lo_part(s, 0)
                row_max(s + 2, 2, cnt)
                pj_lo(n + 2, v_lo[:, 4:6, :], bank(6, C).rearrange("p (k v) -> p k v", v=P), v_hi[:, 4:6, :])
                pt_lo_part(s + 1, 1)
                norm_rows(s + 2, 2, cnt)
                row_max(s + 3, 3, cnt)
                pt_lo_part(s + 2, 2)
                norm_rows(s + 3, 3, cnt)
                if not last:
                    qk(h + 1, n + 3)
                    pj_lo(n + 5, k_lo[:, 0:T], bank(7), k_hi[:, 0:T])
                    pj_lo(n + 6, k_lo[:, T:KEYS], bank(6, C), k_hi[:, T:KEYS])
                pt_lo_part(s + 3, 3)

            qk(0, 0)
            pj_lo(2, k_lo[:, 0:T], bank(7), k_hi[:, 0:T])
            pj_lo(3, k_lo[:, T:KEYS], bank(6, C), k_hi[:, T:KEYS])
            head(0, 3, step, head0=True)
            PER_HEAD = 9
            n0 = step.n
            with dve.Fori(1, H - 1) as h:
                cnt = Steps(dve, dve_step)
                cnt.n = h * PER_HEAD + (n0 - PER_HEAD)
                head(h, 7 * h + 3, cnt)
            step.n = n0 + (H - 2) * PER_HEAD
            head(H - 1, 7 * (H - 1) + 3, step, last=True)
            merge(H - 1, 7 * H + 3 - 4, step)

            def mid(tt):
                dve.wait_ge(ystd_ready, tt + 1)
                step.link(v.reciprocal(rs[:, tt:tt + 1], std[:, tt:tt + 1]))
                step.link(v.scalar_tensor_tensor(out=ytmp[tt % 2][:, :], in0=banks2(2 * tt, D), scalar=rs[:, tt:tt + 1],
                                                 in1=g_row[:, 0, :], op0=ALU.mult, op1=ALU.mult))
                v.tensor_tensor(x_sb[:, tt, :], x_sb[:, tt, :], ytmp[tt % 2][:, :], ALU.add).then_inc(xmid_ready, 1)

            def mid_norm(tt):
                dve.wait_ge(xmstd_ready, tt + 1)
                step.link(v.reciprocal(rs2[:, tt:tt + 1], std2[:, tt:tt + 1]))
                v.tensor_scalar(xm_n[:, tt, :], x_sb[:, tt, :], rs2[:, tt:tt + 1], None, ALU.mult).then_inc(xmn_ready, 1)
            dve.wait_ge(rows_ready, 2)
            mid(0)
            for tt in range(1, TT):
                mid(tt)
                mid_norm(tt - 1)
            mid_norm(TT - 1)
            for k in range(KC):
                dve.wait_ge(hf_hi_ready, k + 1)
                turned_lo(k, ht_lo[:, k, :], bank(k % 4), T, a_ffn[:, k:k + 1], modc[:, 3 * KC + k, 0:1],
                          ftmp[k % 2], ht_hi[:, k, :]).then_inc(hf_lo_ready, 1)
            dve.wait_ge(keys_hi_s, 1)
            v.tensor_tensor(keys_lo[:, :, :], keys_raw[:, :, :], keys_hi[:, :, :].bitcast(F32), ALU.subtract).then_inc(keys_lo_s, 1)

            def q_part(m, b):
                dve.wait_ge(q_hi_s, m + 1)
                v.tensor_tensor(q_lo[b][:, :], bank(b), q_hi[b][:, :].bitcast(F32), ALU.subtract).then_inc(q_lo_s, 1)
            with dve.Fori(0, PH) as i:
                q_part(2 * i, 0)
                q_part(2 * i + 1, 1)

            dve.wait_ge(sc_copied, 2 * PH)
            n0 = step.n

            def route_tile(tt, cnt):
                def sync():
                    cnt.sync()
                    v.memset(spacer[:, :], 0.0)
                cnt.add(v.tensor_copy(s_cur[:, :, :], s_sb[:, bass.ds(tt, 1), :, :].rearrange("p o h n -> p (o h) n")))
                sync()
                for h in range(2 * PH):
                    cnt.add(v.max(top[:, h, 0:8], s_cur[:, h, :]))
                sync()
                for h in range(2 * PH):
                    cnt.add(v.max_index(top_i[:, h, 0:8], top[:, h, 0:8], s_cur[:, h, :]))
                    cnt.add(v.match_replace(s_work[:, h, :], top[:, h, 0:8], s_cur[:, h, :], -3.0e38))
                sync()
                for h in range(2 * PH):
                    cnt.add(v.max(top[:, h, 8:16], s_work[:, h, :]))
                sync()
                for h in range(2 * PH):
                    cnt.add(v.max_index(top_i[:, h, 8:16], top[:, h, 8:16], s_work[:, h, :]))
                sync()
                tv = top.rearrange("p (h two) k -> p h two k", two=2)
                for h in range(PH):
                    cnt.add(v.tensor_tensor(cand[:, h, :].rearrange("p (x y) -> p x y", y=TOPK),
                                            tv[:, h, 0, :].unsqueeze(2).to_broadcast([P, TOPK, TOPK]),
                                            tv[:, h, 1, :].unsqueeze(1).to_broadcast([P, TOPK, TOPK]), ALU.add))
                sync()
                for h in range(PH):
                    cnt.add(v.max(best[:, h, 0:8], cand[:, h, :]))
                sync()
                for h in range(PH):
                    cnt.add(v.max_index(pos[:, h, 0:8], best[:, h, 0:8], cand[:, h, :]))
                    cnt.add(v.match_replace(cand_work[:, h, :], best[:, h, 0:8], cand[:, h, :], -3.0e38))
                sync()
                for h in range(PH):
                    cnt.add(v.max(best[:, h, 8:16], cand_work[:, h, :]))
                sync()
                for h in range(PH):
                    cnt.add(v.max_index(pos[:, h, 8:16], best[:, h, 8:16], cand_work[:, h, :]))
                cnt.add(v.tensor_tensor(sel_e[:, bass.ds(tt * PH, PH), :], best[:, :, :],
                                        best[:, :, 0:1].to_broadcast([P, PH, TOPK]), ALU.subtract))
                sync()
                pf = pos.rearrange("p h k -> p (h k)")
                cnt.add(v.tensor_scalar(pos_a[:, :], pf, 4, None, ALU.logical_shift_right))
                cnt.add(v.tensor_scalar(pos_b[:, :], pf, 15, None, ALU.bitwise_and))
                sync()
                iv = top_i.rearrange("p (h two) k -> p h two k", two=2)
                for half, (pp, dst) in enumerate(((pos_a, sel_i), (pos_b, sel_j))):
                    cnt.link(v.tensor_tensor(eq[:, :, :], pp[:, :].unsqueeze(2).to_broadcast([P, PH * TOPK, TOPK]),
                                             iota[:, 0:TOPK].unsqueeze(1).to_broadcast([P, PH * TOPK, TOPK]), ALU.is_equal))
                    cnt.link(v.tensor_tensor(eq2.rearrange("p (h k) r -> p h k r", h=PH),
                                             eq.rearrange("p (h k) r -> p h k r", h=PH),
                                             iv[:, :, half, :].unsqueeze(2).to_broadcast([P, PH, TOPK, TOPK]), ALU.mult))
                    v.tensor_reduce(dst[:, bass.ds(tt, 1), :].rearrange("p o k -> p (o k)"), eq2[:, :, :],
                                    AX.X, ALU.add).then_inc(logits_ready, 1)
            ROUTE_STEPS = 1 + 2 * PH * 5 + PH * 6 + 1 + 2 + 4
            with dve.Fori(0, TT) as tt:
                cnt = Steps(dve, dve_step)
                cnt.n = tt * ROUTE_STEPS + n0
                route_tile(tt, cnt)
            step.n = n0 + TT * ROUTE_STEPS
            dve.wait_ge(exp_all, 1)
            step.link(v.tensor_reduce(sel_s[:, :], sel_e[:, :, :], AX.X, ALU.add))
            step.link(v.reciprocal(sel_r[:, :], sel_s[:, :]))
            v.tensor_tensor(sel_e[:, :, :], sel_e[:, :, :], sel_r[:, :].unsqueeze(2).to_broadcast([P, TT * PH, TOPK]),
                            ALU.mult).then_inc(sel_ready, 1)
            dve.wait_ge(sel_turned, 1)
            step.add(v.tensor_copy(kt_i[:, :], bank(0)))
            step.add(v.tensor_copy(kt_j[:, :], bank(1)))
            step.add(v.tensor_copy(kt_g[:, :], bank(2)))
            step.sync()
            step.link(v.tensor_copy(kt_ghi[:, :], kt_g[:, :]))
            step.link(v.tensor_tensor(kt_glo[:, :], kt_g[:, :], kt_ghi[:, :].bitcast(F32), ALU.subtract))

            def onehots(u, b, first=False):
                if not first:
                    dve.wait_ge(g_built, u - 1)
                for q in range(G_TOK):
                    tok = G_TOK * u + q
                    def at(t):
                        return t[:, bass.ds(tok, 1)]
                    v.tensor_scalar(oh_i[b][:, q, :], iota[:, :], at(kt_i), None, ALU.is_equal)
                    v.tensor_scalar(oh_jhi[b][:, q, :], iota[:, :], at(kt_j), at(kt_ghi[:, :].bitcast(F32)), ALU.is_equal, ALU.mult)
                    ins = v.tensor_scalar(oh_jlo[b][:, q, :], iota[:, :], at(kt_j), at(kt_glo), ALU.is_equal, ALU.mult)
                ins.then_inc(oh_ready, 1)
            onehots(0, 0, True)
            onehots(1, 1, True)
            with dve.Fori(1, T // G_TOK // 2) as i:
                onehots(2 * i, 0)
                onehots(2 * i + 1, 1)

            def weigh(j, half, b, q, first=False):
                if b == 0:
                    dve.wait_ge(pair_in[q], 32 * half + 32)
                v.tensor_tensor(a_f[b].rearrange("p (k t) -> p k t", t=G_BLK),
                                gh_in[q][:, b, :].rearrange("p (k t) -> p k t", t=G_BLK),
                                g_in[q][:, :, b, :], ALU.mult).then_inc(a_ready, 1)
                dve.wait_ge(a_hi_s, j + 1)
                if not first:
                    dve.wait_ge(ring_used, R_V + j - 1)
                v.tensor_tensor(a_lo[b][:, :], a_f[b][:, :], a_hi[b][:, :].bitcast(F32), ALU.subtract).then_inc(a_lo_s, 1)
            for n in range(4):
                weigh(n, 0, n % 2, n // 2, n < 2)
            with dve.Fori(1, JT // 4) as i:
                for n in range(4):
                    weigh(4 * i + n, i, n % 2, n // 2)
            for tt in range(TT):
                dve.wait_ge(ostd_ready, tt + 1)
                step.link(v.reciprocal(rs[:, tt:tt + 1], std[:, tt:tt + 1]))
                step.link(v.scalar_tensor_tensor(out=ytmp[tt % 2][:, :], in0=banks2(2 * tt, D), scalar=rs[:, tt:tt + 1],
                                                 in1=g_row[:, 1, :], op0=ALU.mult, op1=ALU.mult))
                v.tensor_tensor(x_sb[:, tt, :], x_sb[:, tt, :], ytmp[tt % 2][:, :], ALU.add).then_inc(out_ready, 1)

        @block.tensor
        def _(pe):
            mm = nc.tensor.matmul

            def mod(half, b, first=False):
                c = 2 * half + b
                pe.wait_ge(ada_in[b], 16 * half + 16)
                if not first:
                    pe.wait_ge(mod_copied, c - 1)
                for m in range(ADA_W // P):
                    for k in range(KC):
                        ins = mm(ps[:, 2 + b, 2 * m:2 * m + 2], ada[b][:, k, m * P:(m + 1) * P], silu[:, k, :],
                                 start=(k == 0), stop=(k == KC - 1))
                ins.then_inc(mod_done, 1)

            def ring_wait(t):
                pe.wait_ge(ring_hi, t + 1)
                pe.wait_ge(ring_lo, t + 1)

            def project(b, dst, hi_t, lo_t, n):
                q = 0
                for k in range(KC):
                    ks = slice(k * P, (k + 1) * P)
                    for w, m in ((w_hi[b], hi_t), (w_hi[b], lo_t), (w_lo[b], hi_t)):
                        ins = mm(dst, w[:, ks], m[:, k, :], start=(q == 0), stop=(q == 3 * KC - 1))
                        q += 1
                return ins

            pe.wait_ge(silu_ready, 1)
            mod(0, 0, True)
            mod(0, 1, True)
            with pe.Fori(1, ADA_FIRST // 2) as i:
                mod(i, 0)
                mod(i, 1)
            pe.wait_ge(const_in, 96)
            pe.wait_ge(xn_ready, TT + CT)
            for k in range(KC):
                for s, (t0, tn) in enumerate(((0, TT), (TT, CT))):
                    if k >= 2:
                        pe.wait_ge(ht_lo_ready, 2 * (k - 2) + s + 1)
                    for n in range(tn):
                        ins = nc.tensor.transpose(ps[:, 4 + 2 * (k % 2) + s, n * P:(n + 1) * P],
                                                  xn[:, t0 + n, k * P:(k + 1) * P], ident[:, :])
                    ins.then_inc(ht_turned, 1)
            pe.wait_ge(ht_lo_ready, 2 * KC)
            for t in range(4):
                ring_wait(t)
                if t < 2:
                    project(t, bank(2 * t), ht_hi, ht_lo, T)
                    ins = project(t, bank(2 * t + 1, C), hc_hi, hc_lo, C)
                else:
                    ins = project(t % 2, bank(2 + t), ht_hi, ht_lo, T)
                ins.then_inc(ring_used, 1)
            pe.wait_ge(kvq_copied, 3)
            pe.wait_ge(krt_ready, 1)

            def plain_tile(t, n, b, first=False):
                ring_wait(t)
                if not first:
                    pe.wait_ge(tile_copied, n - 1)
                project(b, bank(b), ht_hi, ht_lo, T).then_inc(ring_used, 1)
            plain_tile(R_POOLX, 0, 0, True)
            plain_tile(R_POOLX + 1, 1, 1, True)
            with pe.Fori(1, 4) as i:
                for b in range(2):
                    plain_tile(R_POOLX + 2 * i + b, 2 * i + b, b)
            pe.wait_ge(ones_ready, 1)
            pe.wait_ge(sq_ready, 1)
            mm(bank(6), ones[:, :], sq[:, 0:T], start=True, stop=True)
            mm(bank(7, C), ones[:, :], sq[:, T:KEYS], start=True, stop=True)
            mm(bank(4), ones[:, :], sq[:, KEYS:KEYS + T], start=True, stop=False)
            mm(bank(4), ones[:, :], sq[:, KEYS + T:KEYS + 2 * T], start=False, stop=True).then_inc(sums_done, 1)
            pe.wait_ge(tile_copied, 8)
            mm(bank(5), fold[:, :], krt[:, 0:T], start=True, stop=True)
            mm(bank(1, C), fold[:, :], krt[:, T:KEYS], start=True, stop=True).then_inc(sums_done, 1)
            pe.wait_ge(nstd_ready, 1)
            pe.wait_ge(split_lo, 1)
            with pe.Fori(0, 8) as i:
                for b in range(2):
                    plain_tile(R_GATES + 2 * i + b, 8 + 2 * i + b, b)
                    mod(ADA_FIRST // 2 + i, b)
            pe.wait_ge(pooled_lo, 4)
            pe.wait_ge(tile_copied, 24)
            pe.wait_ge(mod_copied, ADA_CHUNKS)
            for m in range(KC):
                g, half = m // 2, m % 2
                t = R_WPOOL + g // 2
                b = t % 2
                if m % 4 == 0:
                    ring_wait(t)
                q = 0
                for k in range(2):
                    at = (g % 2) * 512 + k * 256 + half * P
                    for w, x in ((w_hi[b], ht_hi), (w_hi[b], ht_lo), (w_lo[b], ht_hi)):
                        ins = mm(bank(m), w[:, at:at + P], x[:, 2 * g + k, :], start=(q == 0), stop=(q == 5))
                        q += 1
                if m % 4 == 3:
                    ins.then_inc(ring_used, 1)
            for n in range(2):
                pe.wait_ge(diag_ready, (n + 1) * KC)
                pe.wait_ge(pmix_used, KC)
                for q in range(2):
                    ins = mm(bank(2 * n + q), ones[:, :], diag[:, n, q * 512:(q + 1) * 512], start=True, stop=True)
                ins.then_inc(rows_done, 1)
            pe.wait_ge(rows_ready, 2)

            def three(dst, parts):
                last = 3 * len(parts) - 1
                q = 0
                for sh, sl, mh, ml in parts:
                    for w, m in ((sh, mh), (sh, ml), (sl, mh)):
                        ins = mm(dst, w, m, start=(q == 0), stop=(q == last))
                        q += 1
                return ins

            def scores(s, qt, first=False):
                if not first:
                    pe.wait_ge(exp_ready, s - 1)
                qs = slice(qt * P, (qt + 1) * P)
                for dst, ks in ((bank(2 * (qt % 2)), slice(0, T)), (bank(2 * (qt % 2) + 1, C), slice(T, KEYS))):
                    ins = three(dst, [(qn_hi[:, qs], qn_lo[:, qs], k_hi[:, ks], k_lo[:, ks]),
                                      (qr_hi[:, qs], qr_lo[:, qs], kr_hi[:, ks], kr_lo[:, ks])])
                ins.then_inc(s_done, 1)

            def turn(s, qt, first=False):
                pe.wait_ge(prob_ready, s + 1)
                if not first:
                    pe.wait_ge(pt_lo_s, s)
                for k in range(KT):
                    ins = nc.tensor.transpose(banks2(4, KEYS)[:, k * P:(k + 1) * P],
                                              prob[qt % 2][:, k * P:(k + 1) * P], ident[:, :])
                ins.then_inc(pt_turned, 1)

            def value_product(n, pts):
                pe.wait_ge(pt_lo_s, pts)
                pe.wait_ge(pj_free, n)
                three(bank(6), [(v_hi[:, k, :], v_lo[:, k, :], pt_hi[:, k, :], pt_lo[:, k, :])
                                for k in range(KT)]).then_inc(pj_done, 1)

            def values(h, n, k0, kn, bk, freed):
                pe.wait_ge(wv_lo_s, h + 1)
                pe.wait_ge(pj_free, freed)
                for k in range(k0, k0 + kn):
                    ks = slice(k * P, (k + 1) * P)
                    ins = three(ps[:, bk, (k - k0) * P:(k - k0 + 1) * P],
                                [(kvn_hi[:, ks], kvn_lo[:, ks], wv_hi[:, :], wv_lo[:, :])])
                ins.then_inc(pj_done, 1)

            def queries_keys(h, n, freed=None):
                pe.wait_ge(wqk_lo_s, h + 1)
                if freed is not None:
                    pe.wait_ge(pj_free, n - 1)
                for q, (bk, at) in enumerate(((7, 0), (6, P))):
                    if q == 1 and freed is not None:
                        pe.wait_ge(pj_free, n)
                    three(bank(bk), [(wqk_hi[:, 2 * P * k + at:2 * P * k + at + P], wqk_lo[:, 2 * P * k + at:2 * P * k + at + P],
                                      cqn_hi[:, k, :], cqn_lo[:, k, :]) for k in range(2)]).then_inc(pj_done, 1)
                pe.wait_ge(pj_free, n + 1)
                wk = slice(4 * P, 5 * P)
                three(bank(7), [(wqk_hi[:, wk], wqk_lo[:, wk], kvn_hi[:, 0:T], kvn_lo[:, 0:T])]).then_inc(pj_done, 1)
                pe.wait_ge(pj_free, n + 2)
                three(bank(6, C), [(wqk_hi[:, wk], wqk_lo[:, wk], kvn_hi[:, T:KEYS], kvn_lo[:, T:KEYS])]).then_inc(pj_done, 1)

            def head(h, n, head0=False, last=False):
                s = 4 * h
                pe.wait_ge(pj_free, 4 if head0 else n)
                scores(s, 0, head0)
                scores(s + 1, 1, head0)
                if not head0:
                    value_product(n, s)
                values(h, n + 1, 0, 4, 7, 4 if head0 else n)
                turn(s, 0, head0)
                scores(s + 2, 2)
                values(h, n + 2, 4, 2, 6, 4 if head0 else n + 1)
                turn(s + 1, 1)
                scores(s + 3, 3)
                turn(s + 2, 2)
                if not last:
                    queries_keys(h + 1, n + 3, True)
                turn(s + 3, 3)

            pe.wait_ge(split_lo, 3)
            queries_keys(0, 0)
            head(0, 3, head0=True)
            with pe.Fori(1, H - 1) as h:
                head(h, 7 * h + 3)
            head(H - 1, 7 * (H - 1) + 3, last=True)
            pe.wait_ge(pt_lo_s, 4 * H)
            three(bank(6), [(v_hi[:, k, :], v_lo[:, k, :], pt_hi[:, k, :], pt_lo[:, k, :])
                            for k in range(KT)]).then_inc(pj_done, 1)

            def rows(b, sh, sl, start, stop, done=None):
                for tt in range(TT):
                    ts = slice(tt * P, (tt + 1) * P)
                    for q, (s_, w_) in enumerate(((sh, w_hi[b]), (sh, w_lo[b]), (sl, w_hi[b]))):
                        for dh in range(2):
                            ins = mm(bank(2 * tt + dh), s_[:, ts], w_[:, dh * 512:(dh + 1) * 512],
                                     start=start and q == 0, stop=stop and q == 2)
                    if done is not None and tt < TT - 1:
                        ins.then_inc(done, 1)
                ins.then_inc(ring_used, 1)
            pe.wait_ge(pj_free, 7 * H)
            for k in range(KC):
                t = R_WOUT + k
                ring_wait(t)
                last = k == KC - 1
                rows(t % 2, ht_hi[:, k, :], ht_lo[:, k, :], k == 0, last, y_done if last else None)
            pe.wait_ge(xmn_ready, TT)
            for k in range(KC):
                if k >= 4:
                    pe.wait_ge(hf_lo_ready, k - 3)
                for tt in range(TT):
                    ins = nc.tensor.transpose(ps[:, k % 4, tt * P:(tt + 1) * P], xm_n[:, tt, k * P:(k + 1) * P], ident[:, :])
                ins.then_inc(hf_turned, 1)
            pe.wait_ge(hf_lo_ready, KC)
            def q_tile(m, b, first=False):
                ring_wait(R_WQ + m)
                if not first:
                    pe.wait_ge(q_lo_s, m - 1)
                project(b, bank(b), ht_hi, ht_lo, T).then_inc(ring_used, 1)

            def score_tile(m, b, first=False):
                pe.wait_ge(q_lo_s, m + 1)
                if not first:
                    pe.wait_ge(sc_copied, m - 1)
                for tt in range(TT):
                    ts = slice(tt * P, (tt + 1) * P)
                    ins = three(ps[:, 2 + b, tt * P:(tt + 1) * P],
                                [(q_hi[b][:, ts], q_lo[b][:, ts], keys_hi[:, b, :], keys_lo[:, b, :])])
                ins.then_inc(sc_done, 1)
            q_tile(0, 0, True)
            q_tile(1, 1, True)
            pe.wait_ge(keys_lo_s, 1)
            score_tile(0, 0, True)
            q_tile(2, 0)
            score_tile(1, 1, True)
            with pe.Fori(1, PH - 1) as i:
                q_tile(2 * i + 1, 1)
                score_tile(2 * i, 0)
                q_tile(2 * i + 2, 0)
                score_tile(2 * i + 1, 1)
            q_tile(2 * PH - 1, 1)
            score_tile(2 * PH - 2, 0)
            score_tile(2 * PH - 1, 1)

            def expert(j, b, first=False):
                ring_wait(R_U + j)
                if not first:
                    pe.wait_ge(gelu_done, j - 1)
                project(b, bank(4 + b), ht_hi, ht_lo, T).then_inc(ring_used, 1)

            def gate_matrices(u, b, first=False):
                pe.wait_ge(oh_ready, u + 1)
                if not first:
                    pe.wait_ge(g_copied, u)
                for q in range(G_TOK):
                    dst = ps[:, 6 + q // 4, (q % 4) * NK:(q % 4 + 1) * NK]
                    mm(dst, oh_i[b][:, q, :], oh_jhi[b][:, q, :], start=True, stop=False)
                    ins = mm(dst, oh_i[b][:, q, :], oh_jlo[b][:, q, :], start=False, stop=True)
                ins.then_inc(g_built, 1)
            expert(0, 0, True)
            expert(1, 1, True)
            with pe.Fori(1, JT // 4) as i:
                expert(2 * i, 0)
                expert(2 * i + 1, 1)
            pe.wait_ge(sel_ready, 1)
            for n, src in enumerate((sel_i, sel_j, None)):
                for tt in range(TT):
                    m = src[:, tt, :] if src is not None else \
                        sel_e[:, tt * PH:(tt + 1) * PH, :].rearrange("p h k -> p (h k)")
                    ins = nc.tensor.transpose(ps[:, n, tt * P:(tt + 1) * P], m, ident[:, :])
            ins.then_inc(sel_turned, 1)
            expert(JT // 2, 0)
            gate_matrices(0, 0, True)
            expert(JT // 2 + 1, 1)
            gate_matrices(1, 1)
            with pe.Fori(1, JT // 4) as i:
                for b in range(2):
                    expert(JT // 2 + 2 * i + b, b)
                    gate_matrices(2 * i + b, b)
            pe.wait_ge(gelu_done, JT)
            pe.wait_ge(g_copied, T // G_TOK)

            def combine(j, b, start=False, stop=False):
                ring_wait(R_V + j)
                pe.wait_ge(a_lo_s, j + 1)
                rows(b, a_hi[b], a_lo[b], start, stop, o_done if stop else None)
            combine(0, 0, start=True)
            combine(1, 1)
            with pe.Fori(1, JT // 2 - 1) as i:
                combine(2 * i, 0)
                combine(2 * i + 1, 1)
            combine(JT - 2, 0)
            combine(JT - 1, 1, stop=True)


def _tables():
    import numpy as np
    f = np.float32
    grid_w, n_freq = 64, 16
    t = np.arange(T)
    inv_freq = (f(10000.0) ** (-np.arange(n_freq, dtype=f) / f(n_freq))).astype(f)
    pos = np.stack([t // grid_w, t % grid_w]).astype(f)
    ang = pos[:, None, :] * inv_freq[None, :, None]
    cos, sin = np.cos(ang).astype(f), np.sin(ang).astype(f)
    rot = np.zeros((P, KEYS), f)
    rot[0:64, 0:T] = np.stack([cos, cos], 1).reshape(64, T)
    rot[64:128, 0:T] = np.stack([-sin, sin], 1).reshape(64, T)
    rot[0:64, T:KEYS] = 1.0
    edge = np.zeros((4, 2 * PAD), f)
    for g, w in enumerate(WINDOWS):
        for n in range(2 * PAD):
            tok = n if n < PAD else T - 2 * PAD + n
            edge[g, n] = w / (min(tok + w // 2, T) - max(tok - w // 2, 0))
    p = np.arange(P)
    return {
        "rot": rot,
        "edge": np.ascontiguousarray(np.broadcast_to(edge, (P, 4, 2 * PAD))),
        "ident": np.eye(P, dtype=f),
        "fold": (p[:, None] % 64 == p[None, :] % 64).astype(f),
        "iota": np.ascontiguousarray(np.broadcast_to(np.arange(P, dtype=f), (P, P))),
    }


def _layout(x, c, ctx, c_ctx, w_ada, b_ada, g_mix_pre, g_mix_post, g_ffn_pre, g_ffn_post, w_in, g_q_lora, w_uq,
            g_kv_lora, w_ukv, w_pool, pool_scale, w_out, peer_wq, peer_keys, peer_u, peer_v):
    import numpy as np

    def tiles(w):
        k, n = w.shape[0] // P, w.shape[1] // P
        return w.reshape(k, P, n, P).transpose(2, 1, 0, 3).reshape(n, P, k * P)

    def vec(a):
        return a.reshape(-1, P).T

    swap = (np.arange(64).reshape(2, 2, 16)[:, ::-1]).reshape(-1)
    win = w_in[0]
    rope = win[:, P:P + 64]
    w_in_t = tiles(np.concatenate([win[:, 0:P], rope, rope[:, swap], win[:, P + 64:]], axis=1))
    uq = w_uq[0].reshape(2, P, H, QDIM)
    uq = np.concatenate([uq[..., 0:P], uq[..., P:], uq[..., P:][..., swap]], axis=-1)
    ukv = w_ukv[0].reshape(P, H, 2 * P)
    wqk = np.concatenate([uq[0], uq[1], ukv[..., 0:P]], axis=-1).transpose(1, 0, 2)
    cols = np.concatenate([vec(b_ada[0]), vec(g_mix_pre[0]), vec(g_mix_post[0]), vec(g_ffn_pre[0]), vec(g_ffn_post[0]),
                           vec(pool_scale[0]), vec(g_q_lora[0]), vec(g_kv_lora[0]),
                           np.full((P, 1), EPS, np.float32)], axis=1)
    out = {
        "x": x[0], "ctx": ctx[0],
        "cond": np.stack([vec(c[0]), vec(c_ctx)], axis=-1),
        "cols": cols,
        "w_ada": w_ada[0].reshape(KC, P, ADA_CHUNKS, ADA_W).transpose(2, 1, 0, 3).reshape(ADA_CHUNKS, P, KC * ADA_W),
        "w_in": w_in_t,
        "w_pool": w_pool[0].reshape(2, 2, 2, P, 2 * P).transpose(0, 3, 1, 2, 4).reshape(2, P, D),
        "w_out": w_out[0].reshape(KC, P, D),
        "wq": tiles(peer_wq[0]),
        "wqk": wqk,
        "wv": ukv[..., P:].transpose(1, 0, 2),
        "keys": peer_keys[0].transpose(2, 0, 1),
        "u": peer_u[0].reshape(NK, JT, KC, P).transpose(1, 3, 2, 0).reshape(JT, P, D),
        "v": peer_v[0].reshape(NK, JT, D).transpose(1, 0, 2),
    }
    out.update(_tables())
    return {k: np.ascontiguousarray(w) for k, w in out.items()}


def kernel(**inputs):
    import numpy as _np
    import concourse.bacc as _bacc
    from concourse import mybir as _mybir
    from concourse.bass_utils import run_bass_kernel_spmd as _run

    nc = _bacc.Bacc("TRN2", target_bir_lowering=False, num_devices=1)
    arrays, aps = {}, {}
    for name, w in _layout(**{k: _np.asarray(v) for k, v in inputs.items()}).items():
        arrays[f"in_{name}"] = w
        aps[name] = nc.dram_tensor(f"in_{name}", w.shape, _mybir.dt.from_np(w.dtype), kind="ExternalInput").ap()
    out = nc.dram_tensor("out_0", (T, D), _mybir.dt.float32, kind="ExternalOutput").ap()
    build(nc, aps, out)
    r = _run(nc, [arrays], core_ids=[0])
    return r.results[0]["out_0"].reshape(1, T, D)
```

```python
import concourse.bass as bass
from concourse import mybir
from contextlib import ExitStack

F32 = mybir.dt.float32
F32R = mybir.dt.float32r
U32 = mybir.dt.uint32
ALU = mybir.AluOpType
ACT = mybir.ActivationFunctionType
AX = mybir.AxisListType

P = 128
D = 1024
KC = D // P
T = 512
TT = T // P
C = 256
CT = C // P
KEYS = T + C
H = 8
KT = KEYS // P
QDIM = 192
SCALE = float(QDIM) ** -0.5
WINDOWS = (2, 4, 8, 16)
PAD = 8
PH = 8
NK = 128
TOPK = 16
EPS = 1e-6
JT = 128
G_TOK = 8
G_BLK = 64
G_FIRST = 44
G_STEPS = G_BLK // G_TOK
G_PIECE = NK // G_STEPS

ADA_W = 256
ADA_PE = 2 * D // ADA_W
ADA_DVE = 4 * D // ADA_W

R_IN = 0
R_KVQ, R_POOLX, R_GATES = 0, 4, 12
R_WPOOL = 28
R_WOUT = R_WPOOL + 2
R_WQ = R_WOUT + KC
R_U = R_WQ + 2 * PH
R_V = R_U + JT
R_END = R_V + JT

COLS = {"b_ada": 48, "g_mix_pre": KC, "g_mix_post": KC, "g_ffn_pre": KC, "g_ffn_post": KC,
        "pool_scale": KC, "g_q": 2, "g_kv": 1, "eps": 1}
COL_AT = {}
_n = 0
for _k, _w in COLS.items():
    COL_AT[_k] = _n
    _n += _w
NCOLS = _n


class Steps:

    def __init__(self, eng, sem):
        self.eng, self.sem, self.n = eng, sem, 0

    def add(self, ins):
        ins.then_inc(self.sem, 1)
        self.n = self.n + 1

    def sync(self):
        self.eng.wait_ge(self.sem, self.n)

    def link(self, ins):
        self.add(ins)
        self.sync()


def build(nc, a, out):
    ctx = ExitStack()
    with ctx:
        arena_bytes = nc.sbuf_bytes_remaining // 64 * 64
        ctx.enter_context(nc.sbuf_tensor("arena", [P, arena_bytes // 4], F32))
        base = nc.sbuf_base - arena_bytes

        class Region:

            def __init__(self, at):
                self.at = at

            def __call__(self, name, shape, dt=F32):
                n = 4
                for s in shape[1:]:
                    n *= s
                n = (n + 31) // 32 * 32
                assert self.at + n <= arena_bytes, (name, self.at + n, arena_bytes)
                t = nc.alloc_sbuf_tensor_at(name, list(shape), dt, offset=base + self.at)
                self.at += n
                return t

        sb = Region(0)
        ident = sb("ident", [P, P])
        ones = sb("ones", [P, P])
        fold = sb("fold", [P, P])
        iota = sb("iota", [P, P])
        cols = sb("cols", [P, NCOLS])
        modraw = sb("modraw", [P, 2 * KC, 2])
        modf_raw = sb("modf_raw", [P, 4 * KC])
        modc = sb("modc", [P, 2 * KC, 2])
        modf = sb("modf", [P, 4 * KC])
        a_mix = sb("a_mix", [P, KC, 2])
        a_ffn = sb("a_ffn", [P, KC])
        gcol = sb("gcol", [P, 2, KC])
        cond = sb("cond", [P, KC, 2])
        silu = sb("silu", [P, KC, 2])
        edge = sb("edge", [P, 4, 2 * PAD])
        ss = sb("ss", [P, 8])
        std = sb("std", [P, 8])
        rs = sb("rs", [P, 8])
        ss2 = sb("ss2", [P, 8])
        std2 = sb("std2", [P, 8])
        rs2 = sb("rs2", [P, 8])
        spacer = sb("spacer", [P, 1])
        g_row = sb("g_row", [P, 2, D])
        x_sb = sb("x_sb", [P, TT, D])
        w_raw = [sb(f"w_raw{b}", [P, D]) for b in range(2)]
        w_hi = [sb(f"w_hi{b}", [P, D], F32R) for b in range(2)]
        w_lo = [sb(f"w_lo{b}", [P, D], F32R) for b in range(2)]
        ht_hi = sb("ht_hi", [P, KC, T], F32R)
        ht_lo = sb("ht_lo", [P, KC, T], F32R)
        S = sb.at
        over = Region(S - 2 * 4 * KC * T)
        ada_h = [over(f"ada_h{b}", [P, KC, ADA_W]) for b in range(4)]

        sb = Region(S)
        ada = [sb(f"ada{b}", [P, KC, ADA_W]) for b in range(2)]
        hc_hi = sb("hc_hi", [P, KC, C], F32R)
        hc_lo = sb("hc_lo", [P, KC, C], F32R)
        over = Region(sb.at - 2 * 4 * KC * C)
        ada_c = [over(f"ada_c{b}", [P, KC, ADA_W]) for b in range(2)]
        silu_row = Region(sb.at - 4 * D)("silu_row", [P, D])
        sq = Region(sb.at - 2 * 4 * KC * C)("sq", [P, KEYS + 2 * T])
        nstd = Region(sb.at - 2 * 4 * KC * C + 4 * (KEYS + 2 * T))("nstd", [P, KEYS + T])
        poolx = sb("poolx", [P, 2 * 4, T + 2 * PAD])
        POOLW_AT = sb.at
        poolw = [sb(f"poolw{b}", [P, 2, T + 2 * PAD]) for b in range(2)]
        ckv = sb("ckv", [P, KEYS])
        cq = sb("cq", [P, 2, T])
        krt = sb("krt", [P, KEYS])
        KV_AT = sb.at
        rot = sb("rot", [P, KEYS])
        kvn_hi = sb("kvn_hi", [P, KEYS], F32R)
        kvn_lo = sb("kvn_lo", [P, KEYS], F32R)
        cqn_hi = sb("cqn_hi", [P, 2, T], F32R)
        cqn_lo = sb("cqn_lo", [P, 2, T], F32R)
        kr_hi = sb("kr_hi", [P, KEYS], F32R)
        kr_lo = sb("kr_lo", [P, KEYS], F32R)
        gates = sb("gates", [P, 2 * KC, T])
        over = Region(sb.at - 4 * 2 * KC * T)
        xn = over("xn", [P, TT + CT, D])
        ctx_sb = over("ctx_sb", [P, CT, D])
        assert over.at <= sb.at
        ada_pe = ada + ada_c + ada_h
        assert len(ada_pe) == ADA_PE
        over = Region(POOLW_AT)
        htmp = [over(f"htmp{b}", [P, T]) for b in range(2)]

        sb = Region(S)
        wqk_raw = sb("wqk_raw", [P, 5 * P])
        wqk_hi = sb("wqk_hi", [P, 5 * P], F32R)
        wqk_lo = sb("wqk_lo", [P, 5 * P], F32R)
        wv_raw = sb("wv_raw", [P, P])
        wv_hi = sb("wv_hi", [P, P], F32R)
        wv_lo = sb("wv_lo", [P, P], F32R)
        qn_hi = sb("qn_hi", [P, T], F32R)
        qn_lo = sb("qn_lo", [P, T], F32R)
        qr_f = sb("qr_f", [P, T])
        qr_hi = sb("qr_hi", [P, T], F32R)
        qr_lo = sb("qr_lo", [P, T], F32R)
        k_hi = sb("k_hi", [P, KEYS], F32R)
        k_lo = sb("k_lo", [P, KEYS], F32R)
        v_hi = sb("v_hi", [P, KT, P], F32R)
        v_lo = sb("v_lo", [P, KT, P], F32R)
        prob = [sb(f"prob{b}", [P, KEYS]) for b in range(2)]
        mrg = sb("mrg", [P, T])
        rowmax = sb("rowmax", [P, TT])
        nmax = sb("nmax", [P, TT])
        rsum = sb("rsum", [P, TT])
        rinv = sb("rinv", [P, TT])
        pt_hi = sb("pt_hi", [P, KT, T], F32R)
        pt_lo = sb("pt_lo", [P, KT, T], F32R)
        assert sb.at <= KV_AT, (sb.at, KV_AT)

        sb = Region(S)
        s_sb = sb("s_sb", [P, TT, 2 * PH, NK])
        diag = sb("diag", [P, 2, D])
        xm_n = sb("xm_n", [P, TT, D])
        ytmp = [sb(f"ytmp{b}", [P, D]) for b in range(2)]
        ftmp = [sb(f"ftmp{b}", [P, T]) for b in range(2)]
        junk = sb("junk", [P, D])
        sb = Region(S + 4 * TT * 2 * PH * NK)
        q_hi = [sb(f"q_hi{b}", [P, T], F32R) for b in range(2)]
        q_lo = [sb(f"q_lo{b}", [P, T], F32R) for b in range(2)]
        keys_raw = sb("keys_raw", [P, 2, NK])
        keys_hi = sb("keys_hi", [P, 2, NK], F32R)
        keys_lo = sb("keys_lo", [P, 2, NK], F32R)
        sb = Region(S + 4 * TT * 2 * PH * NK + 4 * 4 * T + 3 * 4 * 2 * NK)
        RT = sb.at
        s_cur = sb("s_cur", [P, 2 * PH, NK])
        s_work = sb("s_work", [P, 2 * PH, NK])
        ROUTE_END = sb.at
        cand = Region(RT)("cand", [P, PH, TOPK * TOPK])
        cand_work = Region(ROUTE_END - 4 * 2 * PH * NK)("cand_work", [P, PH, TOPK * TOPK])
        eq = sb("eq", [P, PH * TOPK, TOPK])
        eq2 = sb("eq2", [P, PH * TOPK, TOPK])
        top = sb("top", [P, 2 * PH, TOPK])
        top_i = sb("top_i", [P, 2 * PH, TOPK], U32)
        best = sb("best", [P, PH, TOPK])
        pos = sb("pos", [P, PH, TOPK], U32)
        pos_a = sb("pos_a", [P, PH * TOPK], U32)
        pos_b = sb("pos_b", [P, PH * TOPK], U32)
        ROUTE_TMP_END = sb.at
        sel_i = sb("sel_i", [P, TT, PH * TOPK])
        sel_j = sb("sel_j", [P, TT, PH * TOPK])
        sel_e = sb("sel_e", [P, TT * PH, TOPK])
        sel_s = sb("sel_s", [P, TT * PH])
        sel_r = sb("sel_r", [P, TT * PH])
        kt_i = sb("kt_i", [P, T])
        kt_j = sb("kt_j", [P, T])
        kt_ghi = sb("kt_ghi", [P, T], F32R)
        kt_g = sb("kt_g", [P, T])
        kt_glo = sb("kt_glo", [P, T])
        gh = [sb(f"gh{b}", [P, T]) for b in range(2)]
        KEEP_END = sb.at
        sb = Region(S)
        g_blk = [sb(f"g_blk{b}", [P, NK, G_BLK]) for b in range(2)]
        assert sb.at <= ROUTE_TMP_END, (sb.at, ROUTE_TMP_END)
        oh_i = [sb(f"oh_i{b}", [P, G_TOK, NK], F32R) for b in range(2)]
        eq_j = [sb("eq_j0", [P, G_TOK, NK])]
        assert sb.at <= ROUTE_TMP_END, (sb.at, ROUTE_TMP_END)
        sb = Region(KEEP_END)
        oh_j = [sb(f"oh_j{b}", [P, G_TOK, 2, NK], F32R) for b in range(2)]
        eq_j.append(sb("eq_j1", [P, G_TOK, NK]))
        g_lo = sb("g_lo", [P, G_TOK, NK])
        sb = Region(S)
        gh_in = [sb(f"gh_in{b}", [P, 2, T]) for b in range(2)]
        g_in = [sb(f"g_in{b}", [P, T // G_BLK, 2, G_BLK]) for b in range(2)]
        a_f = [sb(f"a_f{b}", [P, T]) for b in range(2)]
        a_hi = [sb(f"a_hi{b}", [P, T], F32R) for b in range(2)]
        a_lo = [sb(f"a_lo{b}", [P, T], F32R) for b in range(2)]

        ps = ctx.enter_context(nc.psum_tensor("ps", [P, 8, 512], F32))

        def bank(n, w=512):
            return ps[:, n, 0:w]

        def banks2(n, w):
            return ps[:, n:n + 2, :].rearrange("p a b -> p (a b)")[:, 0:w]

        def col(name, n=0):
            at = COL_AT[name] + n
            return cols[:, at:at + 1]

        gh_d = nc.dram_tensor("gelu_scratch", [JT, P, T], F32).ap()
        g_d = nc.dram_tensor("gate_scratch", [T // G_BLK, P, NK, G_BLK], F32).ap()

        def sem(name):
            return ctx.enter_context(nc.semaphore(name))

        cond_in, crow_in, const_in, x_in, keys_in = map(sem, ("cond_in", "crow_in", "const_in", "x_in", "keys_in"))
        ring_in = [sem(f"ring_in{b}") for b in range(2)]
        ring_hi, ring_lo, ring_used = sem("ring_hi"), sem("ring_lo"), sem("ring_used")
        ada_in = [sem(f"ada_in{b}") for b in range(ADA_PE)]
        modf_done = sem("modf_done")
        mod_done, mod_copied = sem("mod_done"), sem("mod_copied")
        silu_ready, ones_ready, pads_ready = sem("silu_ready"), sem("ones_ready"), sem("pads_ready")
        dve_step, act_step = sem("dve_step"), sem("act_step")
        xstd_ready, xn_ready, amix_ready = sem("xstd_ready"), sem("xn_ready"), sem("amix_ready")
        ht_turned, ht_hi_ready, ht_lo_ready = sem("ht_turned"), sem("ht_hi_ready"), sem("ht_lo_ready")
        kvq_copied, krt_ready, sq_ready = map(sem, ("kvq_copied", "krt_ready", "sq_ready"))
        sums_done, nstd_ready, normed, split_hi, split_lo = map(
            sem, ("sums_done", "nstd_ready", "normed", "split_hi", "split_lo"))
        tile_copied = sem("tile_copied")
        pooled_ready, pooled_hi, pooled_lo, pmix_used = map(
            sem, ("pooled_ready", "pooled_hi", "pooled_lo", "pmix_used"))
        diag_ready, rows_done, rows_ready = sem("diag_ready"), sem("rows_done"), sem("rows_ready")
        wqk_in, wv_in, wqk_hi_s, wqk_lo_s, wv_hi_s, wv_lo_s = map(
            sem, ("wqk_in", "wv_in", "wqk_hi_s", "wqk_lo_s", "wv_hi_s", "wv_lo_s"))
        pj_done, pj_hi, pj_free = sem("pj_done"), sem("pj_hi"), sem("pj_free")
        qr_rotated = sem("qr_rotated")
        s_done, max_ready, exp_ready, prob_ready = map(sem, ("s_done", "max_ready", "exp_ready", "prob_ready"))
        pt_turned, pt_hi_s, pt_lo_s = sem("pt_turned"), sem("pt_hi_s"), sem("pt_lo_s")
        mrg_ready = sem("mrg_ready")
        y_done, ystd_ready, xmid_ready, xmstd_ready, xmn_ready = map(
            sem, ("y_done", "ystd_ready", "xmid_ready", "xmstd_ready", "xmn_ready"))
        hf_turned, hf_hi_ready, hf_lo_ready = sem("hf_turned"), sem("hf_hi_ready"), sem("hf_lo_ready")
        keys_hi_s, keys_lo_s = sem("keys_hi_s"), sem("keys_lo_s")
        q_hi_s, q_lo_s, sc_done, sc_copied = map(sem, ("q_hi_s", "q_lo_s", "sc_done", "sc_copied"))
        gelu_done = sem("gelu_done")
        gh_stored = [sem(f"gh_stored{b}") for b in range(2)]
        g_stored = [sem(f"g_stored{b}") for b in range(2)]
        logits_ready, exp_all, sel_ready, sel_turned = map(sem, ("logits_ready", "exp_all", "sel_ready", "sel_turned"))
        kt_ready, eqj_ready, oh_ready, oh_lo_ready, g_built, g_lo_ready, g_copied = map(
            sem, ("kt_ready", "eqj_ready", "oh_ready", "oh_lo_ready", "g_built", "g_lo_ready", "g_copied"))

        def g_parts():
            return ps[:, 0:4, :].rearrange("p a x -> p (a x)").rearrange("p (t s n) -> p t s n", s=2, n=NK)
        pair_in = [sem(f"pair_in{b}") for b in range(2)]
        a_ready, a_hi_s, a_lo_s = sem("a_ready"), sem("a_hi_s"), sem("a_lo_s")
        o_done, ostd_ready, out_ready, out_stored = map(sem, ("o_done", "ostd_ready", "out_ready", "out_stored"))

        block = ctx.enter_context(nc.Block())

        def ring_src(t0, n):
            for name, first, count in (("w_in", R_IN, 28), ("w_pool", R_WPOOL, 2), ("w_out", R_WOUT, KC),
                                       ("wq", R_WQ, 2 * PH), ("u", R_U, JT), ("v", R_V, JT)):
                if first <= t0 and t0 + n <= first + count:
                    return a[name], t0 - first
            raise AssertionError(t0)

        @block.sync
        def _(sp):
            def ring(t, off, src, b, first=False):
                if not first:
                    sp.wait_ge(ring_lo, t - 1)
                sp.dma_start(w_raw[b][:, :], src[bass.ds(off, 1)].rearrange("o p n -> (o p) n")).then_inc(ring_in[b], 16)

            def ring_at(t):
                src, off = ring_src(t, 1)
                ring(t, off, src, t % 2, first=t < 2)

            def ada_row_load(c, b):
                if isinstance(c, int) and c < 2:
                    sp.wait_ge(mod_done, c + 1)
                else:
                    sp.wait_ge(modf_done, 2 * c - 2)
                sp.dma_start(ada[b].rearrange("p k n -> p (k n)"),
                             a["w_ada_r"][bass.ds(c, 1)].rearrange("o p n -> (o p) n")).then_inc(ada_in[b], 16)

            for c in range(ADA_PE):
                sp.dma_start(ada_pe[c].rearrange("p k n -> p (k n)"), a["w_ada_c"][c]).then_inc(ada_in[c], 16)
            ring_at(0)
            ring_at(1)
            ada_row_load(0, 0)
            ada_row_load(1, 1)
            with sp.Fori(0, R_GATES // 2 - 1) as i:
                for b in range(2):
                    ring(2 * i + 2 + b, 2 * i + 2 + b, a["w_in"], b)
            ring_at(R_GATES)
            ring_at(R_GATES + 1)
            with sp.Fori(0, 7) as i:
                for b in range(2):
                    ring(R_GATES + 2 + 2 * i + b, R_GATES + 2 + 2 * i + b, a["w_in"], b)
                    ada_row_load(2 + 2 * i + b, b)
            ring_at(R_WPOOL)
            ring_at(R_WPOOL + 1)
            def head_weights(h, first=False):
                if not first:
                    sp.wait_ge(wqk_lo_s, h)
                sp.dma_start(wqk_raw[:, :], a["wqk"][bass.ds(h, 1)].rearrange("o p n -> (o p) n")).then_inc(wqk_in, 16)
                if not first:
                    sp.wait_ge(wv_lo_s, h)
                sp.dma_start(wv_raw[:, :], a["wv"][bass.ds(h, 1)].rearrange("o p n -> (o p) n")).then_inc(wv_in, 16)
            sp.wait_ge(pooled_lo, 4)
            sp.wait_ge(split_lo, 3)
            sp.wait_ge(modf_done, 2 * ADA_DVE)
            head_weights(0, True)
            ring_at(R_WOUT)
            ring_at(R_WOUT + 1)
            with sp.Fori(1, H) as h:
                head_weights(h)
            for t in range(R_WOUT + 2, R_WQ):
                ring_at(t)
            with sp.Fori(0, PH) as i:
                for b in range(2):
                    ring(R_WQ + 2 * i + b, 2 * i + b, a["wq"], b)
            ring_at(R_U)
            ring_at(R_U + 1)

            def store_gelu(j, b):
                sp.wait_ge(gelu_done, j + 1)
                sp.dma_start(gh_d[bass.ds(j, 1)].rearrange("o p n -> (o p) n"), gh[b][:, :]).then_inc(gh_stored[b], 16)

            def u_step(half, b):
                j = 2 * half + b
                ring(R_U + 2 + j, j + 2, a["u"], b)
                store_gelu(j, b)
            with sp.Fori(0, (G_FIRST + G_STEPS) // 2) as i:
                u_step(i, 0)
                u_step(i, 1)

            def g_store(blk, piece, bb):
                sp.wait_ge(g_copied, (blk + 1) * G_STEPS)
                ns = bass.ds(G_PIECE * piece, G_PIECE)
                sp.dma_start(g_d[bass.ds(blk, 1), :, ns, :].rearrange("o p n t -> (o p) n t"),
                             g_blk[bb][:, ns, :]).then_inc(g_stored[bb], 16)
            with sp.Fori(0, T // G_BLK // 2) as q:
                for bb in range(2):
                    with sp.Fori(0, G_STEPS // 2) as i:
                        for b in range(2):
                            u_step((G_FIRST + G_STEPS) // 2 + (2 * q + bb) * (G_STEPS // 2) + i, b)
                            g_store(2 * q + bb, 2 * i + b, bb)
            with sp.Fori((G_FIRST + G_STEPS + T // G_TOK) // 2, JT // 2 - 1) as i:
                u_step(i, 0)
                u_step(i, 1)
            for b in range(2):
                sp.wait_ge(g_stored[b], 16 * T // G_BLK // 2 * G_STEPS)
                sp.wait_ge(gh_stored[b], 16 * 2)
            def pair_load(p, b):
                sp.dma_start(gh_in[b][:, :, :], gh_d[bass.ds(2 * p, 2)].rearrange("j p t -> p j t")).then_inc(pair_in[b], 16)
                sp.dma_start(g_in[b][:, :, :, :], g_d[:, :, bass.ds(2 * p, 2), :].rearrange("k p j t -> p k j t")).then_inc(pair_in[b], 16)
            pair_load(0, 0)
            pair_load(1, 1)
            ring_at(R_V)
            store_gelu(JT - 2, 0)
            ring_at(R_V + 1)
            store_gelu(JT - 1, 1)
            for b in range(2):
                sp.wait_ge(gh_stored[b], 16 * JT // 2)
            with sp.Fori(0, JT // 4 - 1) as i:
                for q in range(2):
                    for b in range(2):
                        t = 4 * i + 2 * q + b
                        ring(R_V + 2 + t, t + 2, a["v"], b)
                    sp.wait_ge(a_ready, 4 * i + 2 * q + 2)
                    pair_load(2 * i + q + 2, q)
            ring_at(R_END - 2)
            ring_at(R_END - 1)
            for tt in range(TT):
                sp.wait_ge(out_ready, tt + 1)
                sp.dma_start(out[tt * P:(tt + 1) * P, :], x_sb[:, tt, :]).then_inc(out_stored, 16)
            sp.wait_ge(out_stored, 16 * TT)

        @block.gpsimd
        def _(pool):
            def lo(t, b):
                pool.wait_ge(ring_hi, t + 1)
                nc.gpsimd.tensor_tensor(w_lo[b][:, :], w_raw[b][:, :], w_hi[b][:, :].bitcast(F32),
                                        ALU.subtract).then_inc(ring_lo, 1)

            def head_lo(h):
                pool.wait_ge(wqk_hi_s, h + 1)
                nc.gpsimd.tensor_tensor(wqk_lo[:, :], wqk_raw[:, :], wqk_hi[:, :].bitcast(F32),
                                        ALU.subtract).then_inc(wqk_lo_s, 1)
                pool.wait_ge(wv_hi_s, h + 1)
                nc.gpsimd.tensor_tensor(wv_lo[:, :], wv_raw[:, :], wv_hi[:, :].bitcast(F32),
                                        ALU.subtract).then_inc(wv_lo_s, 1)

            nc.gpsimd.memset(ones[:, :], 1.0).then_inc(ones_ready, 1)
            nc.gpsimd.memset(poolx[:, :, :], 0.0).then_inc(pads_ready, 1)
            with pool.Fori(0, R_WOUT // 2) as i:
                lo(2 * i, 0)
                lo(2 * i + 1, 1)
            head_lo(0)
            lo(R_WOUT, 0)
            lo(R_WOUT + 1, 1)
            with pool.Fori(1, H) as h:
                head_lo(h)
            with pool.Fori(R_WOUT // 2 + 1, (R_U + G_FIRST) // 2 + 1) as i:
                lo(2 * i, 0)
                lo(2 * i + 1, 1)

            def onehot_lo(u, b):
                pool.wait_ge(eqj_ready, u + 1)
                nc.gpsimd.tensor_tensor(oh_j[b][:, :, 1, :], eq_j[b][:, :, :],
                                        kt_glo[:, bass.ds(G_TOK * u, G_TOK)].unsqueeze(2).to_broadcast([P, G_TOK, NK]),
                                        ALU.mult).then_inc(oh_lo_ready, 1)
            onehot_lo(0, 0)
            onehot_lo(1, 1)
            with pool.Fori(1, T // G_TOK // 2) as i:
                for b in range(2):
                    lo(R_U + G_FIRST + 2 * i + b, b)
                    onehot_lo(2 * i + b, b)
            with pool.Fori((R_U + G_FIRST + T // G_TOK) // 2, R_END // 2) as i:
                lo(2 * i, 0)
                lo(2 * i + 1, 1)

        @block.scalar
        def _(act):
            step = Steps(act, act_step)

            def hi(half, b, first=False):
                act.wait_ge(ring_in[b], 16 * half + 16)
                if not first:
                    act.wait_ge(ring_used, 2 * half + b - 1)
                nc.scalar.activation(w_hi[b][:, :], w_raw[b][:, :], ACT.Copy).then_inc(ring_hi, 1)

            def mod_copy(c, b):
                act.wait_ge(mod_done, c + 1)
                nc.scalar.activation(modraw.rearrange("p m s -> p (m s)")[:, bass.ds(4 * c, 4)],
                                     ps[:, 2 + b, 0:4], ACT.Copy).then_inc(mod_copied, 1)

            act.dma_start(cond[:, :, :], a["cond"]).then_inc(cond_in, 16)
            act.dma_start(x_sb[:, :, :], a["x"].rearrange("(a p) d -> p a d", p=P)).then_inc(x_in, 16)
            act.dma_start(ctx_sb[:, :, :], a["ctx"].rearrange("(a p) d -> p a d", p=P)).then_inc(x_in, 16)
            act.dma_start(cols[:, :], a["cols"]).then_inc(const_in, 16)
            act.dma_start(ident[:, :], a["ident"]).then_inc(const_in, 16)
            act.dma_start(fold[:, :], a["fold"]).then_inc(const_in, 16)
            act.dma_start(iota[:, :], a["iota"]).then_inc(const_in, 16)
            act.dma_start(edge[:, :, :], a["edge"]).then_inc(const_in, 16)
            act.dma_start(rot[:, :], a["rot"]).then_inc(const_in, 16)
            act.wait_ge(cond_in, 16)
            nc.scalar.activation(silu[:, :, :], cond[:, :, :], ACT.Silu).then_inc(silu_ready, 1)

            act.wait_ge(x_in, 32)
            for n in range(TT + CT):
                src = x_sb[:, n, :] if n < TT else ctx_sb[:, n - TT, :]
                step.add(nc.scalar.activation(xn[:, n, :], src, ACT.Square, accum_out=ss[:, n:n + 1]))
            step.sync()
            act.wait_ge(const_in, 96)
            nc.scalar.activation(std[:, 0:6], ss[:, 0:6], ACT.Sqrt, scale=1.0 / D, bias=col("eps")).then_inc(xstd_ready, 1)
            with act.Fori(0, ADA_PE // 2) as i:
                mod_copy(2 * i, 0)
                mod_copy(2 * i + 1, 1)
            hi(0, 0, True)
            hi(0, 1, True)
            act.wait_ge(amix_ready, 2)
            for k in range(KC):
                for s, (n, dst) in enumerate(((T, ht_hi), (C, hc_hi))):
                    act.wait_ge(ht_turned, 2 * k + s + 1)
                    nc.scalar.activation(dst[:, k, :], bank(4 + 2 * (k % 2) + s, n), ACT.Identity,
                                         scale=a_mix[:, k, s:s + 1], bias=modc[:, k, s:s + 1]).then_inc(ht_hi_ready, 1)
            hi(1, 0)
            act.wait_ge(ring_used, 1)
            step.add(nc.scalar.activation(ckv[:, 0:T], bank(0), ACT.Copy))
            nc.scalar.activation(ckv[:, T:KEYS], bank(1, C), ACT.Copy).then_inc(kvq_copied, 1)
            hi(1, 1)
            hi(2, 0)
            act.wait_ge(ring_used, 3)
            nc.scalar.activation(cq[:, 0, :], bank(4), ACT.Copy).then_inc(kvq_copied, 1)
            hi(2, 1)
            act.wait_ge(ring_used, 4)
            nc.scalar.activation(cq[:, 1, :], bank(5), ACT.Copy).then_inc(kvq_copied, 1)
            act.dma_start(silu_row[:, :], a["c_row"]).then_inc(crow_in, 16)

            def pool_tile(half, b):
                n = 2 * half + b
                act.wait_ge(ring_used, R_POOLX + n + 1)
                nc.scalar.activation(poolx[:, bass.ds(n, 1), PAD:PAD + T].rearrange("p o t -> p (o t)"),
                                     bank(b), ACT.Copy).then_inc(tile_copied, 1)
                hi(R_POOLX // 2 + 1 + half, b)
            act.wait_ge(pads_ready, 1)
            with act.Fori(0, 4) as i:
                pool_tile(i, 0)
                pool_tile(i, 1)
            act.wait_ge(crow_in, 16)
            nc.scalar.activation(silu_row[:, :], silu_row[:, :], ACT.Silu).then_inc(silu_ready, 1)
            act.wait_ge(sums_done, 1)
            step.add(nc.scalar.activation(nstd[:, 0:KEYS], banks2(6, KEYS), ACT.Sqrt, scale=1.0 / P, bias=col("eps")))
            nc.scalar.activation(nstd[:, KEYS:KEYS + T], bank(4), ACT.Sqrt, scale=0.5 / P, bias=col("eps")).then_inc(nstd_ready, 1)
            act.wait_ge(sums_done, 2)
            nc.scalar.activation(kr_hi[:, 0:T], bank(5), ACT.Copy).then_inc(split_hi, 1)
            nc.scalar.activation(kr_hi[:, T:KEYS], bank(1, C), ACT.Copy).then_inc(split_hi, 1)

            def gate_tile(half, b, ahead=True):
                n = 2 * half + b
                act.wait_ge(ring_used, R_GATES + n + 1)
                nc.scalar.activation(gates[:, bass.ds(n, 1), :].rearrange("p o t -> p (o t)"),
                                     bank(b), ACT.Sigmoid).then_inc(tile_copied, 1)
                hi(R_GATES // 2 + 1 + half, b)
            with act.Fori(0, 8) as i:
                gate_tile(i, 0)
                gate_tile(i, 1)
            act.wait_ge(normed, 1)
            nc.scalar.activation(kvn_hi[:, :], ckv[:, :], ACT.Copy).then_inc(split_hi, 1)
            act.wait_ge(normed, 3)
            nc.scalar.activation(cqn_hi[:, :, :], cq[:, :, :], ACT.Copy).then_inc(split_hi, 1)
            for g in range(4):
                act.wait_ge(pooled_ready, g + 1)
                nc.scalar.activation(ht_hi[:, 2 * g:2 * g + 2, :], poolx[:, 2 * g:2 * g + 2, PAD:PAD + T],
                                     ACT.Copy).then_inc(pooled_hi, 1)
            for n in range(2):
                act.wait_ge(rows_done, n + 1)
                nc.scalar.activation(g_row[:, n, :], banks2(2 * n, D), ACT.Copy).then_inc(rows_ready, 1)

            def wqk_split(h, before=None):
                act.wait_ge(wqk_in, 16 * h + 16)
                if before is not None:
                    act.wait_ge(pj_done, before)
                nc.scalar.activation(wqk_hi[:, :], wqk_raw[:, :], ACT.Copy).then_inc(wqk_hi_s, 1)

            def wv_split(h):
                act.wait_ge(wv_in, 16 * h + 16)
                nc.scalar.activation(wv_hi[:, :], wv_raw[:, :], ACT.Copy).then_inc(wv_hi_s, 1)

            def pj(n, dst, src):
                act.wait_ge(pj_done, n + 1)
                nc.scalar.activation(dst, src, ACT.Copy).then_inc(pj_hi, 1)

            def prob_exp(s, qt, first=False):
                act.wait_ge(max_ready, s + 1)
                if not first:
                    act.wait_ge(pt_turned, s - 1)
                nc.scalar.activation(prob[qt % 2][:, :], banks2(2 * (qt % 2), KEYS), ACT.Exp, scale=SCALE,
                                     bias=nmax[:, qt:qt + 1], accum_out=rsum[:, qt:qt + 1]).then_inc(exp_ready, 1)

            def pt_hi_copy(s, qt):
                act.wait_ge(pt_turned, s + 1)
                nc.scalar.activation(pt_hi[:, :, qt * P:(qt + 1) * P], banks2(4, KEYS).rearrange("p (k q) -> p k q", q=P),
                                     ACT.Copy).then_inc(pt_hi_s, 1)

            def qk_part(h, n):
                pj(n, qn_hi[:, :], bank(7))
                act.wait_ge(qr_rotated, h + 1)
                nc.scalar.activation(qr_hi[:, :], qr_f[:, :], ACT.Copy).then_inc(pj_hi, 1)

            def k_part(n):
                pj(n + 2, k_hi[:, 0:T], bank(7))
                pj(n + 3, k_hi[:, T:KEYS], bank(6, C))

            def mrg_hi_copy(h):
                act.wait_ge(mrg_ready, h + 1)
                nc.scalar.activation(ht_hi[:, bass.ds(h, 1), :].rearrange("p o t -> p (o t)"), mrg[:, :],
                                     ACT.Copy).then_inc(pj_hi, 1)

            def head(h, n, head0=False, last=False):
                s = 4 * h
                if not last:
                    wqk_split(h + 1, 4 if head0 else n)
                prob_exp(s, 0, head0)
                prob_exp(s + 1, 1, head0)
                if not head0:
                    mrg_hi_copy(h - 1)
                pj(n + 1, v_hi[:, 0:4, :], bank(7).rearrange("p (k v) -> p k v", v=P))
                pt_hi_copy(s, 0)
                prob_exp(s + 2, 2)
                pj(n + 2, v_hi[:, 4:6, :], bank(6, C).rearrange("p (k v) -> p k v", v=P))
                if not last:
                    wv_split(h + 1)
                pt_hi_copy(s + 1, 1)
                prob_exp(s + 3, 3)
                pt_hi_copy(s + 2, 2)
                if not last:
                    qk_part(h + 1, n + 3)
                    k_part(n + 3)
                pt_hi_copy(s + 3, 3)

            wqk_split(0)
            wv_split(0)
            hi(R_WOUT // 2, 0)
            hi(R_WOUT // 2, 1)
            qk_part(0, 0)
            k_part(0)
            head(0, 3, head0=True)
            with act.Fori(1, H - 1) as h:
                head(h, 7 * h + 3)
            head(H - 1, 7 * (H - 1) + 3, last=True)
            mrg_hi_copy(H - 1)

            for k in range(KC):
                hi(R_WOUT // 2 + 1 + k // 2, k % 2)

            def y_std(tt):
                if tt < TT - 1:
                    act.wait_ge(y_done, tt + 1)
                else:
                    act.wait_ge(ring_used, R_WQ)
                step.link(nc.scalar.activation(junk[:, :], banks2(2 * tt, D), ACT.Square, accum_out=ss[:, tt:tt + 1]))
                nc.scalar.activation(std[:, tt:tt + 1], ss[:, tt:tt + 1], ACT.Sqrt, scale=1.0 / D,
                                     bias=col("eps")).then_inc(ystd_ready, 1)

            def xm_std(tt):
                act.wait_ge(xmid_ready, tt + 1)
                step.link(nc.scalar.activation(junk[:, :], x_sb[:, tt, :], ACT.Square, accum_out=ss2[:, tt:tt + 1]))
                nc.scalar.activation(std2[:, tt:tt + 1], ss2[:, tt:tt + 1], ACT.Sqrt, scale=1.0 / D,
                                     bias=col("eps")).then_inc(xmstd_ready, 1)
            y_std(0)
            for tt in range(1, TT):
                y_std(tt)
                xm_std(tt - 1)
            xm_std(TT - 1)
            for k in range(KC):
                act.wait_ge(hf_turned, k + 1)
                nc.scalar.activation(ht_hi[:, k, :], bank(k % 4), ACT.Identity, scale=a_ffn[:, k:k + 1],
                                     bias=modf[:, KC + k:KC + k + 1]).then_inc(hf_hi_ready, 1)
            act.dma_start(keys_raw[:, :, :], a["keys"]).then_inc(keys_in, 16)
            act.wait_ge(keys_in, 16)
            nc.scalar.activation(keys_hi[:, :, :], keys_raw[:, :, :], ACT.Copy).then_inc(keys_hi_s, 1)

            def route(half, b, first=False):
                m = 2 * half + b
                act.wait_ge(ring_used, R_WQ + m + 1)
                if not first:
                    act.wait_ge(sc_done, m - 1)
                nc.scalar.activation(q_hi[b][:, :], bank(b), ACT.Copy).then_inc(q_hi_s, 1)
                hi(R_WQ // 2 + 1 + half, b)
                act.wait_ge(sc_done, m + 1)
                nc.scalar.activation(s_sb[:, :, bass.ds(m, 1), :].rearrange("p a o n -> p a (o n)"),
                                     bank(2 + b).rearrange("p (a n) -> p a n", a=TT), ACT.Copy).then_inc(sc_copied, 1)
            route(0, 0, True)
            route(0, 1, True)
            with act.Fori(1, PH) as i:
                route(i, 0)
                route(i, 1)

            def expert(half, b, first=False):
                j = 2 * half + b
                act.wait_ge(ring_used, R_U + j + 1)
                if not first:
                    act.wait_ge(gh_stored[b], 16 * half)
                nc.scalar.activation(gh[b][:, :], bank(4 + b), ACT.Gelu).then_inc(gelu_done, 1)
                hi(R_U // 2 + 1 + half, b)
            expert(0, 0, True)
            expert(0, 1, True)
            with act.Fori(1, G_FIRST // 2 - 2) as i:
                expert(i, 0)
                expert(i, 1)
            act.wait_ge(logits_ready, 2 * TT)
            nc.scalar.activation(sel_e[:, :, :], sel_e[:, :, :], ACT.Exp).then_inc(exp_all, 1)
            with act.Fori(G_FIRST // 2 - 2, G_FIRST // 2) as i:
                expert(i, 0)
                expert(i, 1)
            with act.Fori(0, T // G_TOK // 2) as i:
                for b in range(2):
                    expert(G_FIRST // 2 + i, b)
                    act.wait_ge(g_built, 2 * i + b + 1)
                    nc.scalar.activation(g_lo[:, :, :], g_parts()[:, :, 1, :], ACT.Copy).then_inc(g_lo_ready, 1)
            with act.Fori((G_FIRST + T // G_TOK) // 2, JT // 2) as i:
                expert(i, 0)
                expert(i, 1)

            def weigh(half, b, first=False):
                j = 2 * half + b
                act.wait_ge(a_ready, j + 1)
                if not first:
                    act.wait_ge(ring_used, R_V + j - 1)
                nc.scalar.activation(a_hi[b][:, :], a_f[b][:, :], ACT.Copy).then_inc(a_hi_s, 1)
            weigh(0, 0, True)
            weigh(0, 1, True)
            with act.Fori(1, JT // 2) as i:
                for b in range(2):
                    hi(R_V // 2 + i, b)
                    weigh(i, b)
            for tt in range(TT):
                if tt < TT - 1:
                    act.wait_ge(o_done, tt + 1)
                else:
                    act.wait_ge(ring_used, R_END)
                step.link(nc.scalar.activation(junk[:, :], banks2(2 * tt, D), ACT.Square, accum_out=ss[:, tt:tt + 1]))
                nc.scalar.activation(std[:, tt:tt + 1], ss[:, tt:tt + 1], ACT.Sqrt, scale=1.0 / D,
                                     bias=col("eps")).then_inc(ostd_ready, 1)

        @block.vector
        def _(dve):
            step = Steps(dve, dve_step)
            v = nc.vector

            dve.wait_ge(xstd_ready, 1)
            step.link(v.reciprocal(rs[:, 0:6], std[:, 0:6]))
            for n in range(TT + CT):
                src = x_sb[:, n, :] if n < TT else ctx_sb[:, n - TT, :]
                v.tensor_scalar(xn[:, n, :], src, rs[:, n:n + 1], None, ALU.mult).then_inc(xn_ready, 1)
            dve.wait_ge(mod_copied, ADA_PE)
            bada = cols[:, COL_AT["b_ada"]:COL_AT["b_ada"] + 48]
            step.link(v.tensor_tensor(modc[:, :, :], modraw[:, :, :],
                                      bada[:, 0:2 * KC].unsqueeze(2).to_broadcast([P, 2 * KC, 2]), ALU.add))
            for s in range(2):
                g = cols[:, COL_AT["g_mix_pre"]:COL_AT["g_mix_pre"] + KC]
                v.scalar_tensor_tensor(out=a_mix[:, :, s], in0=modc[:, KC:2 * KC, s], scalar=1.0, in1=g,
                                       op0=ALU.add, op1=ALU.mult).then_inc(amix_ready, 1)
            def turned_lo(k, dst, src, n, scale, shift, tmp, hi_view):
                step.link(v.tensor_scalar(tmp[:, 0:n], src, scale, shift, ALU.mult, ALU.add))
                return v.tensor_tensor(dst, tmp[:, 0:n], hi_view.bitcast(F32), ALU.subtract)
            dve.wait_ge(amix_ready, 2)
            for k in range(KC):
                for s, (n, hi_t, lo_t) in enumerate(((T, ht_hi, ht_lo), (C, hc_hi, hc_lo))):
                    dve.wait_ge(ht_hi_ready, 2 * k + s + 1)
                    turned_lo(k, lo_t[:, k, :], bank(4 + 2 * (k % 2) + s, n), n, a_mix[:, k, s:s + 1],
                              modc[:, k, s:s + 1], htmp[s], hi_t[:, k, :]).then_inc(ht_lo_ready, 1)
            dve.wait_ge(ring_used, 2)
            v.tensor_tensor(krt[:, 0:T], bank(2), rot[:, 0:T], ALU.mult)
            v.tensor_tensor(krt[:, T:KEYS], bank(3, C), rot[:, T:KEYS], ALU.mult).then_inc(krt_ready, 1)
            dve.wait_ge(kvq_copied, 3)
            v.tensor_tensor(sq[:, 0:KEYS], ckv[:, :], ckv[:, :], ALU.mult)
            v.tensor_tensor(sq[:, KEYS:KEYS + 2 * T], cq.rearrange("p a t -> p (a t)"), cq.rearrange("p a t -> p (a t)"),
                            ALU.mult).then_inc(sq_ready, 1)
            dve.wait_ge(nstd_ready, 1)
            step.link(v.reciprocal(nstd[:, :], nstd[:, :]))
            v.scalar_tensor_tensor(out=ckv[:, :], in0=ckv[:, :], scalar=col("g_kv"), in1=nstd[:, 0:KEYS],
                                   op0=ALU.mult, op1=ALU.mult).then_inc(normed, 1)
            for k in range(2):
                v.scalar_tensor_tensor(out=cq[:, k, :], in0=cq[:, k, :], scalar=col("g_q", k),
                                       in1=nstd[:, KEYS:KEYS + T], op0=ALU.mult, op1=ALU.mult).then_inc(normed, 1)
            dve.wait_ge(split_hi, 2)
            v.tensor_tensor(kr_lo[:, 0:T], bank(5), kr_hi[:, 0:T].bitcast(F32), ALU.subtract)
            v.tensor_tensor(kr_lo[:, T:KEYS], bank(1, C), kr_hi[:, T:KEYS].bitcast(F32), ALU.subtract).then_inc(split_lo, 1)

            def mod_rows(half, b):
                dve.wait_ge(ada_in[b], 16 * half + 32)
                for n in range(2):
                    m = 2 * (2 * half + b) + n
                    v.scalar_tensor_tensor(out=ada_row[b][:, n, :], in0=ada_row[b][:, n, :], scalar=1.0,
                                           in1=silu_row[:, :], op0=ALU.mult, op1=ALU.mult,
                                           accum_out=modf_raw[:, bass.ds(m, 1)]).then_inc(modf_done, 1)
            ada_row = [t.rearrange("p k n -> p (k n)").rearrange("p (a d) -> p a d", d=D) for t in ada]

            for g, w in enumerate(WINDOWS):
                gs = slice(2 * g, 2 * g + 2)
                dve.wait_ge(tile_copied, 2 * g + 2)
                if g:
                    dve.wait_ge(pooled_ready, g)
                xg = poolx[:, gs, :]
                lo_i, hi_i = 1, T + 2 * PAD
                step.link(v.tensor_tensor(poolw[0][:, :, 1:hi_i], xg[:, :, 0:hi_i - 1], xg[:, :, 1:hi_i], ALU.add))
                cur, sh = 0, 1
                while 2 * sh < w:
                    nl, nh = lo_i + sh, hi_i - sh
                    step.link(v.tensor_tensor(poolw[1 - cur][:, :, nl:nh], poolw[cur][:, :, nl - sh:nh - sh],
                                              poolw[cur][:, :, nl + sh:nh + sh], ALU.add))
                    lo_i, hi_i, cur, sh = nl, nh, 1 - cur, 2 * sh
                assert lo_i <= PAD and hi_i >= PAD + T
                W = poolw[cur]
                for e0, at in ((0, PAD), (PAD, T)):
                    ee = edge[:, g, e0:e0 + PAD].unsqueeze(1).to_broadcast([P, 2, PAD])
                    step.add(v.tensor_tensor(W[:, :, at:at + PAD], W[:, :, at:at + PAD], ee, ALU.mult))
                step.sync()
                v.scalar_tensor_tensor(out=poolx[:, gs, PAD:PAD + T], in0=W[:, :, PAD:PAD + T], scalar=1.0 / w,
                                       in1=poolx[:, gs, PAD:PAD + T], op0=ALU.mult, op1=ALU.subtract).then_inc(pooled_ready, 1)
            dve.wait_ge(silu_ready, 2)
            with dve.Fori(0, ADA_DVE // 2) as i:
                mod_rows(i, 0)
                mod_rows(i, 1)
            dve.wait_ge(split_hi, 3)
            v.tensor_tensor(kvn_lo[:, :], ckv[:, :], kvn_hi[:, :].bitcast(F32), ALU.subtract).then_inc(split_lo, 1)
            dve.wait_ge(split_hi, 4)
            v.tensor_tensor(cqn_lo[:, :, :], cq[:, :, :], cqn_hi[:, :, :].bitcast(F32), ALU.subtract).then_inc(split_lo, 1)
            for g in range(4):
                dve.wait_ge(pooled_hi, g + 1)
                v.tensor_tensor(ht_lo[:, 2 * g:2 * g + 2, :], poolx[:, 2 * g:2 * g + 2, PAD:PAD + T],
                                ht_hi[:, 2 * g:2 * g + 2, :].bitcast(F32), ALU.subtract).then_inc(pooled_lo, 1)
            dve.wait_ge(modf_done, 2 * ADA_DVE)
            step.link(v.tensor_tensor(modf[:, :], modf_raw[:, :], bada[:, 2 * KC:6 * KC], ALU.add))
            g = cols[:, COL_AT["g_ffn_pre"]:COL_AT["g_ffn_pre"] + KC]
            step.add(v.scalar_tensor_tensor(out=a_ffn[:, :], in0=modf[:, 2 * KC:3 * KC], scalar=1.0, in1=g,
                                            op0=ALU.add, op1=ALU.mult))
            for n, (m0, name) in enumerate(((0, "g_mix_post"), (3 * KC, "g_ffn_post"))):
                g = cols[:, COL_AT[name]:COL_AT[name] + KC]
                step.add(v.tensor_tensor(gcol[:, n, :], modf[:, m0:m0 + KC], g, ALU.mult))
            step.sync()
            for n in range(2):
                for k in range(KC):
                    v.tensor_scalar(diag[:, n, k * P:(k + 1) * P], ident[:, :], gcol[:, n, k:k + 1], None,
                                    ALU.mult).then_inc(diag_ready, 1)
            for m in range(KC):
                dve.wait_ge(ring_used, R_WPOOL + m // 4 + 1)
                v.scalar_tensor_tensor(out=gates[:, KC + m, :], in0=bank(m), scalar=col("pool_scale", m),
                                       in1=gates[:, KC + m, :], op0=ALU.mult, op1=ALU.mult).then_inc(pmix_used, 1)

            def pj_lo(n, dst, src, hi_view):
                dve.wait_ge(pj_hi, n + 1)
                v.tensor_tensor(dst, src, hi_view.bitcast(F32), ALU.subtract).then_inc(pj_free, 1)

            rot_q = rot[:, 0:T]

            def row_max(s, qt, cnt):
                dve.wait_ge(s_done, s + 1)
                cnt.link(v.tensor_reduce(rowmax[:, qt:qt + 1], banks2(2 * (qt % 2), KEYS), AX.X, ALU.max))
                v.tensor_scalar(nmax[:, qt:qt + 1], rowmax[:, qt:qt + 1], -SCALE, None, ALU.mult).then_inc(max_ready, 1)

            def norm_rows(s, qt, cnt):
                dve.wait_ge(exp_ready, s + 1)
                cnt.link(v.reciprocal(rinv[:, qt:qt + 1], rsum[:, qt:qt + 1]))
                v.tensor_scalar(prob[qt % 2][:, :], prob[qt % 2][:, :], rinv[:, qt:qt + 1], None,
                                ALU.mult).then_inc(prob_ready, 1)

            def pt_lo_part(s, qt):
                dve.wait_ge(pt_hi_s, s + 1)
                q = slice(qt * P, (qt + 1) * P)
                v.tensor_tensor(pt_lo[:, :, q], banks2(4, KEYS).rearrange("p (k q) -> p k q", q=P),
                                pt_hi[:, :, q].bitcast(F32), ALU.subtract).then_inc(pt_lo_s, 1)

            def merge(h, n, cnt):
                dve.wait_ge(pj_done, n + 1)
                cnt.link(v.tensor_tensor(mrg[:, :], bank(6), gates[:, bass.ds(h, 1), :].rearrange("p o t -> p (o t)"), ALU.mult))
                v.tensor_tensor(mrg[:, :], mrg[:, :], gates[:, bass.ds(KC + h, 1), :].rearrange("p o t -> p (o t)"),
                                ALU.add).then_inc(mrg_ready, 1)
                dve.wait_ge(pj_hi, n + 1)
                v.tensor_tensor(ht_lo[:, bass.ds(h, 1), :].rearrange("p o t -> p (o t)"), mrg[:, :],
                                ht_hi[:, bass.ds(h, 1), :].rearrange("p o t -> p (o t)").bitcast(F32),
                                ALU.subtract).then_inc(pj_free, 1)

            def qk(h, n):
                dve.wait_ge(pj_done, n + 2)
                v.tensor_tensor(qr_f[:, :], bank(6), rot_q, ALU.mult).then_inc(qr_rotated, 1)
                pj_lo(n, qn_lo[:, :], bank(7), qn_hi[:, :])
                pj_lo(n + 1, qr_lo[:, :], qr_f[:, :], qr_hi[:, :])

            def head(h, n, cnt, head0=False, last=False):
                s = 4 * h
                row_max(s, 0, cnt)
                row_max(s + 1, 1, cnt)
                norm_rows(s, 0, cnt)
                norm_rows(s + 1, 1, cnt)
                if not head0:
                    merge(h - 1, n, cnt)
                pj_lo(n + 1, v_lo[:, 0:4, :], bank(7).rearrange("p (k v) -> p k v", v=P), v_hi[:, 0:4, :])
                pt_lo_part(s, 0)
                row_max(s + 2, 2, cnt)
                pj_lo(n + 2, v_lo[:, 4:6, :], bank(6, C).rearrange("p (k v) -> p k v", v=P), v_hi[:, 4:6, :])
                pt_lo_part(s + 1, 1)
                norm_rows(s + 2, 2, cnt)
                row_max(s + 3, 3, cnt)
                pt_lo_part(s + 2, 2)
                norm_rows(s + 3, 3, cnt)
                if not last:
                    qk(h + 1, n + 3)
                    pj_lo(n + 5, k_lo[:, 0:T], bank(7), k_hi[:, 0:T])
                    pj_lo(n + 6, k_lo[:, T:KEYS], bank(6, C), k_hi[:, T:KEYS])
                pt_lo_part(s + 3, 3)

            qk(0, 0)
            pj_lo(2, k_lo[:, 0:T], bank(7), k_hi[:, 0:T])
            pj_lo(3, k_lo[:, T:KEYS], bank(6, C), k_hi[:, T:KEYS])
            head(0, 3, step, head0=True)
            PER_HEAD = 9
            n0 = step.n
            with dve.Fori(1, H - 1) as h:
                cnt = Steps(dve, dve_step)
                cnt.n = h * PER_HEAD + (n0 - PER_HEAD)
                head(h, 7 * h + 3, cnt)
            step.n = n0 + (H - 2) * PER_HEAD
            head(H - 1, 7 * (H - 1) + 3, step, last=True)
            merge(H - 1, 7 * H + 3 - 4, step)

            def mid(tt):
                dve.wait_ge(ystd_ready, tt + 1)
                step.link(v.reciprocal(rs[:, tt:tt + 1], std[:, tt:tt + 1]))
                step.link(v.scalar_tensor_tensor(out=ytmp[tt % 2][:, :], in0=banks2(2 * tt, D), scalar=rs[:, tt:tt + 1],
                                                 in1=g_row[:, 0, :], op0=ALU.mult, op1=ALU.mult))
                v.tensor_tensor(x_sb[:, tt, :], x_sb[:, tt, :], ytmp[tt % 2][:, :], ALU.add).then_inc(xmid_ready, 1)

            def mid_norm(tt):
                dve.wait_ge(xmstd_ready, tt + 1)
                step.link(v.reciprocal(rs2[:, tt:tt + 1], std2[:, tt:tt + 1]))
                v.tensor_scalar(xm_n[:, tt, :], x_sb[:, tt, :], rs2[:, tt:tt + 1], None, ALU.mult).then_inc(xmn_ready, 1)
            dve.wait_ge(rows_ready, 2)
            mid(0)
            for tt in range(1, TT):
                mid(tt)
                mid_norm(tt - 1)
            mid_norm(TT - 1)
            for k in range(KC):
                dve.wait_ge(hf_hi_ready, k + 1)
                turned_lo(k, ht_lo[:, k, :], bank(k % 4), T, a_ffn[:, k:k + 1], modf[:, KC + k:KC + k + 1],
                          ftmp[k % 2], ht_hi[:, k, :]).then_inc(hf_lo_ready, 1)
            dve.wait_ge(keys_hi_s, 1)
            v.tensor_tensor(keys_lo[:, :, :], keys_raw[:, :, :], keys_hi[:, :, :].bitcast(F32), ALU.subtract).then_inc(keys_lo_s, 1)

            def q_part(m, b):
                dve.wait_ge(q_hi_s, m + 1)
                v.tensor_tensor(q_lo[b][:, :], bank(b), q_hi[b][:, :].bitcast(F32), ALU.subtract).then_inc(q_lo_s, 1)
            with dve.Fori(0, PH) as i:
                q_part(2 * i, 0)
                q_part(2 * i + 1, 1)

            dve.wait_ge(sc_copied, 2 * PH)
            n0 = step.n

            def route_tile(tt, cnt):
                def sync():
                    cnt.sync()
                    v.memset(spacer[:, :], 0.0)
                cnt.add(v.tensor_copy(s_cur[:, :, :], s_sb[:, bass.ds(tt, 1), :, :].rearrange("p o h n -> p (o h) n")))
                sync()
                for h in range(2 * PH):
                    cnt.add(v.max(top[:, h, 0:8], s_cur[:, h, :]))
                sync()
                for h in range(2 * PH):
                    cnt.add(v.max_index(top_i[:, h, 0:8], top[:, h, 0:8], s_cur[:, h, :]))
                    cnt.add(v.match_replace(s_work[:, h, :], top[:, h, 0:8], s_cur[:, h, :], -3.0e38))
                sync()
                for h in range(2 * PH):
                    cnt.add(v.max(top[:, h, 8:16], s_work[:, h, :]))
                sync()
                for h in range(2 * PH):
                    cnt.add(v.max_index(top_i[:, h, 8:16], top[:, h, 8:16], s_work[:, h, :]))
                sync()
                tv = top.rearrange("p (h two) k -> p h two k", two=2)
                for h in range(PH):
                    cnt.add(v.tensor_tensor(cand[:, h, :].rearrange("p (x y) -> p x y", y=TOPK),
                                            tv[:, h, 0, :].unsqueeze(2).to_broadcast([P, TOPK, TOPK]),
                                            tv[:, h, 1, :].unsqueeze(1).to_broadcast([P, TOPK, TOPK]), ALU.add))
                sync()
                for h in range(PH):
                    cnt.add(v.max(best[:, h, 0:8], cand[:, h, :]))
                sync()
                for h in range(PH):
                    cnt.add(v.max_index(pos[:, h, 0:8], best[:, h, 0:8], cand[:, h, :]))
                    cnt.add(v.match_replace(cand_work[:, h, :], best[:, h, 0:8], cand[:, h, :], -3.0e38))
                sync()
                for h in range(PH):
                    cnt.add(v.max(best[:, h, 8:16], cand_work[:, h, :]))
                sync()
                for h in range(PH):
                    cnt.add(v.max_index(pos[:, h, 8:16], best[:, h, 8:16], cand_work[:, h, :]))
                cnt.add(v.tensor_tensor(sel_e[:, bass.ds(tt * PH, PH), :], best[:, :, :],
                                        best[:, :, 0:1].to_broadcast([P, PH, TOPK]), ALU.subtract))
                sync()
                pf = pos.rearrange("p h k -> p (h k)")
                cnt.add(v.tensor_scalar(pos_a[:, :], pf, 4, None, ALU.logical_shift_right))
                cnt.add(v.tensor_scalar(pos_b[:, :], pf, 15, None, ALU.bitwise_and))
                sync()
                iv = top_i.rearrange("p (h two) k -> p h two k", two=2)
                for half, (pp, dst) in enumerate(((pos_a, sel_i), (pos_b, sel_j))):
                    cnt.link(v.tensor_tensor(eq[:, :, :], pp[:, :].unsqueeze(2).to_broadcast([P, PH * TOPK, TOPK]),
                                             iota[:, 0:TOPK].unsqueeze(1).to_broadcast([P, PH * TOPK, TOPK]), ALU.is_equal))
                    cnt.link(v.tensor_tensor(eq2.rearrange("p (h k) r -> p h k r", h=PH),
                                             eq.rearrange("p (h k) r -> p h k r", h=PH),
                                             iv[:, :, half, :].unsqueeze(2).to_broadcast([P, PH, TOPK, TOPK]), ALU.mult))
                    v.tensor_reduce(dst[:, bass.ds(tt, 1), :].rearrange("p o k -> p (o k)"), eq2[:, :, :],
                                    AX.X, ALU.add).then_inc(logits_ready, 1)
            ROUTE_STEPS = 1 + 2 * PH * 5 + PH * 6 + 1 + 2 + 4
            with dve.Fori(0, TT) as tt:
                cnt = Steps(dve, dve_step)
                cnt.n = tt * ROUTE_STEPS + n0
                route_tile(tt, cnt)
            step.n = n0 + TT * ROUTE_STEPS
            dve.wait_ge(exp_all, 1)
            step.link(v.tensor_reduce(sel_s[:, :], sel_e[:, :, :], AX.X, ALU.add))
            step.link(v.reciprocal(sel_r[:, :], sel_s[:, :]))
            v.tensor_tensor(sel_e[:, :, :], sel_e[:, :, :], sel_r[:, :].unsqueeze(2).to_broadcast([P, TT * PH, TOPK]),
                            ALU.mult).then_inc(sel_ready, 1)
            dve.wait_ge(sel_turned, 1)
            step.add(v.tensor_copy(kt_i[:, :], bank(0)))
            step.add(v.tensor_copy(kt_j[:, :], bank(1)))
            step.add(v.tensor_copy(kt_g[:, :], bank(2)))
            step.sync()
            step.link(v.tensor_copy(kt_ghi[:, :], kt_g[:, :]))
            v.tensor_tensor(kt_glo[:, :], kt_g[:, :], kt_ghi[:, :].bitcast(F32), ALU.subtract).then_inc(kt_ready, 1)
            dve.wait_ge(kt_ready, 1)

            def onehots(u, b, first=False):
                def per_token(t):
                    return t[:, bass.ds(G_TOK * u, G_TOK)].unsqueeze(2).to_broadcast([P, G_TOK, NK])
                keys = iota[:, :].unsqueeze(1).to_broadcast([P, G_TOK, NK])
                if not first:
                    dve.wait_ge(oh_lo_ready, u - 1)
                v.tensor_tensor(eq_j[b][:, :, :], keys, per_token(kt_j), ALU.is_equal).then_inc(eqj_ready, 1)
                v.tensor_tensor(oh_i[b][:, :, :], keys, per_token(kt_i), ALU.is_equal)
                dve.wait_ge(eqj_ready, u + 1)
                v.tensor_tensor(oh_j[b][:, :, 0, :], eq_j[b][:, :, :], per_token(kt_ghi[:, :].bitcast(F32)),
                                ALU.mult).then_inc(oh_ready, 1)

            def g_sum(u, at, bb, stored):
                if stored is not None:
                    dve.wait_ge(g_stored[bb], stored)
                dve.wait_ge(g_lo_ready, u + 1)
                v.tensor_tensor(g_blk[bb][:, :, bass.ds(at, G_TOK)].rearrange("p n t -> p t n"),
                                g_parts()[:, :, 0, :], g_lo[:, :, :], ALU.add).then_inc(g_copied, 1)
            onehots(0, 0, True)
            onehots(1, 1, True)

            def g_block(q, bb, first=False, last=False):
                def pair(i, ahead=True):
                    for b in range(2):
                        u = (2 * q + bb) * G_STEPS + 2 * i + b
                        if ahead:
                            dve.wait_ge(g_built, u + 1)
                            onehots(u + 2, b)
                        g_sum(u, 2 * G_TOK * i + G_TOK * b, bb, None if first else 16 * G_STEPS * q)
                with dve.Fori(0, G_STEPS // 2 - 1) as i:
                    pair(i)
                pair(G_STEPS // 2 - 1, ahead=not last)
            g_block(0, 0, True)
            g_block(0, 1, True)
            with dve.Fori(1, T // G_BLK // 2 - 1) as q:
                g_block(q, 0)
                g_block(q, 1)
            g_block(T // G_BLK // 2 - 1, 0)
            g_block(T // G_BLK // 2 - 1, 1, last=True)

            def weigh(j, half, b, q, first=False):
                if b == 0:
                    dve.wait_ge(pair_in[q], 32 * half + 32)
                v.tensor_tensor(a_f[b].rearrange("p (k t) -> p k t", t=G_BLK),
                                gh_in[q][:, b, :].rearrange("p (k t) -> p k t", t=G_BLK),
                                g_in[q][:, :, b, :], ALU.mult).then_inc(a_ready, 1)
                dve.wait_ge(a_hi_s, j + 1)
                if not first:
                    dve.wait_ge(ring_used, R_V + j - 1)
                v.tensor_tensor(a_lo[b][:, :], a_f[b][:, :], a_hi[b][:, :].bitcast(F32), ALU.subtract).then_inc(a_lo_s, 1)
            for n in range(4):
                weigh(n, 0, n % 2, n // 2, n < 2)
            with dve.Fori(1, JT // 4) as i:
                for n in range(4):
                    weigh(4 * i + n, i, n % 2, n // 2)
            for tt in range(TT):
                dve.wait_ge(ostd_ready, tt + 1)
                step.link(v.reciprocal(rs[:, tt:tt + 1], std[:, tt:tt + 1]))
                step.link(v.scalar_tensor_tensor(out=ytmp[tt % 2][:, :], in0=banks2(2 * tt, D), scalar=rs[:, tt:tt + 1],
                                                 in1=g_row[:, 1, :], op0=ALU.mult, op1=ALU.mult))
                v.tensor_tensor(x_sb[:, tt, :], x_sb[:, tt, :], ytmp[tt % 2][:, :], ALU.add).then_inc(out_ready, 1)

        @block.tensor
        def _(pe):
            mm = nc.tensor.matmul

            def mod(c):
                pe.wait_ge(ada_in[c], 16)
                if c >= 2:
                    pe.wait_ge(mod_copied, c - 1)
                for m in range(ADA_W // P):
                    for k in range(KC):
                        ins = mm(ps[:, 2 + c % 2, 2 * m:2 * m + 2], ada_pe[c][:, k, m * P:(m + 1) * P], silu[:, k, :],
                                 start=(k == 0), stop=(k == KC - 1))
                ins.then_inc(mod_done, 1)

            def ring_wait(t):
                pe.wait_ge(ring_hi, t + 1)
                pe.wait_ge(ring_lo, t + 1)

            def project(b, dst, hi_t, lo_t, n):
                q = 0
                for k in range(KC):
                    ks = slice(k * P, (k + 1) * P)
                    for w, m in ((w_hi[b], hi_t), (w_hi[b], lo_t), (w_lo[b], hi_t)):
                        ins = mm(dst, w[:, ks], m[:, k, :], start=(q == 0), stop=(q == 3 * KC - 1))
                        q += 1
                return ins

            pe.wait_ge(silu_ready, 1)
            for c in range(ADA_PE):
                mod(c)
            pe.wait_ge(const_in, 96)
            pe.wait_ge(xn_ready, TT + CT)
            for k in range(KC):
                for s, (t0, tn) in enumerate(((0, TT), (TT, CT))):
                    if k >= 2:
                        pe.wait_ge(ht_lo_ready, 2 * (k - 2) + s + 1)
                    for n in range(tn):
                        ins = nc.tensor.transpose(ps[:, 4 + 2 * (k % 2) + s, n * P:(n + 1) * P],
                                                  xn[:, t0 + n, k * P:(k + 1) * P], ident[:, :])
                    ins.then_inc(ht_turned, 1)
            pe.wait_ge(ht_lo_ready, 2 * KC)
            for t in range(4):
                ring_wait(t)
                if t < 2:
                    project(t, bank(2 * t), ht_hi, ht_lo, T)
                    ins = project(t, bank(2 * t + 1, C), hc_hi, hc_lo, C)
                else:
                    ins = project(t % 2, bank(2 + t), ht_hi, ht_lo, T)
                ins.then_inc(ring_used, 1)
            pe.wait_ge(kvq_copied, 3)
            pe.wait_ge(krt_ready, 1)

            def plain_tile(t, n, b, first=False):
                ring_wait(t)
                if not first:
                    pe.wait_ge(tile_copied, n - 1)
                project(b, bank(b), ht_hi, ht_lo, T).then_inc(ring_used, 1)
            plain_tile(R_POOLX, 0, 0, True)
            plain_tile(R_POOLX + 1, 1, 1, True)
            with pe.Fori(1, 4) as i:
                for b in range(2):
                    plain_tile(R_POOLX + 2 * i + b, 2 * i + b, b)
            pe.wait_ge(ones_ready, 1)
            pe.wait_ge(sq_ready, 1)
            mm(bank(6), ones[:, :], sq[:, 0:T], start=True, stop=True)
            mm(bank(7, C), ones[:, :], sq[:, T:KEYS], start=True, stop=True)
            mm(bank(4), ones[:, :], sq[:, KEYS:KEYS + T], start=True, stop=False)
            mm(bank(4), ones[:, :], sq[:, KEYS + T:KEYS + 2 * T], start=False, stop=True).then_inc(sums_done, 1)
            pe.wait_ge(tile_copied, 8)
            mm(bank(5), fold[:, :], krt[:, 0:T], start=True, stop=True)
            mm(bank(1, C), fold[:, :], krt[:, T:KEYS], start=True, stop=True).then_inc(sums_done, 1)
            pe.wait_ge(nstd_ready, 1)
            pe.wait_ge(split_lo, 1)
            with pe.Fori(0, 8) as i:
                for b in range(2):
                    plain_tile(R_GATES + 2 * i + b, 8 + 2 * i + b, b)
            pe.wait_ge(pooled_lo, 4)
            pe.wait_ge(tile_copied, 24)
            for m in range(KC):
                g, half = m // 2, m % 2
                t = R_WPOOL + g // 2
                b = t % 2
                if m % 4 == 0:
                    ring_wait(t)
                q = 0
                for k in range(2):
                    at = (g % 2) * 512 + k * 256 + half * P
                    for w, x in ((w_hi[b], ht_hi), (w_hi[b], ht_lo), (w_lo[b], ht_hi)):
                        ins = mm(bank(m), w[:, at:at + P], x[:, 2 * g + k, :], start=(q == 0), stop=(q == 5))
                        q += 1
                if m % 4 == 3:
                    ins.then_inc(ring_used, 1)
            for n in range(2):
                pe.wait_ge(diag_ready, (n + 1) * KC)
                pe.wait_ge(pmix_used, KC)
                for q in range(2):
                    ins = mm(bank(2 * n + q), ones[:, :], diag[:, n, q * 512:(q + 1) * 512], start=True, stop=True)
                ins.then_inc(rows_done, 1)
            pe.wait_ge(rows_ready, 2)

            def three(dst, parts):
                last = 3 * len(parts) - 1
                q = 0
                for sh, sl, mh, ml in parts:
                    for w, m in ((sh, mh), (sh, ml), (sl, mh)):
                        ins = mm(dst, w, m, start=(q == 0), stop=(q == last))
                        q += 1
                return ins

            def scores(s, qt, first=False):
                if not first:
                    pe.wait_ge(exp_ready, s - 1)
                qs = slice(qt * P, (qt + 1) * P)
                for dst, ks in ((bank(2 * (qt % 2)), slice(0, T)), (bank(2 * (qt % 2) + 1, C), slice(T, KEYS))):
                    ins = three(dst, [(qn_hi[:, qs], qn_lo[:, qs], k_hi[:, ks], k_lo[:, ks]),
                                      (qr_hi[:, qs], qr_lo[:, qs], kr_hi[:, ks], kr_lo[:, ks])])
                ins.then_inc(s_done, 1)

            def turn(s, qt, first=False):
                pe.wait_ge(prob_ready, s + 1)
                if not first:
                    pe.wait_ge(pt_lo_s, s)
                for k in range(KT):
                    ins = nc.tensor.transpose(banks2(4, KEYS)[:, k * P:(k + 1) * P],
                                              prob[qt % 2][:, k * P:(k + 1) * P], ident[:, :])
                ins.then_inc(pt_turned, 1)

            def value_product(n, pts):
                pe.wait_ge(pt_lo_s, pts)
                pe.wait_ge(pj_free, n)
                three(bank(6), [(v_hi[:, k, :], v_lo[:, k, :], pt_hi[:, k, :], pt_lo[:, k, :])
                                for k in range(KT)]).then_inc(pj_done, 1)

            def values(h, n, k0, kn, bk, freed):
                pe.wait_ge(wv_lo_s, h + 1)
                pe.wait_ge(pj_free, freed)
                for k in range(k0, k0 + kn):
                    ks = slice(k * P, (k + 1) * P)
                    ins = three(ps[:, bk, (k - k0) * P:(k - k0 + 1) * P],
                                [(kvn_hi[:, ks], kvn_lo[:, ks], wv_hi[:, :], wv_lo[:, :])])
                ins.then_inc(pj_done, 1)

            def queries_keys(h, n, freed=None):
                pe.wait_ge(wqk_lo_s, h + 1)
                if freed is not None:
                    pe.wait_ge(pj_free, n - 1)
                for q, (bk, at) in enumerate(((7, 0), (6, P))):
                    if q == 1 and freed is not None:
                        pe.wait_ge(pj_free, n)
                    three(bank(bk), [(wqk_hi[:, 2 * P * k + at:2 * P * k + at + P], wqk_lo[:, 2 * P * k + at:2 * P * k + at + P],
                                      cqn_hi[:, k, :], cqn_lo[:, k, :]) for k in range(2)]).then_inc(pj_done, 1)
                pe.wait_ge(pj_free, n + 1)
                wk = slice(4 * P, 5 * P)
                three(bank(7), [(wqk_hi[:, wk], wqk_lo[:, wk], kvn_hi[:, 0:T], kvn_lo[:, 0:T])]).then_inc(pj_done, 1)
                pe.wait_ge(pj_free, n + 2)
                three(bank(6, C), [(wqk_hi[:, wk], wqk_lo[:, wk], kvn_hi[:, T:KEYS], kvn_lo[:, T:KEYS])]).then_inc(pj_done, 1)

            def head(h, n, head0=False, last=False):
                s = 4 * h
                pe.wait_ge(pj_free, 4 if head0 else n)
                scores(s, 0, head0)
                scores(s + 1, 1, head0)
                if not head0:
                    value_product(n, s)
                values(h, n + 1, 0, 4, 7, 4 if head0 else n)
                turn(s, 0, head0)
                scores(s + 2, 2)
                values(h, n + 2, 4, 2, 6, 4 if head0 else n + 1)
                turn(s + 1, 1)
                scores(s + 3, 3)
                turn(s + 2, 2)
                if not last:
                    queries_keys(h + 1, n + 3, True)
                turn(s + 3, 3)

            pe.wait_ge(split_lo, 3)
            queries_keys(0, 0)
            head(0, 3, head0=True)
            with pe.Fori(1, H - 1) as h:
                head(h, 7 * h + 3)
            head(H - 1, 7 * (H - 1) + 3, last=True)
            pe.wait_ge(pt_lo_s, 4 * H)
            three(bank(6), [(v_hi[:, k, :], v_lo[:, k, :], pt_hi[:, k, :], pt_lo[:, k, :])
                            for k in range(KT)]).then_inc(pj_done, 1)

            def rows(b, sh, sl, start, stop, done=None):
                for tt in range(TT):
                    ts = slice(tt * P, (tt + 1) * P)
                    for q, (s_, w_) in enumerate(((sh, w_hi[b]), (sh, w_lo[b]), (sl, w_hi[b]))):
                        for dh in range(2):
                            ins = mm(bank(2 * tt + dh), s_[:, ts], w_[:, dh * 512:(dh + 1) * 512],
                                     start=start and q == 0, stop=stop and q == 2)
                    if done is not None and tt < TT - 1:
                        ins.then_inc(done, 1)
                ins.then_inc(ring_used, 1)
            pe.wait_ge(pj_free, 7 * H)
            for k in range(KC):
                t = R_WOUT + k
                ring_wait(t)
                last = k == KC - 1
                rows(t % 2, ht_hi[:, k, :], ht_lo[:, k, :], k == 0, last, y_done if last else None)
            pe.wait_ge(xmn_ready, TT)
            for k in range(KC):
                if k >= 4:
                    pe.wait_ge(hf_lo_ready, k - 3)
                for tt in range(TT):
                    ins = nc.tensor.transpose(ps[:, k % 4, tt * P:(tt + 1) * P], xm_n[:, tt, k * P:(k + 1) * P], ident[:, :])
                ins.then_inc(hf_turned, 1)
            pe.wait_ge(hf_lo_ready, KC)
            def q_tile(m, b, first=False):
                ring_wait(R_WQ + m)
                if not first:
                    pe.wait_ge(q_lo_s, m - 1)
                project(b, bank(b), ht_hi, ht_lo, T).then_inc(ring_used, 1)

            def score_tile(m, b, first=False):
                pe.wait_ge(q_lo_s, m + 1)
                if not first:
                    pe.wait_ge(sc_copied, m - 1)
                for tt in range(TT):
                    ts = slice(tt * P, (tt + 1) * P)
                    ins = three(ps[:, 2 + b, tt * P:(tt + 1) * P],
                                [(q_hi[b][:, ts], q_lo[b][:, ts], keys_hi[:, b, :], keys_lo[:, b, :])])
                ins.then_inc(sc_done, 1)
            q_tile(0, 0, True)
            q_tile(1, 1, True)
            pe.wait_ge(keys_lo_s, 1)
            score_tile(0, 0, True)
            q_tile(2, 0)
            score_tile(1, 1, True)
            with pe.Fori(1, PH - 1) as i:
                q_tile(2 * i + 1, 1)
                score_tile(2 * i, 0)
                q_tile(2 * i + 2, 0)
                score_tile(2 * i + 1, 1)
            q_tile(2 * PH - 1, 1)
            score_tile(2 * PH - 2, 0)
            score_tile(2 * PH - 1, 1)

            def expert(j, b, first=False):
                ring_wait(R_U + j)
                if not first:
                    pe.wait_ge(gelu_done, j - 1)
                project(b, bank(4 + b), ht_hi, ht_lo, T).then_inc(ring_used, 1)

            def gate_matrices(u, b, first=False):
                pe.wait_ge(oh_ready, u + 1)
                pe.wait_ge(oh_lo_ready, u + 1)
                if not first:
                    pe.wait_ge(g_copied, u)
                for q in range(G_TOK):
                    ins = mm(ps[:, q // 2, (q % 2) * 2 * NK:(q % 2 + 1) * 2 * NK], oh_i[b][:, q, :],
                             oh_j[b][:, q, :, :].rearrange("p s n -> p (s n)"), start=True, stop=True)
                ins.then_inc(g_built, 1)
            expert(0, 0, True)
            expert(1, 1, True)
            with pe.Fori(1, G_FIRST // 2) as i:
                expert(2 * i, 0)
                expert(2 * i + 1, 1)
            pe.wait_ge(sel_ready, 1)
            for n, src in enumerate((sel_i, sel_j, None)):
                for tt in range(TT):
                    m = src[:, tt, :] if src is not None else \
                        sel_e[:, tt * PH:(tt + 1) * PH, :].rearrange("p h k -> p (h k)")
                    ins = nc.tensor.transpose(ps[:, n, tt * P:(tt + 1) * P], m, ident[:, :])
            ins.then_inc(sel_turned, 1)
            expert(G_FIRST, 0)
            gate_matrices(0, 0, True)
            expert(G_FIRST + 1, 1)
            gate_matrices(1, 1)
            with pe.Fori(1, T // G_TOK // 2) as i:
                for b in range(2):
                    expert(G_FIRST + 2 * i + b, b)
                    gate_matrices(2 * i + b, b)
            with pe.Fori((G_FIRST + T // G_TOK) // 2, JT // 2) as i:
                expert(2 * i, 0)
                expert(2 * i + 1, 1)
            pe.wait_ge(gelu_done, JT)
            pe.wait_ge(g_copied, T // G_TOK)

            def combine(j, b, start=False, stop=False):
                ring_wait(R_V + j)
                pe.wait_ge(a_lo_s, j + 1)
                rows(b, a_hi[b], a_lo[b], start, stop, o_done if stop else None)
            combine(0, 0, start=True)
            combine(1, 1)
            with pe.Fori(1, JT // 2 - 1) as i:
                combine(2 * i, 0)
                combine(2 * i + 1, 1)
            combine(JT - 2, 0)
            combine(JT - 1, 1, stop=True)


def _tables():
    import numpy as np
    f = np.float32
    grid_w, n_freq = 64, 16
    t = np.arange(T)
    inv_freq = (f(10000.0) ** (-np.arange(n_freq, dtype=f) / f(n_freq))).astype(f)
    pos = np.stack([t // grid_w, t % grid_w]).astype(f)
    ang = pos[:, None, :] * inv_freq[None, :, None]
    cos, sin = np.cos(ang).astype(f), np.sin(ang).astype(f)
    rot = np.zeros((P, KEYS), f)
    rot[0:64, 0:T] = np.stack([cos, cos], 1).reshape(64, T)
    rot[64:128, 0:T] = np.stack([-sin, sin], 1).reshape(64, T)
    rot[0:64, T:KEYS] = 1.0
    edge = np.zeros((4, 2 * PAD), f)
    for g, w in enumerate(WINDOWS):
        for n in range(2 * PAD):
            tok = n if n < PAD else T - 2 * PAD + n
            edge[g, n] = w / (min(tok + w // 2, T) - max(tok - w // 2, 0))
    p = np.arange(P)
    return {
        "rot": rot,
        "edge": np.ascontiguousarray(np.broadcast_to(edge, (P, 4, 2 * PAD))),
        "ident": np.eye(P, dtype=f),
        "fold": (p[:, None] % 64 == p[None, :] % 64).astype(f),
        "iota": np.ascontiguousarray(np.broadcast_to(np.arange(P, dtype=f), (P, P))),
    }


def _layout(x, c, ctx, c_ctx, w_ada, b_ada, g_mix_pre, g_mix_post, g_ffn_pre, g_ffn_post, w_in, g_q_lora, w_uq,
            g_kv_lora, w_ukv, w_pool, pool_scale, w_out, peer_wq, peer_keys, peer_u, peer_v):
    import numpy as np

    def tiles(w):
        k, n = w.shape[0] // P, w.shape[1] // P
        return w.reshape(k, P, n, P).transpose(2, 1, 0, 3).reshape(n, P, k * P)

    def vec(a):
        return a.reshape(-1, P).T

    swap = (np.arange(64).reshape(2, 2, 16)[:, ::-1]).reshape(-1)
    win = w_in[0]
    rope = win[:, P:P + 64]
    w_in_t = tiles(np.concatenate([win[:, 0:P], rope, rope[:, swap], win[:, P + 64:]], axis=1))
    uq = w_uq[0].reshape(2, P, H, QDIM)
    uq = np.concatenate([uq[..., 0:P], uq[..., P:], uq[..., P:][..., swap]], axis=-1)
    ukv = w_ukv[0].reshape(P, H, 2 * P)
    wqk = np.concatenate([uq[0], uq[1], ukv[..., 0:P]], axis=-1).transpose(1, 0, 2)
    cols = np.concatenate([vec(b_ada[0]), vec(g_mix_pre[0]), vec(g_mix_post[0]), vec(g_ffn_pre[0]), vec(g_ffn_post[0]),
                           vec(pool_scale[0]), vec(g_q_lora[0]), vec(g_kv_lora[0]),
                           np.full((P, 1), EPS, np.float32)], axis=1)
    out = {
        "x": x[0], "ctx": ctx[0],
        "cond": np.stack([vec(c[0]), vec(c_ctx)], axis=-1),
        "cols": cols,
        "w_ada_c": w_ada[0][:, :2 * D].reshape(KC, P, ADA_PE, ADA_W).transpose(2, 1, 0, 3).reshape(ADA_PE, P, KC * ADA_W),
        "w_ada_r": w_ada[0][:, 2 * D:].T.reshape(ADA_DVE, 2, P, D).transpose(0, 2, 1, 3).reshape(ADA_DVE, P, 2 * D),
        "c_row": np.broadcast_to(c, (P, D)),
        "w_in": w_in_t,
        "w_pool": w_pool[0].reshape(2, 2, 2, P, 2 * P).transpose(0, 3, 1, 2, 4).reshape(2, P, D),
        "w_out": w_out[0].reshape(KC, P, D),
        "wq": tiles(peer_wq[0]),
        "wqk": wqk,
        "wv": ukv[..., P:].transpose(1, 0, 2),
        "keys": peer_keys[0].transpose(2, 0, 1),
        "u": peer_u[0].reshape(NK, JT, KC, P).transpose(1, 3, 2, 0).reshape(JT, P, D),
        "v": peer_v[0].reshape(NK, JT, D).transpose(1, 0, 2),
    }
    out.update(_tables())
    return {k: np.ascontiguousarray(w) for k, w in out.items()}


def kernel(**inputs):
    import numpy as _np
    import concourse.bacc as _bacc
    from concourse import mybir as _mybir
    from concourse.bass_utils import run_bass_kernel_spmd as _run

    nc = _bacc.Bacc("TRN2", target_bir_lowering=False, num_devices=1)
    arrays, aps = {}, {}
    for name, w in _layout(**{k: _np.asarray(v) for k, v in inputs.items()}).items():
        arrays[f"in_{name}"] = w
        aps[name] = nc.dram_tensor(f"in_{name}", w.shape, _mybir.dt.from_np(w.dtype), kind="ExternalInput").ap()
    out = nc.dram_tensor("out_0", (T, D), _mybir.dt.float32, kind="ExternalOutput").ap()
    build(nc, aps, out)
    r = _run(nc, [arrays], core_ids=[0])
    return r.results[0]["out_0"].reshape(1, T, D)
```

```python
import concourse.bass as bass
from concourse import mybir
from contextlib import ExitStack

F32 = mybir.dt.float32
F32R = mybir.dt.float32r
U32 = mybir.dt.uint32
ALU = mybir.AluOpType
ACT = mybir.ActivationFunctionType
AX = mybir.AxisListType

P = 128
D = 1024
KC = D // P
T = 512
TT = T // P
C = 256
CT = C // P
KEYS = T + C
H = 8
KT = KEYS // P
QDIM = 192
SCALE = float(QDIM) ** -0.5
WINDOWS = (2, 4, 8, 16)
PAD = 8
PH = 8
NK = 128
TOPK = 16
EPS = 1e-6
JT = 128
G_TOK = 8
G_BLK = 64
G_FIRST = 44
G_STEPS = G_BLK // G_TOK
G_PIECE = NK // G_STEPS

ADA_W = 256
ADA_PE = 2 * D // ADA_W
ADA_DVE = 4 * D // ADA_W

R_IN = 0
R_KVQ, R_POOLX, R_GATES = 0, 4, 12
R_WPOOL = 28
R_WOUT = R_WPOOL + 2
R_WQ = R_WOUT + KC
R_U = R_WQ + 2 * PH
R_V = R_U + JT
R_END = R_V + JT

COLS = {"b_ada": 48, "g_mix_pre": KC, "g_mix_post": KC, "g_ffn_pre": KC, "g_ffn_post": KC,
        "pool_scale": KC, "g_q": 2, "g_kv": 1, "eps": 1}
COL_AT = {}
_n = 0
for _k, _w in COLS.items():
    COL_AT[_k] = _n
    _n += _w
NCOLS = _n


class Steps:

    def __init__(self, eng, sem):
        self.eng, self.sem, self.n = eng, sem, 0

    def add(self, ins):
        ins.then_inc(self.sem, 1)
        self.n = self.n + 1

    def sync(self):
        self.eng.wait_ge(self.sem, self.n)

    def link(self, ins):
        self.add(ins)
        self.sync()


def build(nc, a, out):
    ctx = ExitStack()
    with ctx:
        arena_bytes = nc.sbuf_bytes_remaining // 64 * 64
        ctx.enter_context(nc.sbuf_tensor("arena", [P, arena_bytes // 4], F32))
        base = nc.sbuf_base - arena_bytes

        class Region:

            def __init__(self, at):
                self.at = at

            def __call__(self, name, shape, dt=F32):
                n = 4
                for s in shape[1:]:
                    n *= s
                n = (n + 31) // 32 * 32
                assert self.at + n <= arena_bytes, (name, self.at + n, arena_bytes)
                t = nc.alloc_sbuf_tensor_at(name, list(shape), dt, offset=base + self.at)
                self.at += n
                return t

        sb = Region(0)
        ident = sb("ident", [P, P])
        ones = sb("ones", [P, P])
        fold = sb("fold", [P, P])
        iota = sb("iota", [P, P])
        cols = sb("cols", [P, NCOLS])
        modf_raw = sb("modf_raw", [P, 4 * KC])
        modc = sb("modc", [P, 2 * KC, 2])
        modf = sb("modf", [P, 4 * KC])
        a_mix = sb("a_mix", [P, KC, 2])
        a_ffn = sb("a_ffn", [P, KC])
        gcol = sb("gcol", [P, 2, KC])
        cond = sb("cond", [P, KC, 2])
        silu = sb("silu", [P, KC, 2])
        edge = sb("edge", [P, 4, 2 * PAD])
        ss = sb("ss", [P, 8])
        std = sb("std", [P, 8])
        rs = sb("rs", [P, 8])
        ss2 = sb("ss2", [P, 8])
        std2 = sb("std2", [P, 8])
        rs2 = sb("rs2", [P, 8])
        spacer = sb("spacer", [P, 1])
        gq_scaled = sb("gq_scaled", [P, 2])
        g_row = sb("g_row", [P, 2, D])
        x_sb = sb("x_sb", [P, TT, D])
        w_raw = [sb(f"w_raw{b}", [P, D]) for b in range(2)]
        w_hi = [sb(f"w_hi{b}", [P, D], F32R) for b in range(2)]
        w_lo = [sb(f"w_lo{b}", [P, D], F32R) for b in range(2)]
        ht_hi = sb("ht_hi", [P, KC, T], F32R)
        ht_lo = sb("ht_lo", [P, KC, T], F32R)
        S = sb.at
        over = Region(S - 2 * 4 * KC * T)
        ada_h = [over(f"ada_h{b}", [P, KC, ADA_W]) for b in range(4)]

        sb = Region(S)
        ada = [sb(f"ada{b}", [P, KC, ADA_W]) for b in range(2)]
        hc_hi = sb("hc_hi", [P, KC, C], F32R)
        hc_lo = sb("hc_lo", [P, KC, C], F32R)
        over = Region(sb.at - 2 * 4 * KC * C)
        ada_c = [over(f"ada_c{b}", [P, KC, ADA_W]) for b in range(2)]
        silu_row = Region(sb.at - 4 * D)("silu_row", [P, D])
        sq = Region(sb.at - 2 * 4 * KC * C)("sq", [P, KEYS + 2 * T])
        nstd = Region(sb.at - 2 * 4 * KC * C + 4 * (KEYS + 2 * T))("nstd", [P, KEYS + T])
        xn_t = Region(sb.at)("xn_t", [P, KC, KEYS])
        poolx = sb("poolx", [P, 2 * 4, T + 2 * PAD])
        diag = Region(sb.at)("diag", [P, 2, D])
        poolw = [sb(f"poolw{b}", [P, 2, T + 2 * PAD]) for b in range(2)]
        mod_row = Region(sb.at)("mod_row", [2, 2 * D])
        over = Region(sb.at)
        htmp = [over(f"htmp{b}", [P, T]) for b in range(2)]
        ctmp = [over(f"ctmp{b}", [P, C]) for b in range(2)]
        ckv = sb("ckv", [P, KEYS])
        cq = sb("cq", [P, 2, T])
        krt = sb("krt", [P, KEYS])
        KV_AT = sb.at
        rot = sb("rot", [P, KEYS])
        kvn_hi = sb("kvn_hi", [P, KEYS], F32R)
        kvn_lo = sb("kvn_lo", [P, KEYS], F32R)
        cqn_hi = sb("cqn_hi", [P, 2, T], F32R)
        cqn_lo = sb("cqn_lo", [P, 2, T], F32R)
        kr_hi = sb("kr_hi", [P, KEYS], F32R)
        kr_lo = sb("kr_lo", [P, KEYS], F32R)
        gates = sb("gates", [P, 2 * KC, T])
        over = Region(sb.at - 4 * 2 * KC * T)
        xn = over("xn", [P, TT + CT, D])
        ctx_sb = over("ctx_sb", [P, CT, D])
        assert over.at <= sb.at
        ada_pe = ada + ada_c + ada_h
        assert len(ada_pe) == ADA_PE

        sb = Region(S)
        wqk_raw = sb("wqk_raw", [P, 5 * P])
        wqk_hi = sb("wqk_hi", [P, 5 * P], F32R)
        wqk_lo = sb("wqk_lo", [P, 5 * P], F32R)
        wv_raw = sb("wv_raw", [P, P])
        wv_hi = sb("wv_hi", [P, P], F32R)
        wv_lo = sb("wv_lo", [P, P], F32R)
        qn_hi = sb("qn_hi", [P, T], F32R)
        qn_lo = sb("qn_lo", [P, T], F32R)
        qr_f = sb("qr_f", [P, T])
        qr_hi = sb("qr_hi", [P, T], F32R)
        qr_lo = sb("qr_lo", [P, T], F32R)
        k_hi = sb("k_hi", [P, KEYS], F32R)
        k_lo = sb("k_lo", [P, KEYS], F32R)
        v_hi = sb("v_hi", [P, KT, P], F32R)
        v_lo = sb("v_lo", [P, KT, P], F32R)
        prob = [sb(f"prob{b}", [P, KEYS]) for b in range(2)]
        mrg = sb("mrg", [P, T])
        nmax = sb("nmax", [P, TT])
        rsum = sb("rsum", [P, TT])
        rinv = sb("rinv", [P, TT])
        pt_hi = sb("pt_hi", [P, KT, T], F32R)
        pt_lo = sb("pt_lo", [P, KT, T], F32R)
        assert sb.at <= KV_AT, (sb.at, KV_AT)

        sb = Region(S)
        s_sb = sb("s_sb", [P, TT, 2 * PH, NK])
        xm_n = sb("xm_n", [P, TT, D])
        ytmp = [sb(f"ytmp{tt}", [P, D]) for tt in range(TT)]
        ftmp = [sb(f"ftmp{b}", [P, T]) for b in range(4)]
        junk = sb("junk", [P, D])
        sb = Region(S + 4 * TT * 2 * PH * NK)
        q_hi = [sb(f"q_hi{b}", [P, T], F32R) for b in range(2)]
        q_lo = [sb(f"q_lo{b}", [P, T], F32R) for b in range(2)]
        keys_raw = sb("keys_raw", [P, 2, NK])
        keys_hi = sb("keys_hi", [P, 2, NK], F32R)
        keys_lo = sb("keys_lo", [P, 2, NK], F32R)
        sb = Region(S + 4 * TT * 2 * PH * NK + 4 * 4 * T + 3 * 4 * 2 * NK)
        RT = sb.at
        s_cur = sb("s_cur", [P, 2 * PH, NK])
        s_work = sb("s_work", [P, 2 * PH, NK])
        ROUTE_END = sb.at
        cand = Region(RT)("cand", [P, PH, TOPK * TOPK])
        cand_work = Region(ROUTE_END - 4 * 2 * PH * NK)("cand_work", [P, PH, TOPK * TOPK])
        eq = sb("eq", [P, PH * TOPK, TOPK])
        eq2 = sb("eq2", [P, PH * TOPK, TOPK])
        top = sb("top", [P, 2 * PH, TOPK])
        top_i = sb("top_i", [P, 2 * PH, TOPK], U32)
        best = sb("best", [P, PH, TOPK])
        pos = sb("pos", [P, PH, TOPK], U32)
        pos_a = sb("pos_a", [P, PH * TOPK], U32)
        pos_b = sb("pos_b", [P, PH * TOPK], U32)
        ROUTE_TMP_END = sb.at
        sel_i = sb("sel_i", [P, TT, PH * TOPK])
        sel_j = sb("sel_j", [P, TT, PH * TOPK])
        sel_e = sb("sel_e", [P, TT * PH, TOPK])
        sel_s = sb("sel_s", [P, TT * PH])
        sel_r = sb("sel_r", [P, TT * PH])
        kt_i = sb("kt_i", [P, T])
        kt_j = sb("kt_j", [P, T])
        kt_ghi = sb("kt_ghi", [P, T], F32R)
        kt_g = sb("kt_g", [P, T])
        kt_glo = sb("kt_glo", [P, T])
        gh = [sb(f"gh{b}", [P, T]) for b in range(2)]
        KEEP_END = sb.at
        sb = Region(S)
        g_blk = [sb(f"g_blk{b}", [P, NK, G_BLK]) for b in range(2)]
        assert sb.at <= ROUTE_TMP_END, (sb.at, ROUTE_TMP_END)
        oh_i = [sb(f"oh_i{b}", [P, G_TOK, NK], F32R) for b in range(2)]
        eq_j = [sb("eq_j0", [P, G_TOK, NK])]
        assert sb.at <= ROUTE_TMP_END, (sb.at, ROUTE_TMP_END)
        sb = Region(KEEP_END)
        oh_j = [sb(f"oh_j{b}", [P, G_TOK, 2, NK], F32R) for b in range(2)]
        eq_j.append(sb("eq_j1", [P, G_TOK, NK]))
        g_lo = sb("g_lo", [P, G_TOK, NK])
        sb = Region(S)
        gh_in = [sb(f"gh_in{b}", [P, 2, T]) for b in range(2)]
        g_in = [sb(f"g_in{b}", [P, T // G_BLK, 2, G_BLK]) for b in range(2)]
        a_f = [sb(f"a_f{b}", [P, T]) for b in range(2)]
        a_hi = [sb(f"a_hi{b}", [P, T], F32R) for b in range(2)]
        a_lo = [sb(f"a_lo{b}", [P, T], F32R) for b in range(2)]

        ps = ctx.enter_context(nc.psum_tensor("ps", [P, 8, 512], F32))

        def bank(n, w=512):
            return ps[:, n, 0:w]

        def banks2(n, w):
            return ps[:, n:n + 2, :].rearrange("p a b -> p (a b)")[:, 0:w]

        def col(name, n=0):
            at = COL_AT[name] + n
            return cols[:, at:at + 1]

        gh_d = nc.dram_tensor("gelu_scratch", [JT, P, T], F32).ap()
        g_d = nc.dram_tensor("gate_scratch", [T // G_BLK, P, NK, G_BLK], F32).ap()

        def sem(name):
            return ctx.enter_context(nc.semaphore(name))

        cond_in, crow_in, const_in, table_in, x_in, keys_in = map(
            sem, ("cond_in", "crow_in", "const_in", "table_in", "x_in", "keys_in"))
        ring_in = [sem(f"ring_in{b}") for b in range(2)]
        ring_hi, ring_lo, ring_used = sem("ring_hi"), sem("ring_lo"), sem("ring_used")
        ada_in = [sem(f"ada_in{b}") for b in range(ADA_PE)]
        modf_done = sem("modf_done")
        mod_done, mod_copied = sem("mod_done"), sem("mod_copied")
        silu_ready, ones_ready, pads_ready = sem("silu_ready"), sem("ones_ready"), sem("pads_ready")
        dve_step, act_step = sem("dve_step"), sem("act_step")
        xstd_ready, xn_ready, amix_ready = sem("xstd_ready"), sem("xn_ready"), sem("amix_ready")
        x_turned, xt_ready, ct_ready, mod_turned = map(sem, ("x_turned", "xt_ready", "ct_ready", "mod_turned"))
        ht_hi_ready, htmp_ready, ht_lo_ready, hc_lo_ready = map(
            sem, ("ht_hi_ready", "htmp_ready", "ht_lo_ready", "hc_lo_ready"))
        kvq_copied, krt_ready, sq_ready = map(sem, ("kvq_copied", "krt_ready", "sq_ready"))
        sums_done, nstd_ready, normed, split_hi, split_lo = map(
            sem, ("sums_done", "nstd_ready", "normed", "split_hi", "split_lo"))
        tile_copied = sem("tile_copied")
        pooled_ready, pooled_hi, pooled_lo, pmix_used = map(
            sem, ("pooled_ready", "pooled_hi", "pooled_lo", "pmix_used"))
        diag_ready, rows_done, rows_ready = sem("diag_ready"), sem("rows_done"), sem("rows_ready")
        wqk_in, wv_in, wqk_hi_s, wqk_lo_s, wv_hi_s, wv_lo_s = map(
            sem, ("wqk_in", "wv_in", "wqk_hi_s", "wqk_lo_s", "wv_hi_s", "wv_lo_s"))
        pj_done, pj_hi, pj_free = sem("pj_done"), sem("pj_hi"), sem("pj_free")
        qr_rotated = sem("qr_rotated")
        s_done, max_ready, exp_ready, prob_ready = map(sem, ("s_done", "max_ready", "exp_ready", "prob_ready"))
        pt_turned, pt_hi_s, pt_lo_s = sem("pt_turned"), sem("pt_hi_s"), sem("pt_lo_s")
        mrg_ready = sem("mrg_ready")
        y_done, ystd_ready, xmid_ready, xmstd_ready, xmn_ready = map(
            sem, ("y_done", "ystd_ready", "xmid_ready", "xmstd_ready", "xmn_ready"))
        hf_turned, hf_hi_ready, hf_lo_even, hf_lo_odd, ytmp_ready, xmid_even, ftmp_ready = map(
            sem, ("hf_turned", "hf_hi_ready", "hf_lo_even", "hf_lo_odd", "ytmp_ready", "xmid_even", "ftmp_ready"))
        keys_hi_s, keys_lo_s = sem("keys_hi_s"), sem("keys_lo_s")
        q_hi_s, q_lo_s, sc_done, sc_copied = map(sem, ("q_hi_s", "q_lo_s", "sc_done", "sc_copied"))
        gelu_done = sem("gelu_done")
        gh_stored = [sem(f"gh_stored{b}") for b in range(2)]
        g_stored = [sem(f"g_stored{b}") for b in range(2)]
        logits_ready, exp_all, sel_ready, sel_turned = map(sem, ("logits_ready", "exp_all", "sel_ready", "sel_turned"))
        kt_ready, eqj_ready, oh_ready, oh_lo_ready, g_built, g_lo_ready, g_copied = map(
            sem, ("kt_ready", "eqj_ready", "oh_ready", "oh_lo_ready", "g_built", "g_lo_ready", "g_copied"))

        def g_parts():
            return ps[:, 0:4, :].rearrange("p a x -> p (a x)").rearrange("p (t s n) -> p t s n", s=2, n=NK)
        pair_in = [sem(f"pair_in{b}") for b in range(2)]
        a_ready, a_hi_s, a_lo_s = sem("a_ready"), sem("a_hi_s"), sem("a_lo_s")
        o_done, ostd_ready, otmp_ready, out_even, out_ready, out_stored = map(
            sem, ("o_done", "ostd_ready", "otmp_ready", "out_even", "out_ready", "out_stored"))

        block = ctx.enter_context(nc.Block())

        ring_sources = (("v", R_V), ("u", R_U), ("wq", R_WQ), ("w_out", R_WOUT), ("w_pool", R_WPOOL), ("w_in", R_IN))

        @block.sync
        def _(sp):
            def ring(t, off, src, b, first=False):
                if not first:
                    sp.wait_ge(ring_lo, t - 1)
                sp.dma_start(w_raw[b][:, :], src[bass.ds(off, 1)].rearrange("o p n -> (o p) n")).then_inc(ring_in[b], 16)

            def ring_at(t):
                name, start = next(x for x in ring_sources if x[1] <= t)
                ring(t, t - start, a[name], t % 2, first=t < 2)

            def ada_row_load(c, b):
                if isinstance(c, int) and c < 2:
                    sp.wait_ge(mod_done, c + 1)
                else:
                    sp.wait_ge(modf_done, 2 * c - 2)
                sp.dma_start(ada[b].rearrange("p k n -> p (k n)"),
                             a["w_ada_r"][bass.ds(c, 1)].rearrange("o p n -> (o p) n")).then_inc(ada_in[b], 16)

            sp.dma_start(x_sb[:, :, :], a["x"].rearrange("(a p) d -> p a d", p=P)).then_inc(x_in, 16)
            sp.dma_start(ctx_sb[:, :, :], a["ctx"].rearrange("(a p) d -> p a d", p=P)).then_inc(x_in, 16)
            for c in range(ADA_PE):
                sp.dma_start(ada_pe[c].rearrange("p k n -> p (k n)"), a["w_ada_c"][c]).then_inc(ada_in[c], 16)
                if c == ADA_PE - 3:
                    ring_at(0)
                    ring_at(1)
            ada_row_load(0, 0)
            ada_row_load(1, 1)
            with sp.Fori(0, R_GATES // 2 - 1) as i:
                for b in range(2):
                    ring(2 * i + 2 + b, 2 * i + 2 + b, a["w_in"], b)
            ring_at(R_GATES)
            ring_at(R_GATES + 1)
            with sp.Fori(0, 7) as i:
                for b in range(2):
                    ring(R_GATES + 2 + 2 * i + b, R_GATES + 2 + 2 * i + b, a["w_in"], b)
                    ada_row_load(2 + 2 * i + b, b)
            ring_at(R_WPOOL)
            ring_at(R_WPOOL + 1)
            def head_weights(h, first=False):
                if not first:
                    sp.wait_ge(wqk_lo_s, h)
                sp.dma_start(wqk_raw[:, :], a["wqk"][bass.ds(h, 1)].rearrange("o p n -> (o p) n")).then_inc(wqk_in, 16)
                if not first:
                    sp.wait_ge(wv_lo_s, h)
                sp.dma_start(wv_raw[:, :], a["wv"][bass.ds(h, 1)].rearrange("o p n -> (o p) n")).then_inc(wv_in, 16)
            sp.wait_ge(modf_done, 2 * ADA_DVE)
            head_weights(0, True)
            ring_at(R_WOUT)
            ring_at(R_WOUT + 1)
            with sp.Fori(1, H) as h:
                head_weights(h)
            for t in range(R_WOUT + 2, R_WQ):
                ring_at(t)
            with sp.Fori(0, PH) as i:
                for b in range(2):
                    ring(R_WQ + 2 * i + b, 2 * i + b, a["wq"], b)
            ring_at(R_U)
            ring_at(R_U + 1)

            def load_u(half, b):
                j = 2 * half + b
                ring(R_U + 2 + j, j + 2, a["u"], b)
            with sp.Fori(0, (G_FIRST + G_STEPS) // 2) as i:
                load_u(i, 0)
                load_u(i, 1)

            def g_store(blk, piece, bb):
                sp.wait_ge(g_copied, (blk + 1) * G_STEPS)
                ns = bass.ds(G_PIECE * piece, G_PIECE)
                sp.dma_start(g_d[bass.ds(blk, 1), :, ns, :].rearrange("o p n t -> (o p) n t"),
                             g_blk[bb][:, ns, :]).then_inc(g_stored[bb], 16)
            with sp.Fori(0, T // G_BLK // 2) as q:
                for bb in range(2):
                    with sp.Fori(0, G_STEPS // 2) as i:
                        for b in range(2):
                            load_u((G_FIRST + G_STEPS) // 2 + (2 * q + bb) * (G_STEPS // 2) + i, b)
                            g_store(2 * q + bb, 2 * i + b, bb)
            with sp.Fori((G_FIRST + G_STEPS + T // G_TOK) // 2, JT // 2 - 3) as i:
                load_u(i, 0)
                load_u(i, 1)
            for b in range(2):
                sp.wait_ge(g_stored[b], 16 * T // G_BLK // 2 * G_STEPS)
                sp.wait_ge(gh_stored[b], 16 * 2)
            def pair_load(p, b):
                sp.dma_start(gh_in[b][:, :, :], gh_d[bass.ds(2 * p, 2)].rearrange("j p t -> p j t")).then_inc(pair_in[b], 16)
                sp.dma_start(g_in[b][:, :, :, :], g_d[:, :, bass.ds(2 * p, 2), :].rearrange("k p j t -> p k j t")).then_inc(pair_in[b], 16)
            for p in range(2):
                pair_load(p, p)
                for b in range(2):
                    load_u(JT // 2 - 3 + p, b)
            ring_at(R_V)
            ring_at(R_V + 1)
            for b in range(2):
                sp.wait_ge(gh_stored[b], 16 * JT // 2)
            with sp.Fori(0, JT // 4 - 1) as i:
                for q in range(2):
                    for b in range(2):
                        t = 4 * i + 2 * q + b
                        ring(R_V + 2 + t, t + 2, a["v"], b)
                    sp.wait_ge(a_ready, 4 * i + 2 * q + 2)
                    pair_load(2 * i + q + 2, q)
            ring_at(R_END - 2)
            ring_at(R_END - 1)
            for tt in range(TT):
                sp.wait_ge(out_even if tt % 2 == 0 else out_ready, tt // 2 + 1)
                sp.dma_start(out[tt * P:(tt + 1) * P, :], x_sb[:, tt, :]).then_inc(out_stored, 16)
            sp.wait_ge(out_stored, 16 * TT)

        @block.gpsimd
        def _(pool):
            def lo(t, b):
                pool.wait_ge(ring_hi, t + 1)
                nc.gpsimd.tensor_tensor(w_lo[b][:, :], w_raw[b][:, :], w_hi[b][:, :].bitcast(F32),
                                        ALU.subtract).then_inc(ring_lo, 1)

            def head_lo(h):
                pool.wait_ge(wqk_hi_s, h + 1)
                nc.gpsimd.tensor_tensor(wqk_lo[:, :], wqk_raw[:, :], wqk_hi[:, :].bitcast(F32),
                                        ALU.subtract).then_inc(wqk_lo_s, 1)
                pool.wait_ge(wv_hi_s, h + 1)
                nc.gpsimd.tensor_tensor(wv_lo[:, :], wv_raw[:, :], wv_hi[:, :].bitcast(F32),
                                        ALU.subtract).then_inc(wv_lo_s, 1)

            nc.gpsimd.memset(ones[:, :], 1.0).then_inc(ones_ready, 1)
            lo(0, 0)
            lo(1, 1)
            for k in range(KC):
                pool.wait_ge(htmp_ready, 2 * k + 2)
                pool.wait_ge(ht_hi_ready, 2 * k + 2)
                nc.gpsimd.tensor_tensor(hc_lo[:, k, :], ctmp[k % 2][:, :], hc_hi[:, k, :].bitcast(F32),
                                        ALU.subtract).then_inc(hc_lo_ready, 1)
            nc.gpsimd.memset(poolx[:, :, 0:PAD], 0.0)
            nc.gpsimd.memset(poolx[:, :, PAD + T:], 0.0).then_inc(pads_ready, 1)
            with pool.Fori(1, R_WPOOL // 2) as i:
                lo(2 * i, 0)
                lo(2 * i + 1, 1)
            lo(R_WPOOL, 0)
            head_lo(0)
            lo(R_WPOOL + 1, 1)
            lo(R_WOUT, 0)
            lo(R_WOUT + 1, 1)
            with pool.Fori(1, H) as h:
                head_lo(h)
            with pool.Fori(R_WOUT // 2 + 1, R_WQ // 2 + 1) as i:
                lo(2 * i, 0)
                lo(2 * i + 1, 1)
            for tt in range(0, TT, 2):
                pool.wait_ge(ytmp_ready, tt + 1)
                nc.gpsimd.tensor_tensor(x_sb[:, tt, :], x_sb[:, tt, :], ytmp[tt][:, :], ALU.add).then_inc(xmid_even, 1)
            for k in range(1, KC, 2):
                pool.wait_ge(ftmp_ready, k + 1)
                pool.wait_ge(hf_hi_ready, k + 1)
                nc.gpsimd.tensor_tensor(ht_lo[:, k, :], ftmp[k % 4][:, :], ht_hi[:, k, :].bitcast(F32),
                                        ALU.subtract).then_inc(hf_lo_odd, 1)
            with pool.Fori(R_WQ // 2 + 1, (R_U + G_FIRST) // 2 + 1) as i:
                lo(2 * i, 0)
                lo(2 * i + 1, 1)

            def onehot_lo(u, b):
                pool.wait_ge(eqj_ready, u + 1)
                nc.gpsimd.tensor_tensor(oh_j[b][:, :, 1, :], eq_j[b][:, :, :],
                                        kt_glo[:, bass.ds(G_TOK * u, G_TOK)].unsqueeze(2).to_broadcast([P, G_TOK, NK]),
                                        ALU.mult).then_inc(oh_lo_ready, 1)
            onehot_lo(0, 0)
            onehot_lo(1, 1)
            with pool.Fori(1, T // G_TOK // 2) as i:
                for b in range(2):
                    lo(R_U + G_FIRST + 2 * i + b, b)
                    onehot_lo(2 * i + b, b)
            with pool.Fori((R_U + G_FIRST + T // G_TOK) // 2, R_END // 2) as i:
                lo(2 * i, 0)
                lo(2 * i + 1, 1)
            for tt in range(0, TT, 2):
                pool.wait_ge(otmp_ready, tt + 1)
                nc.gpsimd.tensor_tensor(x_sb[:, tt, :], x_sb[:, tt, :], ytmp[tt][:, :], ALU.add).then_inc(out_even, 1)

        @block.scalar
        def _(act):
            step = Steps(act, act_step)

            def sqrt_table():
                nc.scalar.activation(std[:, 7:8], col("eps"), ACT.Sqrt)

            def hi(half, b, first=False):
                act.wait_ge(ring_in[b], 16 * half + 16)
                if not first:
                    act.wait_ge(ring_used, 2 * half + b - 1)
                nc.scalar.activation(w_hi[b][:, :], w_raw[b][:, :], ACT.Copy).then_inc(ring_hi, 1)

            act.dma_start(cond[:, :, :], a["cond"]).then_inc(cond_in, 16)
            act.dma_start(cols[:, :], a["cols"]).then_inc(const_in, 16)
            act.dma_start(ident[:, :], a["ident"]).then_inc(const_in, 16)
            act.wait_ge(cond_in, 16)
            nc.scalar.activation(silu[:, :, :], cond[:, :, :], ACT.Silu).then_inc(silu_ready, 1)

            act.wait_ge(x_in, 32)
            for n in range(TT + CT):
                src = x_sb[:, n, :] if n < TT else ctx_sb[:, n - TT, :]
                step.add(nc.scalar.activation(xn[:, n, :], src, ACT.Square, accum_out=ss[:, n:n + 1]))
            step.sync()
            act.wait_ge(const_in, 32)
            for dst, name in ((fold, "fold"), (iota, "iota"), (edge, "edge"), (rot, "rot")):
                act.dma_start(dst[tuple(slice(None) for _ in dst.shape)], a[name]).then_inc(table_in, 16)
            nc.scalar.activation(std[:, 0:6], ss[:, 0:6], ACT.Sqrt, scale=1.0 / D, bias=col("eps")).then_inc(xstd_ready, 1)
            for k in range(KC):
                act.wait_ge(x_turned, 2 * k + 1)
                nc.scalar.activation(xn_t[:, k, 0:T], bank(4 + 2 * (k % 2)), ACT.Copy).then_inc(xt_ready, 1)
            hi(0, 0, True)
            hi(0, 1, True)
            for n in range(4):
                act.wait_ge(mod_done, 2 * n + 2)
                nc.scalar.activation(mod_row[:, n * 512:(n + 1) * 512], ps[0:2, n, :], ACT.Copy).then_inc(mod_copied, 1)
            act.wait_ge(amix_ready, 2)
            for k in range(KC):
                for s, (t0, n, dst) in enumerate(((0, T, ht_hi), (T, C, hc_hi))):
                    if s and k == 0:
                        act.wait_ge(ct_ready, KC)
                    nc.scalar.activation(dst[:, k, :], xn_t[:, k, t0:t0 + n], ACT.Identity,
                                         scale=a_mix[:, k, s:s + 1], bias=modc[:, k, s:s + 1]).then_inc(ht_hi_ready, 1)
            hi(1, 0)
            act.wait_ge(ring_used, 1)
            step.add(nc.scalar.activation(ckv[:, 0:T], bank(0), ACT.Copy))
            nc.scalar.activation(ckv[:, T:KEYS], bank(1, C), ACT.Copy).then_inc(kvq_copied, 1)
            hi(1, 1)
            hi(2, 0)
            act.wait_ge(ring_used, 3)
            nc.scalar.activation(cq[:, 0, :], bank(4), ACT.Copy).then_inc(kvq_copied, 1)
            hi(2, 1)
            act.wait_ge(ring_used, 4)
            nc.scalar.activation(cq[:, 1, :], bank(5), ACT.Copy).then_inc(kvq_copied, 1)
            act.dma_start(silu_row[:, :], a["c_row"]).then_inc(crow_in, 16)

            def pool_tile(half, b):
                n = 2 * half + b
                act.wait_ge(ring_used, R_POOLX + n + 1)
                nc.scalar.activation(poolx[:, bass.ds(n, 1), PAD:PAD + T].rearrange("p o t -> p (o t)"),
                                     bank(b), ACT.Copy).then_inc(tile_copied, 1)
                hi(R_POOLX // 2 + 1 + half, b)
            act.wait_ge(pads_ready, 1)
            pool_tile(0, 0)
            pool_tile(0, 1)
            act.wait_ge(sums_done, 1)
            step.add(nc.scalar.activation(nstd[:, 0:KEYS], banks2(6, KEYS), ACT.Sqrt, scale=1.0 / P, bias=col("eps")))
            nc.scalar.activation(nstd[:, KEYS:KEYS + T], bank(4), ACT.Sqrt, scale=0.5 / P, bias=col("eps")).then_inc(nstd_ready, 1)
            act.wait_ge(sums_done, 2)
            nc.scalar.activation(kr_hi[:, 0:T], bank(5), ACT.Copy).then_inc(split_hi, 1)
            nc.scalar.activation(kr_hi[:, T:KEYS], bank(3, C), ACT.Copy).then_inc(split_hi, 1)
            act.wait_ge(crow_in, 16)
            nc.scalar.activation(silu_row[:, :], silu_row[:, :], ACT.Silu).then_inc(silu_ready, 1)
            with act.Fori(1, 4) as i:
                pool_tile(i, 0)
                pool_tile(i, 1)
            act.wait_ge(normed, 1)
            nc.scalar.activation(kvn_hi[:, :], ckv[:, :], ACT.Copy).then_inc(split_hi, 1)
            act.wait_ge(normed, 3)
            nc.scalar.activation(cqn_hi[:, :, :], cq[:, :, :], ACT.Copy).then_inc(split_hi, 1)

            def gate_tile(half, b):
                n = 2 * half + b
                hi(R_GATES // 2 + 1 + half, b)
                act.wait_ge(ring_used, R_GATES + n + 1)
                nc.scalar.activation(gates[:, bass.ds(n, 1), :].rearrange("p o t -> p (o t)"),
                                     bank(b), ACT.Sigmoid).then_inc(tile_copied, 1)
            with act.Fori(0, 7) as i:
                gate_tile(i, 0)
                gate_tile(i, 1)
            gate_tile(7, 0)
            def wqk_split(h, before=None):
                act.wait_ge(wqk_in, 16 * h + 16)
                if before is not None:
                    act.wait_ge(pj_done, before)
                nc.scalar.activation(wqk_hi[:, :], wqk_raw[:, :], ACT.Copy).then_inc(wqk_hi_s, 1)

            def wv_split(h):
                act.wait_ge(wv_in, 16 * h + 16)
                nc.scalar.activation(wv_hi[:, :], wv_raw[:, :], ACT.Copy).then_inc(wv_hi_s, 1)

            def pj(n, dst, src):
                act.wait_ge(pj_done, n + 1)
                nc.scalar.activation(dst, src, ACT.Copy).then_inc(pj_hi, 1)

            def prob_exp(s, qt, first=False):
                act.wait_ge(max_ready, s + 1)
                if not first:
                    act.wait_ge(pt_turned, s - 1)
                nc.scalar.activation(prob[qt % 2][:, :], banks2(2 * (qt % 2), KEYS), ACT.Exp,
                                     bias=nmax[:, qt:qt + 1], accum_out=rsum[:, qt:qt + 1]).then_inc(exp_ready, 1)

            def pt_hi_copy(s, qt):
                act.wait_ge(pt_turned, s + 1)
                nc.scalar.activation(pt_hi[:, :, qt * P:(qt + 1) * P], banks2(4, KEYS).rearrange("p (k q) -> p k q", q=P),
                                     ACT.Copy).then_inc(pt_hi_s, 1)

            def gate_rows(n):
                act.wait_ge(rows_done, n + 1)
                nc.scalar.activation(g_row[:, n, :], banks2(4 - 2 * n, D), ACT.Copy).then_inc(rows_ready, 1)

            def qk_part(h, n):
                act.wait_ge(pj_done, n + 2)
                nc.scalar.activation(qn_hi[:, :], bank(6), ACT.Copy).then_inc(pj_hi, 1)
                act.wait_ge(qr_rotated, h + 1)
                nc.scalar.activation(qr_hi[:, :], qr_f[:, :], ACT.Copy).then_inc(pj_hi, 1)

            def k_part(n):
                pj(n + 2, k_hi[:, 0:T], bank(7))

            def k_ctx_part(n):
                pj(n + 3, k_hi[:, T:KEYS], bank(6, C))

            def mrg_hi_copy(h):
                act.wait_ge(mrg_ready, h + 1)
                nc.scalar.activation(ht_hi[:, bass.ds(h, 1), :].rearrange("p o t -> p (o t)"), mrg[:, :],
                                     ACT.Copy).then_inc(pj_hi, 1)

            def head(h, n, head0=False, last=False):
                s = 4 * h
                if not last:
                    wqk_split(h + 1, 4 if head0 else n)
                prob_exp(s, 0, head0)
                prob_exp(s + 1, 1, head0)
                pt_hi_copy(s, 0)
                if not head0:
                    mrg_hi_copy(h - 1)
                prob_exp(s + 2, 2)
                pt_hi_copy(s + 1, 1)
                pj(n + 1, v_hi[:, 0:4, :], bank(7).rearrange("p (k v) -> p k v", v=P))
                pj(n + 2, v_hi[:, 4:6, :], bank(6, C).rearrange("p (k v) -> p k v", v=P))
                prob_exp(s + 3, 3)
                pt_hi_copy(s + 2, 2)
                if not last:
                    wv_split(h + 1)
                if not last:
                    qk_part(h + 1, n + 3)
                    k_part(n + 3)
                pt_hi_copy(s + 3, 3)
                if not last:
                    k_ctx_part(n + 3)

            wqk_split(0)
            wv_split(0)
            gate_tile(7, 1)

            def pooled_split(g):
                act.wait_ge(pooled_ready, g + 1)
                nc.scalar.activation(ht_hi[:, 2 * g:2 * g + 2, :], poolx[:, 2 * g:2 * g + 2, PAD:PAD + T],
                                     ACT.Copy).then_inc(pooled_hi, 1)
            pooled_split(0)
            gate_rows(0)
            pooled_split(1)
            gate_rows(1)
            qk_part(0, 0)
            pooled_split(2)
            pooled_split(3)
            k_part(0)
            k_ctx_part(0)
            hi(R_WOUT // 2, 0)
            hi(R_WOUT // 2, 1)
            head(0, 3, head0=True)
            with act.Fori(1, H - 1) as h:
                head(h, 7 * h + 3)
            head(H - 1, 7 * (H - 1) + 3, last=True)
            mrg_hi_copy(H - 1)

            for k in range(KC):
                if k == KC - 1:
                    sqrt_table()
                hi(R_WOUT // 2 + 1 + k // 2, k % 2)

            def y_std(tt):
                if tt < TT - 1:
                    act.wait_ge(y_done, tt + 1)
                else:
                    act.wait_ge(ring_used, R_WQ)
                step.link(nc.scalar.activation(junk[:, :], banks2(2 * tt, D), ACT.Square, accum_out=ss[:, tt:tt + 1]))
                nc.scalar.activation(std[:, tt:tt + 1], ss[:, tt:tt + 1], ACT.Sqrt, scale=1.0 / D,
                                     bias=col("eps")).then_inc(ystd_ready, 1)

            def xm_std(tt):
                act.wait_ge(xmid_even if tt % 2 == 0 else xmid_ready, tt // 2 + 1)
                step.link(nc.scalar.activation(junk[:, :], x_sb[:, tt, :], ACT.Square, accum_out=ss2[:, tt:tt + 1]))
                nc.scalar.activation(std2[:, tt:tt + 1], ss2[:, tt:tt + 1], ACT.Sqrt, scale=1.0 / D,
                                     bias=col("eps")).then_inc(xmstd_ready, 1)
            for tt in range(TT):
                y_std(tt)
            for tt in range(TT):
                xm_std(tt)
            for k in range(KC):
                act.wait_ge(hf_turned, k + 1)
                nc.scalar.activation(ht_hi[:, k, :], bank(k), ACT.Identity, scale=a_ffn[:, k:k + 1],
                                     bias=modf[:, KC + k:KC + k + 1]).then_inc(hf_hi_ready, 1)
            act.dma_start(keys_raw[:, :, :], a["keys"]).then_inc(keys_in, 16)
            act.wait_ge(keys_in, 16)
            nc.scalar.activation(keys_hi[:, :, :], keys_raw[:, :, :], ACT.Copy).then_inc(keys_hi_s, 1)

            def route(half, b, first=False):
                m = 2 * half + b
                act.wait_ge(ring_used, R_WQ + m + 1)
                if not first:
                    act.wait_ge(sc_done, m - 1)
                nc.scalar.activation(q_hi[b][:, :], bank(b), ACT.Copy).then_inc(q_hi_s, 1)
                hi(R_WQ // 2 + 1 + half, b)
                act.wait_ge(sc_done, m + 1)
                nc.scalar.activation(s_sb[:, :, bass.ds(m, 1), :].rearrange("p a o n -> p a (o n)"),
                                     bank(2 + b).rearrange("p (a n) -> p a n", a=TT), ACT.Copy).then_inc(sc_copied, 1)
            route(0, 0, True)
            route(0, 1, True)
            with act.Fori(1, PH) as i:
                route(i, 0)
                route(i, 1)

            def expert(half, b, first=False):
                j = 2 * half + b
                act.wait_ge(ring_used, R_U + j + 1)
                if not first:
                    act.wait_ge(gh_stored[b], 16 * half)
                nc.scalar.activation(gh[b][:, :], bank(4 + b), ACT.Gelu).then_inc(gelu_done, 1)
                hi(R_U // 2 + 1 + half, b)
                act.wait_ge(gelu_done, j + 1)
                act.dma_start(gh_d[bass.ds(j, 1)].rearrange("o p n -> (o p) n"), gh[b][:, :]).then_inc(gh_stored[b], 16)
            expert(0, 0, True)
            expert(0, 1, True)
            with act.Fori(1, G_FIRST // 2 - 2) as i:
                expert(i, 0)
                expert(i, 1)
            act.wait_ge(logits_ready, 2 * TT)
            nc.scalar.activation(sel_e[:, :, :], sel_e[:, :, :], ACT.Exp).then_inc(exp_all, 1)
            with act.Fori(G_FIRST // 2 - 2, G_FIRST // 2) as i:
                expert(i, 0)
                expert(i, 1)
            with act.Fori(0, T // G_TOK // 2) as i:
                for b in range(2):
                    expert(G_FIRST // 2 + i, b)
                    act.wait_ge(g_built, 2 * i + b + 1)
                    nc.scalar.activation(g_lo[:, :, :], g_parts()[:, :, 1, :], ACT.Copy).then_inc(g_lo_ready, 1)
            with act.Fori((G_FIRST + T // G_TOK) // 2, JT // 2 - 1) as i:
                expert(i, 0)
                expert(i, 1)

            def weigh(half, b, first=False):
                j = 2 * half + b
                act.wait_ge(a_ready, j + 1)
                if not first:
                    act.wait_ge(ring_used, R_V + j - 1)
                nc.scalar.activation(a_hi[b][:, :], a_f[b][:, :], ACT.Copy).then_inc(a_hi_s, 1)
            weigh(0, 0, True)
            weigh(0, 1, True)
            expert(JT // 2 - 1, 0)
            expert(JT // 2 - 1, 1)
            with act.Fori(1, JT // 2) as i:
                for b in range(2):
                    hi(R_V // 2 + i, b)
                    weigh(i, b)
            sqrt_table()
            for tt in range(TT):
                if tt < TT - 1:
                    act.wait_ge(o_done, tt + 1)
                else:
                    act.wait_ge(ring_used, R_END)
                step.link(nc.scalar.activation(junk[:, :], banks2(2 * tt, D), ACT.Square, accum_out=ss[:, tt:tt + 1]))
                nc.scalar.activation(std[:, tt:tt + 1], ss[:, tt:tt + 1], ACT.Sqrt, scale=1.0 / D,
                                     bias=col("eps")).then_inc(ostd_ready, 1)

        @block.vector
        def _(dve):
            step = Steps(dve, dve_step)
            v = nc.vector

            dve.wait_ge(xstd_ready, 1)
            step.link(v.reciprocal(rs[:, 0:6], std[:, 0:6]))
            for n in range(TT + CT):
                src = x_sb[:, n, :] if n < TT else ctx_sb[:, n - TT, :]
                v.tensor_scalar(xn[:, n, :], src, rs[:, n:n + 1], None, ALU.mult).then_inc(xn_ready, 1)
            for k in range(KC):
                dve.wait_ge(x_turned, 2 * k + 2)
                v.tensor_copy(xn_t[:, k, T:KEYS], bank(5 + 2 * (k % 2), C)).then_inc(ct_ready, 1)
            bada = cols[:, COL_AT["b_ada"]:COL_AT["b_ada"] + 48]
            dve.wait_ge(mod_turned, 1)
            step.link(v.tensor_tensor(modc[:, :, :], bank(4, 4 * KC).rearrange("p (m s) -> p m s", s=2),
                                      bada[:, 0:2 * KC].unsqueeze(2).to_broadcast([P, 2 * KC, 2]), ALU.add))
            for s in range(2):
                g = cols[:, COL_AT["g_mix_pre"]:COL_AT["g_mix_pre"] + KC]
                v.scalar_tensor_tensor(out=a_mix[:, :, s], in0=modc[:, KC:2 * KC, s], scalar=1.0, in1=g,
                                       op0=ALU.add, op1=ALU.mult).then_inc(amix_ready, 1)
            dve.wait_ge(amix_ready, 2)
            dve.wait_ge(xt_ready, KC)
            for k in range(KC):
                if k >= 2:
                    dve.wait_ge(ht_lo_ready, k - 1)
                    dve.wait_ge(hc_lo_ready, k - 1)
                v.tensor_scalar(htmp[k % 2][:, :], xn_t[:, k, 0:T], a_mix[:, k, 0:1], modc[:, k, 0:1],
                                ALU.mult, ALU.add).then_inc(htmp_ready, 1)
                v.tensor_scalar(ctmp[k % 2][:, :], xn_t[:, k, T:KEYS], a_mix[:, k, 1:2], modc[:, k, 1:2],
                                ALU.mult, ALU.add).then_inc(htmp_ready, 1)
                dve.wait_ge(htmp_ready, 2 * k + 1)
                dve.wait_ge(ht_hi_ready, 2 * k + 1)
                v.tensor_tensor(ht_lo[:, k, :], htmp[k % 2][:, :], ht_hi[:, k, :].bitcast(F32),
                                ALU.subtract).then_inc(ht_lo_ready, 1)

            dve.wait_ge(table_in, 64)
            dve.wait_ge(ring_used, 2)
            v.tensor_tensor(krt[:, 0:T], bank(2), rot[:, 0:T], ALU.mult)
            v.tensor_tensor(krt[:, T:KEYS], bank(3, C), rot[:, T:KEYS], ALU.mult).then_inc(krt_ready, 1)
            dve.wait_ge(kvq_copied, 3)
            v.tensor_tensor(sq[:, 0:KEYS], ckv[:, :], ckv[:, :], ALU.mult)
            v.tensor_tensor(sq[:, KEYS:KEYS + 2 * T], cq.rearrange("p a t -> p (a t)"), cq.rearrange("p a t -> p (a t)"),
                            ALU.mult).then_inc(sq_ready, 1)
            dve.wait_ge(nstd_ready, 1)
            step.link(v.reciprocal(nstd[:, :], nstd[:, :]))
            v.scalar_tensor_tensor(out=ckv[:, :], in0=ckv[:, :], scalar=col("g_kv"), in1=nstd[:, 0:KEYS],
                                   op0=ALU.mult, op1=ALU.mult).then_inc(normed, 1)
            step.link(v.tensor_scalar(gq_scaled[:, :], cols[:, COL_AT["g_q"]:COL_AT["g_q"] + 2], SCALE, None, ALU.mult))
            for k in range(2):
                v.scalar_tensor_tensor(out=cq[:, k, :], in0=cq[:, k, :], scalar=gq_scaled[:, k:k + 1],
                                       in1=nstd[:, KEYS:KEYS + T], op0=ALU.mult, op1=ALU.mult).then_inc(normed, 1)
            dve.wait_ge(split_hi, 2)
            v.tensor_tensor(kr_lo[:, 0:T], bank(5), kr_hi[:, 0:T].bitcast(F32), ALU.subtract)
            v.tensor_tensor(kr_lo[:, T:KEYS], bank(3, C), kr_hi[:, T:KEYS].bitcast(F32), ALU.subtract).then_inc(split_lo, 1)

            def mod_rows(half, b):
                dve.wait_ge(ada_in[b], 16 * half + 32)
                for n in range(2):
                    m = 2 * (2 * half + b) + n
                    v.scalar_tensor_tensor(out=ada_row[b][:, n, :], in0=ada_row[b][:, n, :], scalar=1.0,
                                           in1=silu_row[:, :], op0=ALU.mult, op1=ALU.mult,
                                           accum_out=modf_raw[:, bass.ds(m, 1)]).then_inc(modf_done, 1)
            ada_row = [t.rearrange("p k n -> p (k n)").rearrange("p (a d) -> p a d", d=D) for t in ada]

            for g, w in enumerate(WINDOWS):
                if g == 2:
                    dve.wait_ge(silu_ready, 2)
                    mod_rows(0, 0)
                    mod_rows(0, 1)
                gs = slice(2 * g, 2 * g + 2)
                dve.wait_ge(tile_copied, 2 * g + 2)
                if g:
                    dve.wait_ge(pooled_ready, g)
                xg = poolx[:, gs, :]
                lo_i, hi_i = 1, T + 2 * PAD
                step.link(v.tensor_tensor(poolw[0][:, :, 1:hi_i], xg[:, :, 0:hi_i - 1], xg[:, :, 1:hi_i], ALU.add))
                cur, sh = 0, 1
                while 2 * sh < w:
                    nl, nh = lo_i + sh, hi_i - sh
                    step.link(v.tensor_tensor(poolw[1 - cur][:, :, nl:nh], poolw[cur][:, :, nl - sh:nh - sh],
                                              poolw[cur][:, :, nl + sh:nh + sh], ALU.add))
                    lo_i, hi_i, cur, sh = nl, nh, 1 - cur, 2 * sh
                assert lo_i <= PAD and hi_i >= PAD + T
                W = poolw[cur]
                for e0, at in ((0, PAD), (PAD, T)):
                    ee = edge[:, g, e0:e0 + PAD].unsqueeze(1).to_broadcast([P, 2, PAD])
                    step.add(v.tensor_tensor(W[:, :, at:at + PAD], W[:, :, at:at + PAD], ee, ALU.mult))
                step.sync()
                v.scalar_tensor_tensor(out=poolx[:, gs, PAD:PAD + T], in0=W[:, :, PAD:PAD + T], scalar=1.0 / w,
                                       in1=poolx[:, gs, PAD:PAD + T], op0=ALU.mult, op1=ALU.subtract).then_inc(pooled_ready, 1)
            dve.wait_ge(split_hi, 3)
            v.tensor_tensor(kvn_lo[:, :], ckv[:, :], kvn_hi[:, :].bitcast(F32), ALU.subtract).then_inc(split_lo, 1)
            dve.wait_ge(split_hi, 4)
            v.tensor_tensor(cqn_lo[:, :, :], cq[:, :, :], cqn_hi[:, :, :].bitcast(F32), ALU.subtract).then_inc(split_lo, 1)
            with dve.Fori(1, ADA_DVE // 2) as i:
                mod_rows(i, 0)
                mod_rows(i, 1)
            dve.wait_ge(modf_done, 2 * ADA_DVE)
            step.link(v.tensor_tensor(modf[:, :], modf_raw[:, :], bada[:, 2 * KC:6 * KC], ALU.add))
            g = cols[:, COL_AT["g_ffn_pre"]:COL_AT["g_ffn_pre"] + KC]
            step.add(v.scalar_tensor_tensor(out=a_ffn[:, :], in0=modf[:, 2 * KC:3 * KC], scalar=1.0, in1=g,
                                            op0=ALU.add, op1=ALU.mult))
            for n, (m0, name) in enumerate(((0, "g_mix_post"), (3 * KC, "g_ffn_post"))):
                g = cols[:, COL_AT[name]:COL_AT[name] + KC]
                step.add(v.tensor_tensor(gcol[:, n, :], modf[:, m0:m0 + KC], g, ALU.mult))
            step.sync()
            for n in range(2):
                for k in range(KC):
                    v.tensor_scalar(diag[:, n, k * P:(k + 1) * P], ident[:, :], gcol[:, n, k:k + 1], None,
                                    ALU.mult).then_inc(diag_ready, 1)
            def pooled_part(g):
                dve.wait_ge(pooled_hi, g + 1)
                v.tensor_tensor(ht_lo[:, 2 * g:2 * g + 2, :], poolx[:, 2 * g:2 * g + 2, PAD:PAD + T],
                                ht_hi[:, 2 * g:2 * g + 2, :].bitcast(F32), ALU.subtract).then_inc(pooled_lo, 1)

            def pooled_mix(m):
                dve.wait_ge(ring_used, R_WPOOL + m // 4 + 1)
                v.scalar_tensor_tensor(out=gates[:, KC + m, :], in0=bank((m + 4) % 6), scalar=col("pool_scale", m),
                                       in1=gates[:, KC + m, :], op0=ALU.mult, op1=ALU.mult).then_inc(pmix_used, 1)

            def pj_lo(n, dst, src, hi_view):
                dve.wait_ge(pj_hi, n + 1)
                v.tensor_tensor(dst, src, hi_view.bitcast(F32), ALU.subtract).then_inc(pj_free, 1)

            rot_q = rot[:, 0:T]

            def row_max(s, qt):
                dve.wait_ge(s_done, s + 1)
                v.tensor_reduce(nmax[:, qt:qt + 1], banks2(2 * (qt % 2), KEYS), AX.X, ALU.max,
                                negate=True).then_inc(max_ready, 1)

            def norm_rows(s, qt, cnt):
                dve.wait_ge(exp_ready, s + 1)
                cnt.link(v.reciprocal(rinv[:, qt:qt + 1], rsum[:, qt:qt + 1]))
                v.tensor_scalar(prob[qt % 2][:, :], prob[qt % 2][:, :], rinv[:, qt:qt + 1], None,
                                ALU.mult).then_inc(prob_ready, 1)

            def pt_lo_part(s, qt):
                dve.wait_ge(pt_hi_s, s + 1)
                q = slice(qt * P, (qt + 1) * P)
                v.tensor_tensor(pt_lo[:, :, q], banks2(4, KEYS).rearrange("p (k q) -> p k q", q=P),
                                pt_hi[:, :, q].bitcast(F32), ALU.subtract).then_inc(pt_lo_s, 1)

            def merge_gated(h, n, cnt):
                dve.wait_ge(pj_done, n + 1)
                cnt.link(v.tensor_tensor(mrg[:, :], bank(6), gates[:, bass.ds(h, 1), :].rearrange("p o t -> p (o t)"), ALU.mult))
                v.tensor_tensor(mrg[:, :], mrg[:, :], gates[:, bass.ds(KC + h, 1), :].rearrange("p o t -> p (o t)"),
                                ALU.add).then_inc(mrg_ready, 1)

            def merge_lo(h, n):
                dve.wait_ge(pj_hi, n + 1)
                v.tensor_tensor(ht_lo[:, bass.ds(h, 1), :].rearrange("p o t -> p (o t)"), mrg[:, :],
                                ht_hi[:, bass.ds(h, 1), :].rearrange("p o t -> p (o t)").bitcast(F32),
                                ALU.subtract).then_inc(pj_free, 1)

            def rotate(h, n):
                dve.wait_ge(pj_done, n + 1)
                v.tensor_tensor(qr_f[:, :], bank(7), rot_q, ALU.mult).then_inc(qr_rotated, 1)

            def qk(h, n):
                pj_lo(n, qn_lo[:, :], bank(6), qn_hi[:, :])
                pj_lo(n + 1, qr_lo[:, :], qr_f[:, :], qr_hi[:, :])

            def head(h, n, cnt, head0=False, last=False):
                s = 4 * h
                row_max(s, 0)
                row_max(s + 1, 1)
                norm_rows(s, 0, cnt)
                norm_rows(s + 1, 1, cnt)
                if not head0:
                    merge_gated(h - 1, n, cnt)
                pt_lo_part(s, 0)
                row_max(s + 2, 2)
                if not head0:
                    merge_lo(h - 1, n)
                norm_rows(s + 2, 2, cnt)
                pt_lo_part(s + 1, 1)
                pj_lo(n + 1, v_lo[:, 0:4, :], bank(7).rearrange("p (k v) -> p k v", v=P), v_hi[:, 0:4, :])
                row_max(s + 3, 3)
                pj_lo(n + 2, v_lo[:, 4:6, :], bank(6, C).rearrange("p (k v) -> p k v", v=P), v_hi[:, 4:6, :])
                if not last:
                    rotate(h + 1, n + 3)
                pt_lo_part(s + 2, 2)
                norm_rows(s + 3, 3, cnt)
                if not last:
                    qk(h + 1, n + 3)
                    pj_lo(n + 5, k_lo[:, 0:T], bank(7), k_hi[:, 0:T])
                pt_lo_part(s + 3, 3)
                if not last:
                    pj_lo(n + 6, k_lo[:, T:KEYS], bank(6, C), k_hi[:, T:KEYS])

            pooled_part(0)
            pooled_part(1)
            rotate(0, 0)
            qk(0, 0)
            pooled_part(2)
            pooled_part(3)
            pj_lo(2, k_lo[:, 0:T], bank(7), k_hi[:, 0:T])
            for m in range(4):
                pooled_mix(m)
            pj_lo(3, k_lo[:, T:KEYS], bank(6, C), k_hi[:, T:KEYS])
            for m in range(4, KC):
                pooled_mix(m)
            head(0, 3, step, head0=True)
            PER_HEAD = TT + 1
            n0 = step.n
            with dve.Fori(1, H - 1) as h:
                cnt = Steps(dve, dve_step)
                cnt.n = h * PER_HEAD + (n0 - PER_HEAD)
                head(h, 7 * h + 3, cnt)
            step.n = n0 + (H - 2) * PER_HEAD
            n0 = step.n
            head(H - 1, 7 * (H - 1) + 3, step, last=True)
            assert step.n == n0 + PER_HEAD
            merge_gated(H - 1, 7 * H - 1, step)
            merge_lo(H - 1, 7 * H - 1)

            def scaled_rows(tt, n, ready):
                step.link(v.reciprocal(rs[:, tt:tt + 1], std[:, tt:tt + 1]))
                v.scalar_tensor_tensor(out=ytmp[tt][:, :], in0=banks2(2 * tt, D), scalar=rs[:, tt:tt + 1],
                                       in1=g_row[:, n, :], op0=ALU.mult, op1=ALU.mult).then_inc(ready, 1)

            def residual(tt, ready, done):
                if tt % 2:
                    dve.wait_ge(ready, tt + 1)
                    v.tensor_tensor(x_sb[:, tt, :], x_sb[:, tt, :], ytmp[tt][:, :], ALU.add).then_inc(done, 1)

            def mid_norm(tt):
                dve.wait_ge(xmstd_ready, tt + 1)
                step.link(v.reciprocal(rs2[:, tt:tt + 1], std2[:, tt:tt + 1]))
                v.tensor_scalar(xm_n[:, tt, :], x_sb[:, tt, :], rs2[:, tt:tt + 1], None, ALU.mult).then_inc(xmn_ready, 1)
            dve.wait_ge(rows_ready, 2)
            for tt in range(TT):
                dve.wait_ge(ystd_ready, tt + 1)
                scaled_rows(tt, 0, ytmp_ready)
                if tt >= 2:
                    residual(1 if tt == 2 else 3, ytmp_ready, xmid_ready)
            for tt in range(TT):
                mid_norm(tt)
            for k in range(KC):
                dve.wait_ge(hf_hi_ready, k + 1)
                if k >= 4:
                    dve.wait_ge(hf_lo_odd if k % 2 else hf_lo_even, (k - 4) // 2 + 1)
                v.tensor_scalar(ftmp[k % 4][:, :], bank(k), a_ffn[:, k:k + 1], modf[:, KC + k:KC + k + 1],
                                ALU.mult, ALU.add).then_inc(ftmp_ready, 1)
                if k % 2 == 0:
                    dve.wait_ge(ftmp_ready, k + 1)
                    v.tensor_tensor(ht_lo[:, k, :], ftmp[k % 4][:, :], ht_hi[:, k, :].bitcast(F32),
                                    ALU.subtract).then_inc(hf_lo_even, 1)
            dve.wait_ge(keys_hi_s, 1)
            v.tensor_tensor(keys_lo[:, :, :], keys_raw[:, :, :], keys_hi[:, :, :].bitcast(F32), ALU.subtract).then_inc(keys_lo_s, 1)

            def q_part(m, b):
                dve.wait_ge(q_hi_s, m + 1)
                v.tensor_tensor(q_lo[b][:, :], bank(b), q_hi[b][:, :].bitcast(F32), ALU.subtract).then_inc(q_lo_s, 1)
            with dve.Fori(0, PH) as i:
                q_part(2 * i, 0)
                q_part(2 * i + 1, 1)

            dve.wait_ge(sc_copied, 2 * PH)
            n0 = step.n

            def route_tile(tt, cnt):
                def sync():
                    cnt.sync()
                    v.memset(spacer[:, :], 0.0)
                cnt.add(v.tensor_copy(s_cur[:, :, :], s_sb[:, bass.ds(tt, 1), :, :].rearrange("p o h n -> p (o h) n")))
                sync()
                for h in range(2 * PH):
                    cnt.add(v.max(top[:, h, 0:8], s_cur[:, h, :]))
                sync()
                for h in range(2 * PH):
                    cnt.add(v.max_index(top_i[:, h, 0:8], top[:, h, 0:8], s_cur[:, h, :]))
                    cnt.add(v.match_replace(s_work[:, h, :], top[:, h, 0:8], s_cur[:, h, :], -3.0e38))
                sync()
                for h in range(2 * PH):
                    cnt.add(v.max(top[:, h, 8:16], s_work[:, h, :]))
                sync()
                for h in range(2 * PH):
                    cnt.add(v.max_index(top_i[:, h, 8:16], top[:, h, 8:16], s_work[:, h, :]))
                sync()
                tv = top.rearrange("p (h two) k -> p h two k", two=2)
                for h in range(PH):
                    cnt.add(v.tensor_tensor(cand[:, h, :].rearrange("p (x y) -> p x y", y=TOPK),
                                            tv[:, h, 0, :].unsqueeze(2).to_broadcast([P, TOPK, TOPK]),
                                            tv[:, h, 1, :].unsqueeze(1).to_broadcast([P, TOPK, TOPK]), ALU.add))
                sync()
                for h in range(PH):
                    cnt.add(v.max(best[:, h, 0:8], cand[:, h, :]))
                sync()
                for h in range(PH):
                    cnt.add(v.max_index(pos[:, h, 0:8], best[:, h, 0:8], cand[:, h, :]))
                    cnt.add(v.match_replace(cand_work[:, h, :], best[:, h, 0:8], cand[:, h, :], -3.0e38))
                sync()
                for h in range(PH):
                    cnt.add(v.max(best[:, h, 8:16], cand_work[:, h, :]))
                sync()
                for h in range(PH):
                    cnt.add(v.max_index(pos[:, h, 8:16], best[:, h, 8:16], cand_work[:, h, :]))
                cnt.add(v.tensor_tensor(sel_e[:, bass.ds(tt * PH, PH), :], best[:, :, :],
                                        best[:, :, 0:1].to_broadcast([P, PH, TOPK]), ALU.subtract))
                sync()
                pf = pos.rearrange("p h k -> p (h k)")
                cnt.add(v.tensor_scalar(pos_a[:, :], pf, 4, None, ALU.logical_shift_right))
                cnt.add(v.tensor_scalar(pos_b[:, :], pf, 15, None, ALU.bitwise_and))
                sync()
                iv = top_i.rearrange("p (h two) k -> p h two k", two=2)
                for half, (pp, dst) in enumerate(((pos_a, sel_i), (pos_b, sel_j))):
                    cnt.link(v.tensor_tensor(eq[:, :, :], pp[:, :].unsqueeze(2).to_broadcast([P, PH * TOPK, TOPK]),
                                             iota[:, 0:TOPK].unsqueeze(1).to_broadcast([P, PH * TOPK, TOPK]), ALU.is_equal))
                    cnt.link(v.tensor_tensor(eq2.rearrange("p (h k) r -> p h k r", h=PH),
                                             eq.rearrange("p (h k) r -> p h k r", h=PH),
                                             iv[:, :, half, :].unsqueeze(2).to_broadcast([P, PH, TOPK, TOPK]), ALU.mult))
                    v.tensor_reduce(dst[:, bass.ds(tt, 1), :].rearrange("p o k -> p (o k)"), eq2[:, :, :],
                                    AX.X, ALU.add).then_inc(logits_ready, 1)
            ROUTE_STEPS = 1 + 5 * 2 * PH + 6 * PH + 7
            with dve.Fori(0, TT) as tt:
                cnt = Steps(dve, dve_step)
                cnt.n = tt * ROUTE_STEPS + n0
                route_tile(tt, cnt)
            step.n = n0 + TT * ROUTE_STEPS
            dve.wait_ge(exp_all, 1)
            step.link(v.tensor_reduce(sel_s[:, :], sel_e[:, :, :], AX.X, ALU.add))
            step.link(v.reciprocal(sel_r[:, :], sel_s[:, :]))
            v.tensor_tensor(sel_e[:, :, :], sel_e[:, :, :], sel_r[:, :].unsqueeze(2).to_broadcast([P, TT * PH, TOPK]),
                            ALU.mult).then_inc(sel_ready, 1)
            dve.wait_ge(sel_turned, 1)
            step.add(v.tensor_copy(kt_i[:, :], bank(0)))
            step.add(v.tensor_copy(kt_j[:, :], bank(1)))
            step.add(v.tensor_copy(kt_g[:, :], bank(2)))
            step.sync()
            step.link(v.tensor_copy(kt_ghi[:, :], kt_g[:, :]))
            v.tensor_tensor(kt_glo[:, :], kt_g[:, :], kt_ghi[:, :].bitcast(F32), ALU.subtract).then_inc(kt_ready, 1)
            dve.wait_ge(kt_ready, 1)

            def onehots(u, b, first=False):
                def per_token(t):
                    return t[:, bass.ds(G_TOK * u, G_TOK)].unsqueeze(2).to_broadcast([P, G_TOK, NK])
                keys = iota[:, :].unsqueeze(1).to_broadcast([P, G_TOK, NK])
                if not first:
                    dve.wait_ge(oh_lo_ready, u - 1)
                v.tensor_tensor(eq_j[b][:, :, :], keys, per_token(kt_j), ALU.is_equal).then_inc(eqj_ready, 1)
                v.tensor_tensor(oh_i[b][:, :, :], keys, per_token(kt_i), ALU.is_equal)
                dve.wait_ge(eqj_ready, u + 1)
                v.tensor_tensor(oh_j[b][:, :, 0, :], eq_j[b][:, :, :], per_token(kt_ghi[:, :].bitcast(F32)),
                                ALU.mult).then_inc(oh_ready, 1)

            def g_sum(u, at, bb, stored):
                if stored is not None:
                    dve.wait_ge(g_stored[bb], stored)
                dve.wait_ge(g_lo_ready, u + 1)
                v.tensor_tensor(g_blk[bb][:, :, bass.ds(at, G_TOK)].rearrange("p n t -> p t n"),
                                g_parts()[:, :, 0, :], g_lo[:, :, :], ALU.add).then_inc(g_copied, 1)
            onehots(0, 0, True)
            onehots(1, 1, True)

            def g_block(q, bb, first=False, last=False):
                def pair(i, ahead=True):
                    for b in range(2):
                        u = (2 * q + bb) * G_STEPS + 2 * i + b
                        if ahead:
                            dve.wait_ge(g_built, u + 1)
                            onehots(u + 2, b)
                        g_sum(u, 2 * G_TOK * i + G_TOK * b, bb, None if first else 16 * G_STEPS * q)
                with dve.Fori(0, G_STEPS // 2 - 1) as i:
                    pair(i)
                pair(G_STEPS // 2 - 1, ahead=not last)
            g_block(0, 0, True)
            g_block(0, 1, True)
            with dve.Fori(1, T // G_BLK // 2 - 1) as q:
                g_block(q, 0)
                g_block(q, 1)
            g_block(T // G_BLK // 2 - 1, 0)
            g_block(T // G_BLK // 2 - 1, 1, last=True)

            def weigh(j, half, b, q, first=False):
                if b == 0:
                    dve.wait_ge(pair_in[q], 32 * half + 32)
                v.tensor_tensor(a_f[b].rearrange("p (k t) -> p k t", t=G_BLK),
                                gh_in[q][:, b, :].rearrange("p (k t) -> p k t", t=G_BLK),
                                g_in[q][:, :, b, :], ALU.mult).then_inc(a_ready, 1)
                dve.wait_ge(a_hi_s, j + 1)
                if not first:
                    dve.wait_ge(ring_used, R_V + j - 1)
                v.tensor_tensor(a_lo[b][:, :], a_f[b][:, :], a_hi[b][:, :].bitcast(F32), ALU.subtract).then_inc(a_lo_s, 1)
            for n in range(4):
                weigh(n, 0, n % 2, n // 2, n < 2)
            with dve.Fori(1, JT // 4) as i:
                for n in range(4):
                    weigh(4 * i + n, i, n % 2, n // 2)
            for tt in range(TT):
                dve.wait_ge(ostd_ready, tt + 1)
                scaled_rows(tt, 1, otmp_ready)
                residual(tt, otmp_ready, out_ready)

        @block.tensor
        def _(pe):
            mm = nc.tensor.matmul

            def mod(c):
                pe.wait_ge(ada_in[c], 16)
                for k in range(KC):
                    ins = mm(ps[0:2, c // 2, (c % 2) * ADA_W:(c % 2 + 1) * ADA_W], silu[:, k, :], ada_pe[c][:, k, :],
                             start=(k == 0), stop=(k == KC - 1))
                ins.then_inc(mod_done, 1)

            def ring_wait(t):
                pe.wait_ge(ring_hi, t + 1)
                pe.wait_ge(ring_lo, t + 1)

            def project(b, dst, hi_t, lo_t, n, fresh=False):
                q = 0
                for k in range(KC):
                    ks = slice(k * P, (k + 1) * P)
                    if fresh:
                        pe.wait_ge(hf_lo_odd if k % 2 else hf_lo_even, k // 2 + 1)
                    for w, m in ((w_hi[b], hi_t), (w_hi[b], lo_t), (w_lo[b], hi_t)):
                        ins = mm(dst, w[:, ks], m[:, k, :], start=(q == 0), stop=(q == 3 * KC - 1))
                        q += 1
                return ins

            pe.wait_ge(silu_ready, 1)
            for c in range(ADA_PE - 3):
                mod(c)
            pe.wait_ge(const_in, 32)
            pe.wait_ge(xn_ready, TT + CT)
            for k in range(KC):
                for s, (t0, tn) in enumerate(((0, TT), (TT, CT))):
                    if k >= 2:
                        pe.wait_ge((xt_ready, ct_ready)[s], k - 1)
                    for n in range(tn):
                        ins = nc.tensor.transpose(ps[:, 4 + 2 * (k % 2) + s, n * P:(n + 1) * P],
                                                  xn[:, t0 + n, k * P:(k + 1) * P], ident[:, :])
                    ins.then_inc(x_turned, 1)
            for c in range(ADA_PE - 3, ADA_PE):
                mod(c)
            pe.wait_ge(xt_ready, KC)
            for m in range(2 * KC):
                if m % 4 == 0:
                    pe.wait_ge(mod_copied, m // 4 + 1)
                ins = nc.tensor.transpose(ps[:, 4, 2 * m:2 * m + 2], mod_row[:, m * P:(m + 1) * P], ident[0:2, 0:2])
            ins.then_inc(mod_turned, 1)
            for t in range(2):
                ring_wait(t)
                for k in range(KC):
                    ks = slice(k * P, (k + 1) * P)
                    for dst, hi_t, lo_t, ready in ((bank(2 * t), ht_hi, ht_lo, ht_lo_ready),
                                                   (bank(2 * t + 1, C), hc_hi, hc_lo, hc_lo_ready)):
                        if t == 0:
                            pe.wait_ge(ready, k + 1)
                        for q, (w, m) in enumerate(((w_hi[t], hi_t), (w_hi[t], lo_t), (w_lo[t], hi_t))):
                            ins = mm(dst, w[:, ks], m[:, k, :], start=(k == 0 and q == 0), stop=(k == KC - 1 and q == 2))
                ins.then_inc(ring_used, 1)
            for t in range(2, 4):
                ring_wait(t)
                project(t % 2, bank(2 + t), ht_hi, ht_lo, T).then_inc(ring_used, 1)
            pe.wait_ge(kvq_copied, 1)

            def plain_tile(t, n, b, first=False):
                ring_wait(t)
                if not first:
                    pe.wait_ge(tile_copied, n - 1)
                project(b, bank(b), ht_hi, ht_lo, T).then_inc(ring_used, 1)
            plain_tile(R_POOLX, 0, 0, True)
            plain_tile(R_POOLX + 1, 1, 1, True)
            pe.wait_ge(ones_ready, 1)
            pe.wait_ge(kvq_copied, 3)
            pe.wait_ge(sq_ready, 1)
            mm(bank(6), ones[:, :], sq[:, 0:T], start=True, stop=True)
            mm(bank(7, C), ones[:, :], sq[:, T:KEYS], start=True, stop=True)
            mm(bank(4), ones[:, :], sq[:, KEYS:KEYS + T], start=True, stop=False)
            mm(bank(4), ones[:, :], sq[:, KEYS + T:KEYS + 2 * T], start=False, stop=True).then_inc(sums_done, 1)
            pe.wait_ge(krt_ready, 1)
            mm(bank(5), fold[:, :], krt[:, 0:T], start=True, stop=True)
            mm(bank(3, C), fold[:, :], krt[:, T:KEYS], start=True, stop=True).then_inc(sums_done, 1)
            with pe.Fori(1, 4) as i:
                for b in range(2):
                    plain_tile(R_POOLX + 2 * i + b, 2 * i + b, b)
            with pe.Fori(0, 8) as i:
                for b in range(2):
                    plain_tile(R_GATES + 2 * i + b, 8 + 2 * i + b, b)
            def three(dst, parts):
                last = 3 * len(parts) - 1
                q = 0
                for sh, sl, mh, ml in parts:
                    for w, m in ((sh, mh), (sh, ml), (sl, mh)):
                        ins = mm(dst, w, m, start=(q == 0), stop=(q == last))
                        q += 1
                return ins

            def scores(s, qt, n=None, first=False):
                if not first:
                    pe.wait_ge(exp_ready, s - 1)
                qs = slice(qt * P, (qt + 1) * P)
                for dst, ks in ((bank(2 * (qt % 2)), slice(0, T)), (bank(2 * (qt % 2) + 1, C), slice(T, KEYS))):
                    if qt == 0 and ks.start == T:
                        pe.wait_ge(pj_free, n)
                    ins = three(dst, [(qn_hi[:, qs], qn_lo[:, qs], k_hi[:, ks], k_lo[:, ks]),
                                      (qr_hi[:, qs], qr_lo[:, qs], kr_hi[:, ks], kr_lo[:, ks])])
                ins.then_inc(s_done, 1)

            def turn(s, qt, first=False):
                pe.wait_ge(prob_ready, s + 1)
                if not first:
                    pe.wait_ge(pt_lo_s, s)
                for k in range(KT):
                    ins = nc.tensor.transpose(banks2(4, KEYS)[:, k * P:(k + 1) * P],
                                              prob[qt % 2][:, k * P:(k + 1) * P], ident[:, :])
                ins.then_inc(pt_turned, 1)

            def value_product(n, pts):
                pe.wait_ge(pt_lo_s, pts)
                three(bank(6), [(v_hi[:, k, :], v_lo[:, k, :], pt_hi[:, k, :], pt_lo[:, k, :])
                                for k in range(KT)]).then_inc(pj_done, 1)

            def values(h, k0, kn, dst):
                pe.wait_ge(wv_lo_s, h + 1)
                for k in range(k0, k0 + kn):
                    ks = slice(k * P, (k + 1) * P)
                    ins = three(dst[:, (k - k0) * P:(k - k0 + 1) * P],
                                [(kvn_hi[:, ks], kvn_lo[:, ks], wv_hi[:, :], wv_lo[:, :])])
                ins.then_inc(pj_done, 1)

            def queries(h, n=None):
                pe.wait_ge(wqk_lo_s, h + 1)
                for q, (bk, at) in enumerate(((7, P), (6, 0))):
                    if n is not None:
                        pe.wait_ge(pj_free, n + 2 + q)
                    three(bank(bk), [(wqk_hi[:, 2 * P * k + at:2 * P * k + at + P], wqk_lo[:, 2 * P * k + at:2 * P * k + at + P],
                                      cqn_hi[:, k, :], cqn_lo[:, k, :]) for k in range(2)]).then_inc(pj_done, 1)

            def keys(h):
                wk = slice(4 * P, 5 * P)
                pe.wait_ge(qr_rotated, h + 1)
                three(bank(7), [(wqk_hi[:, wk], wqk_lo[:, wk], kvn_hi[:, 0:T], kvn_lo[:, 0:T])]).then_inc(pj_done, 1)

            def keys_ctx(n):
                wk = slice(4 * P, 5 * P)
                pe.wait_ge(pj_free, n)
                three(bank(6, C), [(wqk_hi[:, wk], wqk_lo[:, wk], kvn_hi[:, T:KEYS], kvn_lo[:, T:KEYS])]).then_inc(pj_done, 1)

            def head(h, n, head0=False, last=False):
                s = 4 * h
                done = 4 if head0 else n
                pe.wait_ge(pj_free, done - 1)
                if head0:
                    pe.wait_ge(pmix_used, 4)
                scores(s, 0, done, head0)
                if head0:
                    pe.wait_ge(pmix_used, 6)
                scores(s + 1, 1, None, head0)
                if not head0:
                    value_product(n, s)
                turn(s, 0, head0)
                scores(s + 2, 2)
                values(h, 0, 4, bank(7))
                turn(s + 1, 1)
                scores(s + 3, 3)
                if not head0:
                    pe.wait_ge(pj_free, n + 1)
                values(h, 4, 2, bank(6, C))
                turn(s + 2, 2)
                if not last:
                    queries(h + 1, n)
                    keys(h + 1)
                turn(s + 3, 3)
                if not last:
                    keys_ctx(n + 4)

            for n in range(2):
                pe.wait_ge(diag_ready, (n + 1) * KC)
                for q in range(2):
                    ins = mm(bank(4 - 2 * n + q), ones[:, :], diag[:, n, q * 512:(q + 1) * 512], start=True, stop=True)
                ins.then_inc(rows_done, 1)
            pe.wait_ge(split_lo, 3)
            queries(0)
            pe.wait_ge(tile_copied, 24)

            def pooled_branch(m):
                g, half = m // 2, m % 2
                t = R_WPOOL + g // 2
                b = t % 2
                if m % 4 == 0:
                    ring_wait(t)
                if m % 2 == 0:
                    pe.wait_ge(pooled_lo, g + 1)
                if m >= 6:
                    pe.wait_ge(pmix_used, m - 5)
                q = 0
                for k in range(2):
                    at = (g % 2) * 512 + k * 256 + half * P
                    for w, x in ((w_hi[b], ht_hi), (w_hi[b], ht_lo), (w_lo[b], ht_hi)):
                        ins = mm(bank((m + 4) % 6), w[:, at:at + P], x[:, 2 * g + k, :], start=(q == 0), stop=(q == 5))
                        q += 1
                if m % 4 == 3:
                    ins.then_inc(ring_used, 1)
            pe.wait_ge(rows_ready, 1)
            pooled_branch(0)
            pooled_branch(1)
            keys(0)
            pooled_branch(2)
            pooled_branch(3)
            keys_ctx(1)
            pe.wait_ge(rows_ready, 2)
            for m in range(4, KC):
                pooled_branch(m)
            head(0, 3, head0=True)
            with pe.Fori(1, H - 1) as h:
                head(h, 7 * h + 3)
            head(H - 1, 7 * (H - 1) + 3, last=True)
            def rows(b, sh, sl, start, stop, done=None, tiles=range(TT), used=True, after_gelu=False):
                for tt in tiles:
                    if after_gelu and tt == 2:
                        pe.wait_ge(gelu_done, JT)
                    ts = slice(tt * P, (tt + 1) * P)
                    for q, (s_, w_) in enumerate(((sh, w_hi[b]), (sh, w_lo[b]), (sl, w_hi[b]))):
                        for dh in range(2):
                            ins = mm(bank(2 * tt + dh), s_[:, ts], w_[:, dh * 512:(dh + 1) * 512],
                                     start=start and q == 0, stop=stop and q == 2)
                    if done is not None and tt < TT - 1:
                        ins.then_inc(done, 1)
                if used:
                    ins.then_inc(ring_used, 1)
            def out_rows(k, tiles, used=False):
                last = k == KC - 1
                rows(k % 2, ht_hi[:, k, :], ht_lo[:, k, :], k == 0, last, y_done if last else None, tiles, used)
            for k in range(2):
                ring_wait(R_WOUT + k)
                out_rows(k, (0, 1))
            pe.wait_ge(pt_lo_s, 4 * H)
            three(bank(6), [(v_hi[:, k, :], v_lo[:, k, :], pt_hi[:, k, :], pt_lo[:, k, :])
                            for k in range(KT)]).then_inc(pj_done, 1)
            for k in range(2):
                out_rows(k, (2,))
            pe.wait_ge(pj_free, 7 * H)
            for k in range(2):
                out_rows(k, (3,), used=True)
            for k in range(2, KC - 2):
                ring_wait(R_WOUT + k)
                out_rows(k, range(TT), used=True)
            ring_wait(R_WOUT + KC - 2)
            out_rows(KC - 2, range(TT - 1))
            ring_wait(R_WOUT + KC - 1)
            out_rows(KC - 1, range(TT - 1))
            out_rows(KC - 2, (TT - 1,), used=True)
            out_rows(KC - 1, (TT - 1,), used=True)
            pe.wait_ge(xmn_ready, TT)
            for k in range(KC):
                for tt in range(TT):
                    ins = nc.tensor.transpose(ps[:, k, tt * P:(tt + 1) * P], xm_n[:, tt, k * P:(k + 1) * P], ident[:, :])
                ins.then_inc(hf_turned, 1)
            def q_tile(m, b, first=False):
                ring_wait(R_WQ + m)
                if not first:
                    pe.wait_ge(q_lo_s, m - 1)
                project(b, bank(b), ht_hi, ht_lo, T, fresh=first and m == 0).then_inc(ring_used, 1)

            def score_tile(m, b, first=False):
                pe.wait_ge(q_lo_s, m + 1)
                if not first:
                    pe.wait_ge(sc_copied, m - 1)
                for tt in range(TT):
                    ts = slice(tt * P, (tt + 1) * P)
                    ins = three(ps[:, 2 + b, tt * P:(tt + 1) * P],
                                [(q_hi[b][:, ts], q_lo[b][:, ts], keys_hi[:, b, :], keys_lo[:, b, :])])
                ins.then_inc(sc_done, 1)
            q_tile(0, 0, True)
            q_tile(1, 1, True)
            pe.wait_ge(keys_lo_s, 1)
            score_tile(0, 0, True)
            q_tile(2, 0)
            score_tile(1, 1, True)
            with pe.Fori(1, PH - 1) as i:
                q_tile(2 * i + 1, 1)
                score_tile(2 * i, 0)
                q_tile(2 * i + 2, 0)
                score_tile(2 * i + 1, 1)
            q_tile(2 * PH - 1, 1)
            score_tile(2 * PH - 2, 0)

            def expert(j, b, first=False):
                ring_wait(R_U + j)
                if not first:
                    pe.wait_ge(gelu_done, j - 1)
                project(b, bank(4 + b), ht_hi, ht_lo, T).then_inc(ring_used, 1)

            def gate_matrices(u, b, first=False):
                pe.wait_ge(oh_ready, u + 1)
                pe.wait_ge(oh_lo_ready, u + 1)
                if not first:
                    pe.wait_ge(g_copied, u)
                for q in range(G_TOK):
                    ins = mm(ps[:, q // 2, (q % 2) * 2 * NK:(q % 2 + 1) * 2 * NK], oh_i[b][:, q, :],
                             oh_j[b][:, q, :, :].rearrange("p s n -> p (s n)"), start=True, stop=True)
                ins.then_inc(g_built, 1)
            expert(0, 0, True)
            score_tile(2 * PH - 1, 1)
            expert(1, 1, True)
            with pe.Fori(1, G_FIRST // 2 - 1) as i:
                expert(2 * i, 0)
                expert(2 * i + 1, 1)
            pe.wait_ge(sel_ready, 1)
            for n, src in enumerate((sel_i, sel_j, None)):
                for tt in range(TT):
                    m = src[:, tt, :] if src is not None else \
                        sel_e[:, tt * PH:(tt + 1) * PH, :].rearrange("p h k -> p (h k)")
                    ins = nc.tensor.transpose(ps[:, n, tt * P:(tt + 1) * P], m, ident[:, :])
            ins.then_inc(sel_turned, 1)
            expert(G_FIRST - 2, 0)
            expert(G_FIRST - 1, 1)
            expert(G_FIRST, 0)
            gate_matrices(0, 0, True)
            expert(G_FIRST + 1, 1)
            gate_matrices(1, 1)
            with pe.Fori(1, T // G_TOK // 2) as i:
                for b in range(2):
                    expert(G_FIRST + 2 * i + b, b)
                    gate_matrices(2 * i + b, b)
            with pe.Fori((G_FIRST + T // G_TOK) // 2, JT // 2) as i:
                expert(2 * i, 0)
                expert(2 * i + 1, 1)
            pe.wait_ge(g_copied, T // G_TOK)

            def combine(j, b, start=False, stop=False):
                ring_wait(R_V + j)
                pe.wait_ge(a_lo_s, j + 1)
                rows(b, a_hi[b], a_lo[b], start, stop, o_done if stop else None, after_gelu=start)
            combine(0, 0, start=True)
            combine(1, 1)
            with pe.Fori(1, JT // 2 - 1) as i:
                combine(2 * i, 0)
                combine(2 * i + 1, 1)
            for b, tiles, used in ((0, range(TT - 1), False), (1, range(TT - 1), False),
                                   (0, (TT - 1,), True), (1, (TT - 1,), True)):
                if not used:
                    ring_wait(R_END - 2 + b)
                    pe.wait_ge(a_lo_s, JT - 1 + b)
                rows(b, a_hi[b], a_lo[b], False, b == 1, o_done if b else None, tiles, used)


def _tables():
    import numpy as np
    f = np.float32
    grid_w, n_freq = 64, 16
    t = np.arange(T)
    inv_freq = (f(10000.0) ** (-np.arange(n_freq, dtype=f) / f(n_freq))).astype(f)
    pos = np.stack([t // grid_w, t % grid_w]).astype(f)
    ang = pos[:, None, :] * inv_freq[None, :, None]
    cos, sin = np.cos(ang).astype(f), np.sin(ang).astype(f)
    rot = np.zeros((P, KEYS), f)
    rot[0:64, 0:T] = np.stack([cos, cos], 1).reshape(64, T)
    rot[64:128, 0:T] = np.stack([-sin, sin], 1).reshape(64, T)
    rot[0:64, T:KEYS] = 1.0
    edge = np.zeros((4, 2 * PAD), f)
    for g, w in enumerate(WINDOWS):
        for n in range(2 * PAD):
            tok = n if n < PAD else T - 2 * PAD + n
            edge[g, n] = w / (min(tok + w // 2, T) - max(tok - w // 2, 0))
    p = np.arange(P)
    return {
        "rot": rot,
        "edge": np.ascontiguousarray(np.broadcast_to(edge, (P, 4, 2 * PAD))),
        "ident": np.eye(P, dtype=f),
        "fold": (p[:, None] % 64 == p[None, :] % 64).astype(f),
        "iota": np.ascontiguousarray(np.broadcast_to(np.arange(P, dtype=f), (P, P))),
    }


def _layout(x, c, ctx, c_ctx, w_ada, b_ada, g_mix_pre, g_mix_post, g_ffn_pre, g_ffn_post, w_in, g_q_lora, w_uq,
            g_kv_lora, w_ukv, w_pool, pool_scale, w_out, peer_wq, peer_keys, peer_u, peer_v):
    import numpy as np

    def tiles(w):
        k, n = w.shape[0] // P, w.shape[1] // P
        return w.reshape(k, P, n, P).transpose(2, 1, 0, 3).reshape(n, P, k * P)

    def vec(a):
        return a.reshape(-1, P).T

    swap = (np.arange(64).reshape(2, 2, 16)[:, ::-1]).reshape(-1)
    win = w_in[0]
    rope = win[:, P:P + 64]
    w_in_t = tiles(np.concatenate([win[:, 0:P], rope, rope[:, swap], win[:, P + 64:]], axis=1))
    uq = w_uq[0].reshape(2, P, H, QDIM)
    uq = np.concatenate([uq[..., 0:P], uq[..., P:], uq[..., P:][..., swap]], axis=-1)
    ukv = w_ukv[0].reshape(P, H, 2 * P)
    wqk = np.concatenate([uq[0], uq[1], ukv[..., 0:P]], axis=-1).transpose(1, 0, 2)
    cols = np.concatenate([vec(b_ada[0]), vec(g_mix_pre[0]), vec(g_mix_post[0]), vec(g_ffn_pre[0]), vec(g_ffn_post[0]),
                           vec(pool_scale[0]), vec(g_q_lora[0]), vec(g_kv_lora[0]),
                           np.full((P, 1), EPS, np.float32)], axis=1)
    out = {
        "x": x[0], "ctx": ctx[0],
        "cond": np.stack([vec(c[0]), vec(c_ctx)], axis=-1),
        "cols": cols,
        "w_ada_c": w_ada[0][:, :2 * D].reshape(KC, P, ADA_PE, ADA_W).transpose(2, 1, 0, 3).reshape(ADA_PE, P, KC * ADA_W),
        "w_ada_r": w_ada[0][:, 2 * D:].T.reshape(ADA_DVE, 2, P, D).transpose(0, 2, 1, 3).reshape(ADA_DVE, P, 2 * D),
        "c_row": np.broadcast_to(c, (P, D)),
        "w_in": w_in_t,
        "w_pool": w_pool[0].reshape(2, 2, 2, P, 2 * P).transpose(0, 3, 1, 2, 4).reshape(2, P, D),
        "w_out": w_out[0].reshape(KC, P, D),
        "wq": tiles(peer_wq[0]),
        "wqk": wqk,
        "wv": ukv[..., P:].transpose(1, 0, 2),
        "keys": peer_keys[0].transpose(2, 0, 1),
        "u": peer_u[0].reshape(NK, JT, KC, P).transpose(1, 3, 2, 0).reshape(JT, P, D),
        "v": peer_v[0].reshape(NK, JT, D).transpose(1, 0, 2),
    }
    out.update(_tables())
    return {k: np.ascontiguousarray(w) for k, w in out.items()}


def kernel(**inputs):
    import numpy as _np
    import concourse.bacc as _bacc
    from concourse import mybir as _mybir
    from concourse.bass_utils import run_bass_kernel_spmd as _run

    nc = _bacc.Bacc("TRN2", target_bir_lowering=False, num_devices=1)
    arrays, aps = {}, {}
    for name, w in _layout(**{k: _np.asarray(v) for k, v in inputs.items()}).items():
        arrays[f"in_{name}"] = w
        aps[name] = nc.dram_tensor(f"in_{name}", w.shape, _mybir.dt.from_np(w.dtype), kind="ExternalInput").ap()
    out = nc.dram_tensor("out_0", (T, D), _mybir.dt.float32, kind="ExternalOutput").ap()
    build(nc, aps, out)
    r = _run(nc, [arrays], core_ids=[0])
    return r.results[0]["out_0"].reshape(1, T, D)
```
